# Optimizing a Trainium2 kernel written in Bass

```python
import math
import jax, jax.numpy as jnp
from jax import lax
import numpy as np
import jax
import jax.numpy as jnp

D_MODEL = 1024
BATCH = 1
SEQ = 512
DEPTH = 1

CHUNK = 64
D_MIX = D_MODEL
D_A = D_MIX // 2
D_B = D_MIX - D_A
H_A = 8
DH_A = D_A // H_A
H_B = 8
DH_B = D_B // H_B
SGU_BLOCK = 128
Q_BLOCK = 128
D_FF = 2816
N_SUB = 3
OFF_Z_A = 0
OFF_Q = 2 * D_A
OFF_K = OFF_Q + D_B
OFF_V = OFF_K + D_B
OFF_F = OFF_V + D_B
N_IN = OFF_F + H_B
EPS = 1e-6
NEG_INF = -1e30


def rms_norm(x, g):
    xf = x.astype(jnp.float32)
    y = xf * lax.rsqrt(jnp.mean(xf * xf, axis=-1, keepdims=True) + EPS)
    return (y * g.astype(jnp.float32)).astype(x.dtype)

def layer_norm(x, g, b):
    xf = x.astype(jnp.float32)
    mu = jnp.mean(xf, axis=-1, keepdims=True)
    xc = xf - mu
    y = xc * lax.rsqrt(jnp.mean(xc * xc, axis=-1, keepdims=True) + EPS)
    return (y * g.astype(jnp.float32) + b.astype(jnp.float32)).astype(x.dtype)

def modulate(x, g_pre, shift, scale):
    return rms_norm(x, g_pre) * (1 + scale[:, None, :]) + shift[:, None, :]

def swiglu(h, w_gate, w_up, w_down):
    return (jax.nn.silu(h @ w_gate) * (h @ w_up)) @ w_down

def spatial_gating(z, ln_g, ln_b, w_s, b_s):
    b_, s_, _ = z.shape
    z = jax.nn.gelu(z)
    u, v = z[..., :D_A], z[..., D_A:]
    v = layer_norm(v, ln_g, ln_b)
    v = v.reshape(b_, s_ // SGU_BLOCK, SGU_BLOCK, H_A, DH_A)
    pos = jnp.arange(SGU_BLOCK)
    mask = (pos[None, :] // CHUNK) <= (pos[:, None] // CHUNK)
    w = jnp.where(mask[None], w_s, jnp.zeros((), w_s.dtype))
    gate = jnp.einsum('hij,bnjhc->bnihc', w, v) + b_s.T[None, None, :, :, None]
    return u * gate.reshape(b_, s_, D_A)

def forgetting_attention(q, k, v, log_f):
    s_ = q.shape[2]
    cum = jnp.cumsum(log_f, axis=-1)
    scale = DH_B ** -0.5
    outs = []
    for blk in range(s_ // Q_BLOCK):
        q0 = blk * Q_BLOCK
        q1 = q0 + Q_BLOCK
        logits = jnp.einsum('bhqd,bhkd->bhqk', q[:, :, q0:q1], k[:, :, :q1]).astype(jnp.float32) * scale
        logits = logits + cum[:, :, q0:q1, None] - cum[:, :, None, :q1]
        qpos = q0 + jnp.arange(Q_BLOCK)
        kpos = jnp.arange(q1)
        logits = jnp.where(kpos[None, :] <= qpos[:, None], logits, NEG_INF)
        p = jax.nn.softmax(logits, axis=-1).astype(v.dtype)
        outs.append(jnp.einsum('bhqk,bhkd->bhqd', p, v[:, :, :q1]))
    return jnp.concatenate(outs, axis=2)

def hybrid_mixer(h, w_in, sgu_ln_g, sgu_ln_b, sgu_w, sgu_b, fox_b_f, gnorm_a_g, gnorm_b_g, w_out):
    b_, s_, _ = h.shape
    proj = h @ w_in
    y_a = spatial_gating(proj[..., OFF_Z_A:OFF_Q], sgu_ln_g, sgu_ln_b, sgu_w, sgu_b)

    def heads(t):
        return t.reshape(b_, s_, H_B, DH_B).transpose(0, 2, 1, 3)

    q = heads(proj[..., OFF_Q:OFF_K])
    k = heads(proj[..., OFF_K:OFF_V])
    v = heads(proj[..., OFF_V:OFF_F])
    log_f = jax.nn.log_sigmoid(proj[..., OFF_F:N_IN].astype(jnp.float32)
                               + fox_b_f.astype(jnp.float32)).transpose(0, 2, 1)
    y_b = forgetting_attention(q, k, v, log_f).transpose(0, 2, 1, 3).reshape(b_, s_, D_B)
    y = jnp.concatenate([rms_norm(y_a, gnorm_a_g), rms_norm(y_b, gnorm_b_g)], axis=-1)
    return y @ w_out

def first_inputs(seed: int = 0) -> dict:
    key = jax.random.key(seed)
    ks = jax.random.split(key, 20)
    f32 = jnp.float32
    n = lambda k, shape, s: jax.random.normal(k, shape, f32) * s
    return {
        'x': n(ks[0], (BATCH, SEQ, D_MODEL), 1.0),
        'c': n(ks[1], (BATCH, D_MODEL), 1.0),
        'w_ada': n(ks[2], (DEPTH, D_MODEL, N_SUB * 3 * D_MODEL), 0.1 * D_MODEL ** -0.5),
        'b_ada': n(ks[3], (DEPTH, N_SUB * 3 * D_MODEL), 0.01),
        'norm_pre_g': 1.0 + n(ks[4], (DEPTH, N_SUB, D_MODEL), 0.02),
        'norm_post_g': 1.0 + n(ks[5], (DEPTH, N_SUB, D_MODEL), 0.02),
        'ffn_w_gate': n(ks[6], (DEPTH, 2, D_MODEL, D_FF), D_MODEL ** -0.5),
        'ffn_w_up': n(ks[7], (DEPTH, 2, D_MODEL, D_FF), D_MODEL ** -0.5),
        'ffn_w_down': n(ks[8], (DEPTH, 2, D_FF, D_MODEL), D_FF ** -0.5),
        'w_in': n(ks[9], (DEPTH, D_MODEL, N_IN), D_MODEL ** -0.5),
        'sgu_ln_g': 1.0 + n(ks[10], (DEPTH, D_A), 0.02),
        'sgu_ln_b': n(ks[11], (DEPTH, D_A), 0.02),
        'sgu_w': n(ks[12], (DEPTH, H_A, SGU_BLOCK, SGU_BLOCK), SGU_BLOCK ** -0.5),
        'sgu_b': 1.0 + n(ks[13], (DEPTH, H_A, SGU_BLOCK), 0.02),
        'fox_b_f': 2.0 + n(ks[14], (DEPTH, H_B), 0.5),
        'gnorm_a_g': 1.0 + n(ks[15], (DEPTH, D_A), 0.02),
        'gnorm_b_g': 1.0 + n(ks[16], (DEPTH, D_B), 0.02),
        'w_out': n(ks[17], (DEPTH, D_MIX, D_MODEL), D_MIX ** -0.5),
    }

def first_block(x, c, w_ada, b_ada, norm_pre_g, norm_post_g, ffn_w_gate, ffn_w_up, ffn_w_down,
              w_in, sgu_ln_g, sgu_ln_b, sgu_w, sgu_b, fox_b_f, gnorm_a_g, gnorm_b_g, w_out):
    b_ = x.shape[0]
    for l in range(DEPTH):
        mod = (jax.nn.silu(c) @ w_ada[l] + b_ada[l]).reshape(b_, N_SUB, 3, D_MODEL)
        shift, scale, gate = mod[:, :, 0], mod[:, :, 1], mod[:, :, 2]

        h = modulate(x, norm_pre_g[l, 0], shift[:, 0], scale[:, 0])
        h = swiglu(h, ffn_w_gate[l, 0], ffn_w_up[l, 0], ffn_w_down[l, 0])
        x = x + 0.5 * (1 + gate[:, 0, None, :]) * rms_norm(h, norm_post_g[l, 0])

        h = modulate(x, norm_pre_g[l, 1], shift[:, 1], scale[:, 1])
        h = hybrid_mixer(h, w_in[l], sgu_ln_g[l], sgu_ln_b[l], sgu_w[l], sgu_b[l], fox_b_f[l],
                         gnorm_a_g[l], gnorm_b_g[l], w_out[l])
        x = x + (1 + gate[:, 1, None, :]) * rms_norm(h, norm_post_g[l, 1])

        h = modulate(x, norm_pre_g[l, 2], shift[:, 2], scale[:, 2])
        h = swiglu(h, ffn_w_gate[l, 1], ffn_w_up[l, 1], ffn_w_down[l, 1])
        x = x + 0.5 * (1 + gate[:, 2, None, :]) * rms_norm(h, norm_post_g[l, 2])
    return x


_first_inputs = first_inputs


def first_inputs(seed=0):
    import zlib

    import numpy as np

    out = dict(_first_inputs(seed))
    spreads = {}
    factors = {'norm_post_g': 2.973,
     'sgu_ln_g': 8.0,
     'sgu_ln_b': 8.0,
     'sgu_b': 7.465,
     'gnorm_a_g': 5.815,
     'gnorm_b_g': 5.674}
    for name, (base, spread) in spreads.items():
        noise = np.random.default_rng([zlib.crc32(name.encode()), seed]).standard_normal(out[name].shape)
        drawn = base * np.exp(spread * noise) if base else spread * noise
        out[name] = __import__('jax').numpy.asarray(drawn.astype(out[name].dtype))
    for name, factor in factors.items():
        out[name] = (out[name] * factor).astype(out[name].dtype)
    return out


_narrow_inputs = first_inputs


def first_inputs(seed=0):

    out = dict(_narrow_inputs(seed))
    wider = {'sgu_ln_g': 6.95, 'sgu_ln_b': 6.8, 'sgu_b': 6.5, 'gnorm_a_g': 4.9, 'gnorm_b_g': 4.91}
    for name, times in wider.items():
        mean = out[name].mean()
        out[name] = (mean + times * (out[name] - mean)).astype(out[name].dtype)
    return out


D_MIX_2 = D_MODEL
D_RWKV = D_MIX_2 // 2
D_CONV = D_MIX_2 - D_RWKV
HEAD_SIZE = 64
N_HEADS = D_RWKV // HEAD_SIZE
LORA_W = 64
LORA_A = 64
LORA_G = 128
CONV_WIDTH = 31
D_SHIFT = 3 * D_RWKV + LORA_W + LORA_A + LORA_G
D_IN = D_SHIFT + 2 * D_CONV
RMS_EPS = 1e-6
GN_EPS = 64e-5
LN_EPS = 1e-5
DECAY_SCALE = math.exp(-0.5)


def rmsnorm(x, g):
    xf = x.astype(jnp.float32)
    y = xf * lax.rsqrt(jnp.mean(xf * xf, axis=-1, keepdims=True) + RMS_EPS)
    return (y * g.astype(jnp.float32)).astype(x.dtype)

def layernorm(x, g, b):
    xf = x.astype(jnp.float32)
    mu = jnp.mean(xf, axis=-1, keepdims=True)
    var = jnp.mean(jnp.square(xf - mu), axis=-1, keepdims=True)
    y = (xf - mu) * lax.rsqrt(var + LN_EPS)
    return (y * g.astype(jnp.float32) + b.astype(jnp.float32)).astype(x.dtype)

def swiglu_2(x, w_gu, w_down):
    gu = x @ w_gu
    gate, up = gu[..., :D_FF], gu[..., D_FF:]
    return (jax.nn.silu(gate) * up) @ w_down

def token_shift(y):
    return jnp.pad(y[:, :-1], ((0, 0), (1, 0), (0, 0)))

def rwkv7_recurrence(r, w, k, v, z, b):
    bsz, seq, nh, n = r.shape
    n_chunks = seq // CHUNK

    def to_chunks(t):
        return jnp.transpose(t, (1, 0, 2, 3)).reshape(n_chunks, CHUNK, bsz, nh, n)

    xs = tuple(to_chunks(t) for t in (r, w, k, v, z, b))

    def frame_step(state, inp):
        r_t, w_t, k_t, v_t, z_t, b_t = inp
        sz = jnp.einsum('bhij,bhj->bhi', state, z_t)
        state = (state * w_t[:, :, None, :]
                 + sz[..., None] * b_t[:, :, None, :]
                 + v_t[..., None] * k_t[:, :, None, :])
        y_t = jnp.einsum('bhij,bhj->bhi', state, r_t)
        return state, y_t

    def chunk_step(state, chunk_inp):
        return lax.scan(frame_step, state, chunk_inp)

    state0 = jnp.zeros((bsz, nh, n, n), jnp.float32)
    _, ys = lax.scan(chunk_step, state0, xs)
    ys = ys.reshape(seq, bsz, nh, n)
    return jnp.transpose(ys, (1, 0, 2, 3))

def hybrid_mixer_2(h, w_in, shift_mu, w_up, w0, a_up, a0, g_up, k_k, k_a, r_k,
                 gn_w, gn_b, conv_dw, conv_b, conv_ln_w, conv_ln_b, w_out):
    bsz, seq, _ = h.shape
    p = h @ w_in
    ps, pc = p[..., :D_SHIFT], p[..., D_SHIFT:]

    ps = ps + (token_shift(ps) - ps) * shift_mu
    o1, o2, o3 = D_RWKV, 2 * D_RWKV, 3 * D_RWKV
    o4, o5 = o3 + LORA_W, o3 + LORA_W + LORA_A
    r, k, v = ps[..., :o1], ps[..., o1:o2], ps[..., o2:o3]
    xw, xa, xg = ps[..., o3:o4], ps[..., o4:o5], ps[..., o5:]

    d = (w0 + jnp.tanh(xw) @ w_up).astype(jnp.float32)
    decay = jnp.exp(-DECAY_SCALE * jax.nn.sigmoid(d))
    a = jax.nn.sigmoid(a0 + xa @ a_up)
    g = jax.nn.sigmoid(xg) @ g_up

    heads = lambda t: t.reshape(bsz, seq, N_HEADS, HEAD_SIZE).astype(jnp.float32)
    kk = heads(k * k_k)
    kk = kk * lax.rsqrt(jnp.maximum(jnp.sum(kk * kk, axis=-1, keepdims=True), 1e-12))
    k = k * (1.0 + (a - 1.0) * k_a)
    rh, kh, vh, ah, wh = heads(r), heads(k), heads(v), heads(a), heads(decay)

    y = rwkv7_recurrence(rh, wh, kh, vh, -kk, kk * ah)
    mu = jnp.mean(y, axis=-1, keepdims=True)
    var = jnp.mean(jnp.square(y - mu), axis=-1, keepdims=True)
    y = (y - mu) * lax.rsqrt(var + GN_EPS)
    y = y * gn_w.astype(jnp.float32).reshape(N_HEADS, HEAD_SIZE) + gn_b.astype(jnp.float32).reshape(N_HEADS, HEAD_SIZE)
    bonus = jnp.sum(rh * kh * r_k.astype(jnp.float32), axis=-1, keepdims=True) * vh
    y = (y + bonus).reshape(bsz, seq, D_RWKV).astype(h.dtype)
    out_a = y * g

    glu = pc[..., :D_CONV] * jax.nn.sigmoid(pc[..., D_CONV:])
    c = lax.conv_general_dilated(
        glu, conv_dw[:, None, :], window_strides=(1,),
        padding=[(CONV_WIDTH - 1, 0)],
        dimension_numbers=('NWC', 'WIO', 'NWC'),
        feature_group_count=D_CONV) + conv_b
    out_b = jax.nn.silu(layernorm(c, conv_ln_w, conv_ln_b))

    return jnp.concatenate([out_a, out_b], axis=-1) @ w_out

def second_inputs(seed: int = 0) -> dict:
    key = jax.random.key(seed)
    ks = iter(jax.random.split(key, 40))
    f32 = jnp.float32

    def nrm(shape, scale):
        return jax.random.normal(next(ks), shape, f32) * scale

    def gain(shape):
        return 1.0 + nrm(shape, 0.02)

    L = DEPTH
    return {
        "x": nrm((BATCH, SEQ, D_MODEL), 1.0),
        "ffn1_norm_pre": gain((L, D_MODEL)),
        "ffn1_norm_post": gain((L, D_MODEL)),
        "ffn1_w_gu": nrm((L, D_MODEL, 2 * D_FF), D_MODEL ** -0.5),
        "ffn1_w_down": nrm((L, D_FF, D_MODEL), D_FF ** -0.5),
        "mix_norm_pre": gain((L, D_MODEL)),
        "mix_norm_post": gain((L, D_MODEL)),
        "w_in": nrm((L, D_MODEL, D_IN), D_MODEL ** -0.5),
        "shift_mu": jax.random.uniform(next(ks), (L, D_SHIFT), f32, 0.1, 0.9),
        "w_up": nrm((L, LORA_W, D_RWKV), 0.3 * LORA_W ** -0.5),
        "w0": nrm((L, D_RWKV), 0.5),
        "a_up": nrm((L, LORA_A, D_RWKV), 0.3 * LORA_A ** -0.5),
        "a0": nrm((L, D_RWKV), 0.1),
        "g_up": nrm((L, LORA_G, D_RWKV), LORA_G ** -0.5),
        "k_k": 0.85 + nrm((L, D_RWKV), 0.02),
        "k_a": 1.0 + nrm((L, D_RWKV), 0.02),
        "r_k": nrm((L, N_HEADS, HEAD_SIZE), 0.1),
        "gn_w": gain((L, D_RWKV)),
        "gn_b": nrm((L, D_RWKV), 0.01),
        "conv_dw": nrm((L, CONV_WIDTH, D_CONV), CONV_WIDTH ** -0.5),
        "conv_b": nrm((L, D_CONV), 0.01),
        "conv_ln_w": gain((L, D_CONV)),
        "conv_ln_b": nrm((L, D_CONV), 0.01),
        "w_out": nrm((L, D_MIX_2, D_MODEL), D_MIX_2 ** -0.5),
        "ffn2_norm_pre": gain((L, D_MODEL)),
        "ffn2_norm_post": gain((L, D_MODEL)),
        "ffn2_w_gu": nrm((L, D_MODEL, 2 * D_FF), D_MODEL ** -0.5),
        "ffn2_w_down": nrm((L, D_FF, D_MODEL), D_FF ** -0.5),
    }

def second_block(x, ffn1_norm_pre, ffn1_norm_post, ffn1_w_gu, ffn1_w_down,
              mix_norm_pre, mix_norm_post, w_in, shift_mu, w_up, w0, a_up, a0,
              g_up, k_k, k_a, r_k, gn_w, gn_b, conv_dw, conv_b, conv_ln_w,
              conv_ln_b, w_out, ffn2_norm_pre, ffn2_norm_post, ffn2_w_gu,
              ffn2_w_down):
    for l in range(DEPTH):
        f = swiglu_2(rmsnorm(x, ffn1_norm_pre[l]), ffn1_w_gu[l], ffn1_w_down[l])
        x = x + 0.5 * rmsnorm(f, ffn1_norm_post[l])
        m = hybrid_mixer_2(rmsnorm(x, mix_norm_pre[l]), w_in[l], shift_mu[l], w_up[l],
                         w0[l], a_up[l], a0[l], g_up[l], k_k[l], k_a[l], r_k[l],
                         gn_w[l], gn_b[l], conv_dw[l], conv_b[l], conv_ln_w[l],
                         conv_ln_b[l], w_out[l])
        x = x + rmsnorm(m, mix_norm_post[l])
        f = swiglu_2(rmsnorm(x, ffn2_norm_pre[l]), ffn2_w_gu[l], ffn2_w_down[l])
        x = x + 0.5 * rmsnorm(f, ffn2_norm_post[l])
    return x


_first_inputs_2 = second_inputs


def second_inputs(seed=0):
    import zlib

    import numpy as np

    out = dict(_first_inputs_2(seed))
    spreads = {}
    factors = {'ffn1_norm_pre': 3.035,
     'ffn1_norm_post': 4.623,
     'mix_norm_post': 10.723,
     'w_up': 3.071,
     'k_k': 64.0,
     'k_a': 4.862,
     'gn_w': 24.462,
     'gn_b': 50.869,
     'conv_b': 5.48,
     'conv_ln_w': 19.156,
     'conv_ln_b': 36.805,
     'ffn2_norm_pre': 19.576,
     'ffn2_norm_post': 34.489}
    for name, (base, spread) in spreads.items():
        noise = np.random.default_rng([zlib.crc32(name.encode()), seed]).standard_normal(out[name].shape)
        drawn = base * np.exp(spread * noise) if base else spread * noise
        out[name] = __import__('jax').numpy.asarray(drawn.astype(out[name].dtype))
    for name, factor in factors.items():
        out[name] = (out[name] * factor).astype(out[name].dtype)
    return out


_narrow_inputs_2 = second_inputs


def second_inputs(seed=0):

    out = dict(_narrow_inputs_2(seed))
    wider = {'k_k': 12.0,
     'r_k': 3.2,
     'gn_w': 3.59,
     'gn_b': 3.6,
     'conv_ln_w': 3.65,
     'conv_ln_b': 3.6,
     'ffn2_norm_post': 3.74}
    for name, times in wider.items():
        mean = out[name].mean()
        out[name] = (mean + times * (out[name] - mean)).astype(out[name].dtype)
    return out


DEPTH_3 = 2

ROPE_THETA = 10000.0

A_HEADS = D_MODEL // 128
A_HEAD_DIM = 64
D_A_3 = A_HEADS * A_HEAD_DIM
IDX_HEADS = 8
IDX_DIM = 32
TOPK_MAX = 256

B_HEADS = D_MODEL // 256
B_HEAD_DIM = 64
D_B_3 = B_HEADS * 2 * B_HEAD_DIM

D_MIX_3 = D_A_3 + D_B_3
D_FF_3 = -(-8 * D_MODEL // (3 * 256)) * 256

IN_SPLITS = (D_A_3, D_A_3, D_A_3, IDX_HEADS * IDX_DIM, IDX_DIM, IDX_HEADS, D_B_3, D_B_3, D_B_3)
D_IN_3 = D_A_3 * 3 + IDX_HEADS * IDX_DIM + IDX_DIM + IDX_HEADS + D_B_3 * 3


def rms_norm_3(x, g):
    x32 = x.astype(jnp.float32)
    r = lax.rsqrt(jnp.mean(x32 * x32, axis=-1, keepdims=True) + RMS_EPS)
    return (x32 * r * g.astype(jnp.float32)).astype(x.dtype)

def rope_tables(seq_len, dim):
    pos = jnp.arange(seq_len, dtype=jnp.float32)
    inv = ROPE_THETA ** (-jnp.arange(0, dim, 2, dtype=jnp.float32) / dim)
    ang = pos[:, None] * inv[None, :]
    return jnp.cos(ang), jnp.sin(ang)

def apply_rope(x, cos, sin):
    half = x.shape[-1] // 2
    x32 = x.astype(jnp.float32)
    x1, x2 = x32[..., :half], x32[..., half:]
    c = cos[None, :, None, :]
    s = sin[None, :, None, :]
    return jnp.concatenate([x1 * c - x2 * s, x2 * c + x1 * s], axis=-1).astype(x.dtype)

def to_blocks(a):
    b, s = a.shape[:2]
    return jnp.swapaxes(a.reshape(b, s // Q_BLOCK, Q_BLOCK, *a.shape[2:]), 0, 1)

def from_blocks(a):
    nb, b = a.shape[:2]
    return jnp.swapaxes(a, 0, 1).reshape(b, nb * a.shape[2], *a.shape[3:])

def dsa_mixer(q, k, v, iq, ik, iw):
    s_len = q.shape[1]
    topk = min(TOPK_MAX, s_len // 4)
    key_chunk = jnp.arange(s_len) // CHUNK
    scale = A_HEAD_DIM ** -0.5
    gather = jax.vmap(lambda a, i: a[i])

    def block(args):
        bi, qb, iqb, iwb = args
        q_chunk = (bi * Q_BLOCK + jnp.arange(Q_BLOCK)) // CHUNK
        admissible = key_chunk[None, :] <= q_chunk[:, None]
        dots = jnp.einsum('bqhd,bsd->bqhs', iqb, ik,
                          preferred_element_type=jnp.float32) * (IDX_DIM ** -0.5)
        w = iwb.astype(jnp.float32) * (IDX_HEADS ** -0.5)
        score = jnp.einsum('bqhs,bqh->bqs', jax.nn.relu(dots), w)
        score = jnp.where(admissible[None], score, -jnp.inf)
        _, idx = lax.top_k(score, topk)
        k_sel = gather(k, idx)
        v_sel = gather(v, idx)
        valid = (idx // CHUNK) <= q_chunk[None, :, None]
        logits = jnp.einsum('bqhd,bqkhd->bhqk', qb, k_sel,
                            preferred_element_type=jnp.float32) * scale
        logits = jnp.where(valid[:, None], logits, -jnp.inf)
        p = jax.nn.softmax(logits, axis=-1)
        return jnp.einsum('bhqk,bqkhd->bqhd', p.astype(v.dtype), v_sel)

    nb = s_len // Q_BLOCK
    out = lax.map(block, (jnp.arange(nb), to_blocks(q), to_blocks(iq), to_blocks(iw)))
    return from_blocks(out)

def diff_mixer(q, k, v, lam, lam_init, g_subln):
    s_len = q.shape[1]
    key_chunk = jnp.arange(s_len) // CHUNK
    scale = B_HEAD_DIM ** -0.5

    def block(args):
        bi, qb = args
        q_chunk = (bi * Q_BLOCK + jnp.arange(Q_BLOCK)) // CHUNK
        admissible = key_chunk[None, :] <= q_chunk[:, None]
        logits = jnp.einsum('bqhcd,bshcd->bchqs', qb, k,
                            preferred_element_type=jnp.float32) * scale
        logits = jnp.where(admissible[None, None, None], logits, -jnp.inf)
        p = jax.nn.softmax(logits, axis=-1)
        attn = p[:, 0] - lam * p[:, 1]
        return jnp.einsum('bhqs,bshe->bqhe', attn.astype(v.dtype), v)

    nb = s_len // Q_BLOCK
    out = from_blocks(lax.map(block, (jnp.arange(nb), to_blocks(q))))
    return rms_norm_3(out, g_subln) * (1.0 - lam_init)

def third_inputs(seed: int = 0) -> dict:
    key = jax.random.key(seed)
    ks = jax.random.split(key, 14)
    f32 = jnp.float32
    nrm = lambda k, shape, fan_in: jax.random.normal(k, shape, f32) * (fan_in ** -0.5)
    gain = lambda k, shape: 1.0 + 0.02 * jax.random.normal(k, shape, f32)
    return {
        "x": jax.random.normal(ks[0], (BATCH, SEQ, D_MODEL), f32),
        "w_in": nrm(ks[1], (DEPTH_3, D_MODEL, D_IN_3), D_MODEL),
        "w_out": nrm(ks[2], (DEPTH_3, D_MIX_3, D_MODEL), D_MIX_3),
        "g_mix": gain(ks[3], (DEPTH_3, D_MODEL)),
        "lam_q1": 0.1 * jax.random.normal(ks[4], (DEPTH_3, B_HEAD_DIM), f32),
        "lam_k1": 0.1 * jax.random.normal(ks[5], (DEPTH_3, B_HEAD_DIM), f32),
        "lam_q2": 0.1 * jax.random.normal(ks[6], (DEPTH_3, B_HEAD_DIM), f32),
        "lam_k2": 0.1 * jax.random.normal(ks[7], (DEPTH_3, B_HEAD_DIM), f32),
        "g_subln": gain(ks[8], (DEPTH_3, 2 * B_HEAD_DIM)),
        "g_ffn": gain(ks[9], (DEPTH_3, D_MODEL)),
        "w_gate": nrm(ks[10], (DEPTH_3, D_MODEL, D_FF_3), D_MODEL),
        "w_up": nrm(ks[11], (DEPTH_3, D_MODEL, D_FF_3), D_MODEL),
        "w_down": nrm(ks[12], (DEPTH_3, D_FF_3, D_MODEL), D_FF_3),
        "g_final": gain(ks[13], (D_MODEL,)),
    }

def third_block(x, w_in, w_out, g_mix, lam_q1, lam_k1, lam_q2, lam_k2, g_subln,
              g_ffn, w_gate, w_up, w_down, g_final):
    b_, s_len, _ = x.shape
    cos_a, sin_a = rope_tables(s_len, A_HEAD_DIM)
    cos_i, sin_i = rope_tables(s_len, IDX_DIM)
    cos_b, sin_b = rope_tables(s_len, B_HEAD_DIM)
    split_points = [int(o) for o in np.cumsum(IN_SPLITS)[:-1]]

    for layer in range(DEPTH_3):
        h = rms_norm_3(x, g_mix[layer])
        proj = jnp.einsum('bsd,dc->bsc', h, w_in[layer])
        qa, ka, va, iq, ik, iw, qb, kb, vb = jnp.split(proj, split_points, axis=-1)

        qa = apply_rope(qa.reshape(b_, s_len, A_HEADS, A_HEAD_DIM), cos_a, sin_a)
        ka = apply_rope(ka.reshape(b_, s_len, A_HEADS, A_HEAD_DIM), cos_a, sin_a)
        va = va.reshape(b_, s_len, A_HEADS, A_HEAD_DIM)
        iq = apply_rope(iq.reshape(b_, s_len, IDX_HEADS, IDX_DIM), cos_i, sin_i)
        ik = apply_rope(ik[:, :, None, :], cos_i, sin_i)[:, :, 0, :]
        out_a = dsa_mixer(qa, ka, va, iq, ik, iw).reshape(b_, s_len, D_A_3)

        qb = apply_rope(qb.reshape(b_, s_len, 2 * B_HEADS, B_HEAD_DIM), cos_b, sin_b)
        kb = apply_rope(kb.reshape(b_, s_len, 2 * B_HEADS, B_HEAD_DIM), cos_b, sin_b)
        qb = qb.reshape(b_, s_len, B_HEADS, 2, B_HEAD_DIM)
        kb = kb.reshape(b_, s_len, B_HEADS, 2, B_HEAD_DIM)
        vb = vb.reshape(b_, s_len, B_HEADS, 2 * B_HEAD_DIM)
        lam_init = 0.8 - 0.6 * math.exp(-0.3 * layer)
        lam = (jnp.exp(jnp.sum(lam_q1[layer].astype(jnp.float32) * lam_k1[layer].astype(jnp.float32)))
               - jnp.exp(jnp.sum(lam_q2[layer].astype(jnp.float32) * lam_k2[layer].astype(jnp.float32)))
               + lam_init)
        out_b = diff_mixer(qb, kb, vb, lam, lam_init, g_subln[layer]).reshape(b_, s_len, D_B_3)

        mixed = jnp.concatenate([out_a, out_b], axis=-1)
        x = x + jnp.einsum('bsc,cd->bsd', mixed, w_out[layer])

        h2 = rms_norm_3(x, g_ffn[layer])
        gate = jnp.einsum('bsd,df->bsf', h2, w_gate[layer])
        up = jnp.einsum('bsd,df->bsf', h2, w_up[layer])
        x = x + jnp.einsum('bsf,fd->bsd', jax.nn.silu(gate) * up, w_down[layer])

    return rms_norm_3(x, g_final)


def setup_inputs(seed=0):
    out = dict(first_inputs(seed))
    for name, value in second_inputs(seed + 1).items():
        if name != "x":
            out[name + "_2"] = value
    for name, value in third_inputs(seed + 2).items():
        if name != "x":
            out[name + "_3"] = value
    return out


def reference(
    x, c, w_ada, b_ada, norm_pre_g, norm_post_g, ffn_w_gate, ffn_w_up, ffn_w_down, w_in,
    sgu_ln_g, sgu_ln_b, sgu_w, sgu_b, fox_b_f, gnorm_a_g, gnorm_b_g, w_out, ffn1_norm_pre_2,
    ffn1_norm_post_2, ffn1_w_gu_2, ffn1_w_down_2, mix_norm_pre_2, mix_norm_post_2, w_in_2,
    shift_mu_2, w_up_2, w0_2, a_up_2, a0_2, g_up_2, k_k_2, k_a_2, r_k_2, gn_w_2, gn_b_2,
    conv_dw_2, conv_b_2, conv_ln_w_2, conv_ln_b_2, w_out_2, ffn2_norm_pre_2, ffn2_norm_post_2,
    ffn2_w_gu_2, ffn2_w_down_2, w_in_3, w_out_3, g_mix_3, lam_q1_3, lam_k1_3, lam_q2_3,
    lam_k2_3, g_subln_3, g_ffn_3, w_gate_3, w_up_3, w_down_3, g_final_3,
):
    x = first_block(
        x, c, w_ada, b_ada, norm_pre_g, norm_post_g, ffn_w_gate, ffn_w_up, ffn_w_down, w_in,
        sgu_ln_g, sgu_ln_b, sgu_w, sgu_b, fox_b_f, gnorm_a_g, gnorm_b_g, w_out,
    )
    x = second_block(
        x, ffn1_norm_pre_2, ffn1_norm_post_2, ffn1_w_gu_2, ffn1_w_down_2, mix_norm_pre_2,
        mix_norm_post_2, w_in_2, shift_mu_2, w_up_2, w0_2, a_up_2, a0_2, g_up_2, k_k_2, k_a_2,
        r_k_2, gn_w_2, gn_b_2, conv_dw_2, conv_b_2, conv_ln_w_2, conv_ln_b_2, w_out_2,
        ffn2_norm_pre_2, ffn2_norm_post_2, ffn2_w_gu_2, ffn2_w_down_2,
    )
    return third_block(
        x, w_in_3, w_out_3, g_mix_3, lam_q1_3, lam_k1_3, lam_q2_3, lam_k2_3, g_subln_3, g_ffn_3,
        w_gate_3, w_up_3, w_down_3, g_final_3,
    )


_drawn_inputs = setup_inputs


def setup_inputs(seed=0):
    import zlib

    import numpy as np

    out = dict(_drawn_inputs(seed))
    spreads = {}
    factors = {'ffn1_norm_post_2': 2.754,
     'g_mix_3': 8.0,
     'lam_q1_3': 8.0,
     'lam_k1_3': 8.0,
     'lam_q2_3': 8.0,
     'lam_k2_3': 8.0,
     'g_subln_3': 25.296,
     'g_ffn_3': 8.0,
     'g_final_3': 8.881}
    for name, (base, spread) in spreads.items():
        noise = np.random.default_rng([zlib.crc32(name.encode()), seed]).standard_normal(out[name].shape)
        drawn = base * np.exp(spread * noise) if base else spread * noise
        out[name] = jnp.asarray(drawn.astype(out[name].dtype))
    for name, factor in factors.items():
        out[name] = (out[name] * factor).astype(out[name].dtype)
    return out
```

```python
from contextlib import ExitStack

import numpy as np

import concourse.bass as bass
from concourse import mybir

F32 = mybir.dt.float32
F32R = mybir.dt.float32r
BF16 = mybir.dt.bfloat16
ACT = mybir.ActivationFunctionType
ALU = mybir.AluOpType
AX = mybir.AxisListType.X

P = 128
S = 512
D = 1024
KD = D // P
FF = 2816
KF = FF // P
NT = S // P
UNIT = 16 * P
DOWN = KF // 2
SUBS = 3
VECTORS = SUBS * 3
ADA = VECTORS * KD // 2
ADA_FIRST = KD
ORDER = [4, 5, 6, 7, 0, 1, 2, 3]
EPS = 1e-6
BIG = 1.0e30


class Tally:

    def __init__(self):
        self.n = {}

    def __call__(self, name):
        return self.n.get(name, 0)

    def add(self, name, k=1):
        self.n[name] = self.n.get(name, 0) + k
        return self.n[name]


class Chain:

    def __init__(self, eng, sem):
        self.eng, self.sem, self.n = eng, sem, 0

    def __call__(self, ins):
        self.n += 1
        ins.then_inc(self.sem, 1)
        self.eng.wait_ge(self.sem, self.n)

    def mark(self, ins):
        self.n += 1
        ins.then_inc(self.sem, 1)
        return self.n

    def until(self, n):
        self.eng.wait_ge(self.sem, n)


def stream(plan):
    return [(name, i) for sub in plan["subs"] for name, count in sub["units"] for i in range(count)]


def ffn_sub(name, pre, shift, post):
    return dict(kind="ffn", name=name, pre=pre, shift=shift, post=post,
                units=[(name + "_gu", KF), (name + "_down", DOWN)])


def mix_sub(kind, name, pre, shift, post, layer=0):
    units = {
        "mix1": [("f1", 1), ("u1", 2), ("v1", 2), ("q1", 2), ("k1", 2), ("va1", 2)],
        "mix2": [("pc2", 4), ("r2", 2), ("k2", 2), ("v2", 2), ("lora2", 1)],
        "mix3": [(f"ik3_{layer}", 1), (f"iq3_{layer}", 1), (f"qa3_{layer}", 2), (f"ka3_{layer}", 2), (f"va3_{layer}", 2),
                 (f"qb3_{layer}", 2), (f"kb3_{layer}", 2), (f"vb3_{layer}", 2)],
    }[kind]
    return dict(kind=kind, name=name, pre=pre, shift=shift, post=post, layer=layer,
                units=units + [(name + "_out", 4)])


def whole_plan():
    return dict(ada=True, final="g_final", subs=[
        ffn_sub("f10", "pre0", "shift0", "post0"),
        mix_sub("mix1", "m1", "pre1", "shift1", "post1"),
        ffn_sub("f11", "pre2", "shift2", "post2"),
        ffn_sub("f20", "ffn1_pre", None, "ffn1_post_half"),
        mix_sub("mix2", "m2", "mix_pre", None, "mix_post"),
        ffn_sub("f21", "ffn2_pre", None, "ffn2_post_half"),
        mix_sub("mix3", "m30", "g_mix0", None, None, 0),
        ffn_sub("f30", "g_ffn0", None, None),
        mix_sub("mix3", "m31", "g_mix1", None, None, 1),
        ffn_sub("f31", "g_ffn1", None, None),
    ])


def build_program(nc, T, plan):
    n_w = len(stream(plan))
    ctx = ExitStack()

    def sb(name, shape, dt=F32):
        return ctx.enter_context(nc.sbuf_tensor(name, shape, dt))

    with ctx:
        X = sb("X", [P, KD, S])
        RAW = sb("RAW", [P, 2, UNIT])
        WH = sb("WH", [P, 2, UNIT], F32R)
        WL = sb("WL", [P, 2, UNIT], F32R)
        A = sb("A", [P, KF, S])
        R = sb("R", [P, S])
        R0 = sb("R0", [P, S])
        V = sb("V", [P, S])
        SG = sb("SG", [P, 2, S])
        ONES = sb("ONES", [P, P])
        PV = sb("PV", [P, T["pv"].shape[1]])
        CV = sb("CV", [P, VECTORS * KD])
        CN = sb("CN", [P, T["cn"].shape[1]])
        E = sb("E", [P, 16, S])
        with nc.sbuf_tensor("HH", [P, KD, S], F32R) as HH, nc.sbuf_tensor("HL", [P, KD, S], F32R) as HL, \
             nc.sbuf_tensor("AH", [P, 2, 2, S], F32R) as AH, nc.sbuf_tensor("AL", [P, 2, 2, S], F32R) as AL:
            pass
        G = sb("G", [P, 24, S])
        Y, SQ = A[:, 0:KD, :], A[:, KD:2 * KD, :]
        PS = [ctx.enter_context(nc.psum_tensor(f"PS{b}", [P, S], F32)) for b in range(8)]
        cols, cn = T["cols"], T["cncols"]
        sems = {}

        def sem(name):
            if name not in sems:
                sems[name] = ctx.enter_context(nc.semaphore(name))
            return sems[name]

        def col(name, m, n=1):
            for what, at in (("shift", 0), ("pre", KD), ("post", 2 * KD)):
                if name.startswith(what) and name[len(what):].isdigit():
                    c = int(name[len(what):]) * 3 * KD + at + m
                    return CV[:, c:c + n]
            return PV[:, cols[name] + m:cols[name] + m + n]

        def const(name, n=P, rows=slice(0, P)):
            return CN[rows, cn[name]:cn[name] + n]

        EPS_COL = PV[:, cols["eps"]:cols["eps"] + 1]
        raw_loaded = [sem("raw_loaded0"), sem("raw_loaded1")]
        ada_loaded = [sem("ada_loaded0"), sem("ada_loaded1")]
        w_hi, w_lo, w_used = sem("w_hi"), sem("w_lo"), sem("w_used")
        ada_used, cv_read, cv_ready, sc_ready = sem("ada_used"), sem("cv_read"), sem("cv_ready"), sem("sc_ready")
        params = sem("params")
        sq_done, stat_done, v_ready = sem("sq_done"), sem("stat_done"), sem("v_ready")
        r0_done, r_done = sem("r0_done"), sem("r_done")
        y_evac, x_done, t_ready = sem("y_evac"), sem("x_done"), sem("t_ready")
        hh_done, hl_done, out_done = sem("hh_done"), sem("hl_done"), sem("out_done")
        silu_done, act_ready = sem("silu_done"), sem("act_ready")
        ah_done, al_done = sem("ah_done"), sem("al_done")
        stored = sem("stored")
        N_PARAMS = 4 * 16

        def out_wait(eng, t, sub, j):
            if sub["kind"] == "ffn":
                if j < KD - 1:
                    eng.wait_ge(out_done, t("out") + j + 1)
                else:
                    eng.wait_ge(w_used, t("w"))
            elif j % 2 == 0:
                eng.wait_ge(out_done, t("out") + j // 2 + 1)
            else:
                eng.wait_ge(w_used, t("w") - 3 + j // 2)

        def out_passed(t, sub):
            t.add("out", KD - 1 if sub["kind"] == "ffn" else KD // 2)

        S_AT = {0: (0, 384), 1: (2, 0), 2: (0, 0), 3: (1, 0)}
        T_AT = {0: (3, 0), 1: (4, 0), 2: (5, 0), 3: (4, 384)}
        P_AT = [0, 128, 384, 768]
        K_AT = [0, 512, 896, 1152]
        N_P = 1280
        PB = G[:, 0:5, :].rearrange("p a s -> p (a s)").rearrange("p (b n) -> p b n", b=2)
        PT = G[:, 5:10, :].rearrange("p a s -> p (a s)").rearrange("p (b n) -> p b n", b=2)
        NCB = G[:, 10:12, :]
        ATT = sb("ATT", [P, 2, 4, 4])
        IDB, MKC, MKB = (sb(n, [P, P], BF16) for n in ("IDB", "MKC", "MKB"))
        scores_done, score_read = sem("scores_done"), sem("score_read")
        ncb_done, ncb_ready, neg_ready, exp_done = sem("ncb_done"), sem("ncb_ready"), sem("neg_ready"), sem("exp_done")
        p_ready, pt_done, pt_evac, pv_done, pv_evac = (sem(n) for n in ("p_ready", "pt_done", "pt_evac", "pv_done", "pv_evac"))
        proj_evac, consts_ready = sem("proj_evac"), sem("consts_ready")
        IDENT = const("ident")

        def pe_attention(pe, t, jobs):
            g0, e0, v0 = t("jobs"), t("turned"), t("pv_out")

            def scores(j):
                job, g = jobs[j], g0 + j
                if g and t("read_by_vector"):
                    pe.wait_ge(score_read, t("sread"))
                elif g:
                    pe.wait_ge(exp_done, g)
                t.n["read_by_vector"] = bool(job["ncb"])
                t.add("sread", int(bool(job["ncb"])))
                for i in range(NT):
                    b, c = S_AT[i]
                    w = (i + 1) * P
                    masks = job["masks"](i)
                    last = nc.tensor.matmul(PS[b][:, c:c + w], job["q"](i), job["k"](w), start=True, stop=not masks)
                    for n, (m, c0, cn_) in enumerate(masks):
                        last = nc.tensor.matmul(PS[b][:, c + c0:c + c0 + cn_], IDB[:], m, start=False,
                                                stop=n == len(masks) - 1)
                last.then_inc(scores_done, 1)
                if job["ncb"]:
                    if t("ncb"):
                        pe.wait_ge(ncb_ready, t("ncb"))
                    t.add("ncb")
                    nc.tensor.matmul(PS[7][:], *job["ncb"], start=True, stop=True).then_inc(ncb_done, 1)

            def turn(j):
                g, e = g0 + j, t.add("turned")
                pe.wait_ge(p_ready, e)
                if e > 1:
                    pe.wait_ge(pt_evac, e - 1)
                for i in range(NT):
                    for k in range(i + 1):
                        b, c = T_AT[k]
                        c += (i - k) * P
                        last = nc.tensor.transpose(PS[b][:, c:c + P],
                                                   PB[:, j % 2, P_AT[i] + k * P:P_AT[i] + (k + 1) * P], IDENT)
                last.then_inc(pt_done, 1)

            def attend(j):
                job, e = jobs[j], t("turned")
                pe.wait_ge(pt_evac, e)
                if job["first"] and t("pv_out"):
                    pe.wait_ge(pv_evac, t("pv_out"))
                r0, r1 = job["rows"]
                for k in range(NT):
                    last = nc.tensor.matmul(PS[6][r0:r1, k * P:S], job["v"](k), PT[:, e % 2, K_AT[k]:K_AT[k] + S - k * P],
                                            start=k == 0, stop=k == NT - 1)
                last.then_inc(pv_done, 1)
                if job["dest"] is not None:
                    t.add("pv_out")

            scores(0)
            for j, job in enumerate(jobs):
                if j + 1 < len(jobs):
                    scores(j + 1)
                if job["turn"]:
                    turn(j)
                    attend(j)
            t.add("jobs", len(jobs))

        def act_attention(act, t, jobs):
            g0 = t("jobs")

            def exps(j):
                job, g = jobs[j], g0 + j
                if job["ncb"]:
                    act.wait_ge(ncb_done, t.add("ncb"))
                    if t("ncb") > 2:
                        act.wait_ge(neg_ready, g - 1)
                    nc.scalar.activation(NCB[:, j % 2, :], PS[7][:], ACT.Copy).then_inc(ncb_ready, 1)
                if not job["turn"] and j:
                    act.wait_ge(p_ready, t("turned") + 1)
                act.wait_ge(neg_ready, g + 1)
                for i in range(NT):
                    b, c = S_AT[i]
                    w = (i + 1) * P
                    p = PB[:, j % 2, P_AT[i]:P_AT[i] + w]
                    last = nc.scalar.activation(p, p if job["ncb"] else PS[b][:, c:c + w], ACT.Exp,
                                                bias=ATT[:, j % 2, 1, i:i + 1], scale=job["scale"],
                                                accum_out=ATT[:, j % 2, 2, i:i + 1])
                last.then_inc(exp_done, 1)

            def copy_turned(j):
                e = t.add("turned")
                act.wait_ge(pt_done, e)
                if e > 2:
                    act.wait_ge(pv_done, e - 2)
                for b, n, at in ((3, 512, 0), (5, 256, 896)):
                    nc.scalar.activation(PT[:, e % 2, at:at + n], PS[b][:, 0:n], ACT.Copy)
                nc.scalar.activation(PT[:, e % 2, 512:896], PS[4][:, 0:384], ACT.Copy)
                nc.scalar.activation(PT[:, e % 2, 1152:1280], PS[4][:, 384:512], ACT.Copy).then_inc(pt_evac, 1)

            exps(0)
            for j, job in enumerate(jobs):
                if j + 1 < len(jobs):
                    exps(j + 1)
                if job["turn"]:
                    copy_turned(j)
            t.add("jobs", len(jobs))

        def dve_attention(dve, t, jobs, chain, between=lambda j: None):
            g0 = t("jobs")

            def maxima(j):
                job, g = jobs[j], g0 + j
                mx, nm = ATT[:, j % 2, 0, :], ATT[:, j % 2, 1, :]
                dve.wait_ge(scores_done, g + 1)
                if job["ncb"]:
                    dve.wait_ge(ncb_ready, t.add("ncb"))
                if job["ncb"] and t("turned"):
                    dve.wait_ge(pt_done, t("turned"))
                for i in range(NT):
                    b, c = S_AT[i]
                    w = (i + 1) * P
                    if job["ncb"]:
                        last = nc.vector.tensor_tensor_reduce(
                            out=PB[:, j % 2, P_AT[i]:P_AT[i] + w], in0=PS[b][:, c:c + w], in1=NCB[:, j % 2, 0:w],
                            scale=1.0, scalar=-3.0e38, op0=ALU.add, op1=ALU.max, accum_out=mx[:, i:i + 1])
                    else:
                        last = nc.vector.reduce_max(mx[:, i:i + 1], PS[b][:, c:c + w], AX)
                if job["ncb"]:
                    last.then_inc(score_read, 1)
                    dve.wait_ge(score_read, t.add("sread"))
                else:
                    chain(last)
                nc.vector.tensor_scalar(nm, mx, -job["scale"], None, ALU.mult).then_inc(neg_ready, 1)

            def scale(j):
                job, g = jobs[j], g0 + j
                rs, rc = ATT[:, j % 2, 2, :], ATT[:, j % 2, 3, :]
                dve.wait_ge(exp_done, g + 1)
                chain(nc.vector.reciprocal(rc, rs))
                if job["minus"] is not None:
                    chain(nc.vector.tensor_scalar(rc, rc, job["minus"], None, ALU.mult))
                for i in range(NT):
                    w = (i + 1) * P
                    p, first = (PB[:, x, P_AT[i]:P_AT[i] + w] for x in (j % 2, (j + 1) % 2))
                    if job["minus"] is not None:
                        last = nc.vector.scalar_tensor_tensor(p, p, rc[:, i:i + 1], first, ALU.mult, ALU.add)
                    else:
                        last = nc.vector.tensor_scalar(p, p, rc[:, i:i + 1], None, ALU.mult)
                if job["turn"]:
                    last.then_inc(p_ready, 1)
                    t.add("turned")
                else:
                    chain(last)

            def copy_out(j):
                if jobs[j]["turn"] and jobs[j]["dest"] is not None:
                    dve.wait_ge(pv_done, t("turned_out") + 1)
                    nc.vector.tensor_copy(jobs[j]["dest"], PS[6][:]).then_inc(pv_evac, 1)
                if jobs[j]["turn"]:
                    t.add("turned_out")

            maxima(0)
            for j in range(len(jobs)):
                if j + 1 < len(jobs):
                    maxima(j + 1)
                scale(j)
                if j:
                    copy_out(j - 1)
            copy_out(len(jobs) - 1)
            t.add("jobs", len(jobs))
            t.add("pv_out", sum(job["dest"] is not None for job in jobs))
            dve.wait_ge(pv_evac, t("pv_out"))

        def pe_bank(pe, t, j):
            if j >= 8:
                pe.wait_ge(proj_evac, t("proj") + j - 7)
            return j % 8

        def pe_token_major(pe, h, w, banks):
            for u in range(2):
                h["unit_arrives"](w + u)
                wh, wl = (x[:, (w + u) % 2, :].rearrange("p (k c) -> p k c", k=4) for x in (WH, WL))
                for k in range(4):
                    kk = 4 * u + k
                    for i, b in enumerate(banks):
                        last = h["mm3"](PS[b][:], HH[:, kk, i * P:(i + 1) * P], HL[:, kk, i * P:(i + 1) * P],
                                        wh[:, k, :], wl[:, k, :], kk == 0, kk == KD - 1)
                last.then_inc(w_used, 1)

        U1, V1, Q1 = E[:, 0:4, :], E[:, 4:8, :], E[:, 8:16, :]
        K1, VA1, YB1 = A[:, 4:8, :], G[:, 16:20, :], G[:, 12:16, :]
        WT1, YA1 = A[:, 16:18, :].rearrange("p a (h i) -> p (a h) i", i=P), A[:, 18:22, :]
        LNG, LNB, SGB = G[:, 20, :], G[:, 21, :], G[:, 22, :]
        F1, F2, NC1 = (A[0:8, c, :] for c in (12, 13, 14))
        ST1 = sb("ST1", [P, NT, 12])
        m1_loads, q_zero, wt_masked, v_ready1, ln_r0 = (sem(n) for n in ("m1_loads", "q_zero", "wt_masked", "v_ready1", "ln_r0"))
        ln_var, v_normed, sgu_done, ya_ready, lf_done, nc_ready, ya_sq = (
            sem(n) for n in ("ln_var", "v_normed", "sgu_done", "ya_ready", "lf_done", "nc_ready", "ya_sq"))
        sgu_read = sem("sgu_read")

        def jobs_fox():
            def job(h):
                m, par = h // 2, h % 2
                return dict(q=lambda i: Q1[:, h, i * P:(i + 1) * P], k=lambda w: K1[:, m, 0:w],
                            masks=lambda i: [(MKC[:], i * P, P)], scale=1.0,
                            ncb=(IDENT[0:8, h:h + 1].to_broadcast([8, P]), NC1),
                            v=lambda k: VA1[:, k, h * 64:(h + 1) * 64], rows=(64 * par, 64 * par + 64),
                            first=par == 0, dest=YB1[:, m, :] if par else None, turn=True, minus=None)
            return [job(h) for h in range(8)]

        def pool_mix1(pool):
            if plan["ada"]:
                pool.wait_ge(ada_used, ADA)
            pool.memset(E[:, 8:16, :], 0.0).then_inc(q_zero, 1)
            pool.wait_ge(w_used, M1_START)
            pool.wait_ge(hl_done, M1_HL)
            pool.dma_start(WT1, T["sgu_w"]).then_inc(m1_loads, 16)
            for x, name in ((LNG, "ln_g"), (LNB, "ln_b"), (SGB, "sgu_b")):
                pool.dma_start(x, T[name]).then_inc(m1_loads, 16)

        def pe_mix1(pe, t, sub, h):
            w = t("w")
            t.add("hl", KD)
            h["unit_arrives"](w)
            wh, wl = h["blocks"](w)
            for k in range(KD):
                pe.wait_ge(hl_done, t("hl") - KD + k + 1)
                last = h["mm3"](PS[0][:], wh[:, k, :], wl[:, k, :], HH[:, k, :], HL[:, k, :], k == 0, k == KD - 1)
            last.then_inc(w_used, 1)
            j = 1
            at = w + 1
            for what in "uvqka":
                if what in "va":
                    banks = [pe_bank(pe, t, j + i) for i in range(4)]
                    pe_token_major(pe, h, at, banks)
                else:
                    for u in range(2):
                        h["unit_arrives"](at + u)
                        banks = [pe_bank(pe, t, j + 2 * u + c) for c in range(2)]
                        h["project"](at + u, banks).then_inc(w_used, 1)
                at += 2
                j += 4
            pe.wait_ge(v_normed, 1)
            pe.wait_ge(wt_masked, 1)
            pe.wait_ge(proj_evac, t("proj") + j)
            t.add("proj", j)
            for m in range(4):
                for par in range(2):
                    hd = 2 * m + par
                    for n in range(NT):
                        last = nc.tensor.matmul(PS[m][64 * par:64 * par + 64, n * P:(n + 1) * P],
                                                V1[:, n, hd * 64:(hd + 1) * 64], WT1[:, hd, :], start=True, stop=True)
                last.then_inc(sgu_done, 1)
            h["norm"](4)
            pe.wait_ge(nc_ready, 1)
            pe.wait_ge(ya_ready, 4)
            pe.wait_ge(r_done, t("norms"))
            pe_attention(pe, t, jobs_fox())
            h["norm"](4)
            t.add("w", 11)

        def act_mix1(act, t, sub, h):
            w, split, chain = t("w"), h["split"], h["chain"]

            def done(n):
                act.wait_ge(w_used, w + n + 1)

            done(0)
            chain(nc.scalar.activation(F1, PS[0][0:8, :], ACT.Identity, bias=PV[0:8, cols["fox_b"]:cols["fox_b"] + 1]))
            nc.scalar.activation(F2, F1, ACT.Abs).then_inc(proj_evac, 1)
            split(w + 2)
            for n in (1, 2):
                done(n)
                for c in range(2):
                    m = 2 * (n - 1) + c
                    nc.scalar.activation(U1[:, m, :], PS[(1 + m) % 8][:], ACT.Gelu_apprx_tanh).then_inc(proj_evac, 1)
                split(w + n + 2)
            done(3)
            split(w + 5)
            done(4)
            for i in range(NT):
                nc.scalar.activation(V1[:, i, :], PS[(5 + i) % 8][:], ACT.Gelu_apprx_tanh).then_inc(proj_evac, 1)
            split(w + 6)
            act.wait_ge(q_zero, 1)
            for n in (5, 6):
                done(n)
                for c in range(2):
                    m = 2 * (n - 5) + c
                    ps = PS[(9 + m) % 8]
                    nc.scalar.activation(Q1[0:64, 2 * m, :], ps[0:64, :], ACT.Copy, scale=0.125)
                    nc.scalar.activation(Q1[64:P, 2 * m + 1, :], ps[64:P, :], ACT.Copy, scale=0.125)\
                        .then_inc(proj_evac, 1)
                split(w + n + 2)
            for n in (7, 8):
                done(n)
                for c in range(2):
                    m = 2 * (n - 7) + c
                    nc.scalar.activation(K1[:, m, :], PS[(13 + m) % 8][:], ACT.Copy).then_inc(proj_evac, 1)
                split(w + n + 2)
            act.wait_ge(ln_var, 1)
            chain(nc.scalar.activation(ST1[:, :, 8], ST1[:, :, 7], ACT.Ln))
            nc.scalar.activation(ST1[:, :, 8], ST1[:, :, 8], ACT.Exp, scale=-0.5).then_inc(ln_r0, 1)
            chain(nc.scalar.activation(F2, F2, ACT.Exp, scale=-1.0))
            nc.scalar.activation(F2, F2, ACT.Ln, bias=1.0).then_inc(lf_done, 1)
            done(9)
            split(w + 11)
            done(10)
            for i in range(NT):
                nc.scalar.activation(VA1[:, i, :], PS[(17 + i) % 8][:], ACT.Copy).then_inc(proj_evac, 1)
            split(w + 12)
            t.add("w", 11)
            for m in range(4):
                act.wait_ge(ya_ready, m + 1)
                nc.scalar.activation(SQ[:, m, :], YA1[:, m, :], ACT.Square).then_inc(sq_done, 1)
            h["rsqrt"]()
            act_attention(act, t, jobs_fox())
            for m in range(4):
                act.wait_ge(pv_evac, m + 1)
                nc.scalar.activation(SQ[:, m, :], YB1[:, m, :], ACT.Square).then_inc(sq_done, 1)
            h["rsqrt"]()
            h["high"](Y)

        def dve_mix1(dve, t, sub, h):
            w, split, chain = t("w"), h["split"], h["chain"]
            dve.wait_ge(m1_loads, 4 * 16)
            nc.vector.memset(WT1[64:P, :, 0:64], 0.0).then_inc(wt_masked, 1)
            for n in range(5):
                split(w + n + 2)
            base = t("proj")
            for i in range(NT):
                dve.wait_ge(proj_evac, base + 6 + i)
                chain(nc.vector.bn_stats(ST1[:, i, 0:6], V1[:, i, :]))
                chain(nc.vector.bn_aggr(ST1[:, i, 6:8], ST1[:, i, 0:6]))
            chain(nc.vector.tensor_copy(ST1[:, :, 9], ST1[:, :, 6]))
            nc.vector.tensor_scalar(ST1[:, :, 7], ST1[:, :, 7], EPS, None, ALU.add).then_inc(ln_var, 1)
            for n in (5, 6, 7, 8):
                split(w + n + 2)
            v_, r0_, tmp = ST1[:, :, 7], ST1[:, :, 8], ST1[:, :, 10]
            dve.wait_ge(ln_r0, 1)
            chain(nc.vector.tensor_tensor(tmp, r0_, r0_, ALU.mult))
            chain(nc.vector.tensor_tensor(tmp, tmp, v_, ALU.mult))
            chain(nc.vector.tensor_scalar(tmp, tmp, -0.5, 1.5, ALU.mult, ALU.add))
            chain(nc.vector.tensor_tensor(tmp, tmp, r0_, ALU.mult))
            for i in range(NT):
                v = V1[:, i, :]
                chain(nc.vector.tensor_scalar(v, v, ST1[:, i, 9:10], ST1[:, i, 10:11], ALU.subtract, ALU.mult))
                chain(nc.vector.tensor_tensor(v, v, LNG, ALU.mult))
                last = nc.vector.tensor_tensor(v, v, LNB, ALU.add)
                if i < NT - 1:
                    chain(last)
            last.then_inc(v_normed, 1)
            dve.wait_ge(lf_done, 1)
            chain(nc.vector.scalar_tensor_tensor(F1, F1, 0.0, F2, ALU.min, ALU.subtract))
            chain(nc.vector.memset(F2, 1.0))
            chain(nc.vector.tensor_tensor_scan(NC1, F2, F1, 0.0, ALU.mult, ALU.add))
            nc.vector.tensor_scalar(NC1, NC1, -1.0, None, ALU.mult).then_inc(nc_ready, 1)
            split(w + 11)
            split(w + 12)
            t.add("w", 11)
            t.add("proj", 21)
            for m in range(4):
                dve.wait_ge(sgu_done, m + 1)
                ya = YA1[:, m, :].rearrange("p (n i) -> p n i", n=NT)
                bias = SGB[:, m * P:(m + 1) * P].unsqueeze(1).to_broadcast([P, NT, P])
                chain(nc.vector.tensor_tensor(ya, PS[m][:].rearrange("p (n i) -> p n i", n=NT), bias, ALU.add))
                nc.vector.tensor_tensor(YA1[:, m, :], YA1[:, m, :], U1[:, m, :], ALU.mult).then_inc(ya_ready, 1)
            h["rsqrt"](4)
            dve.wait_ge(ya_ready, 4)
            for m in range(4):
                nc.vector.scalar_tensor_tensor(Y[:, m, :], YA1[:, m, :], col("gnorm_a", m), R[:], ALU.mult, ALU.mult)\
                    .then_inc(t_ready, 1)
            dve_attention(dve, t, jobs_fox(), chain)
            h["rsqrt"](4)
            lo = h["low"](Y)
            for m in range(4):
                nc.vector.scalar_tensor_tensor(Y[:, 4 + m, :], YB1[:, m, :], col("gnorm_b", m), R[:], ALU.mult, ALU.mult)\
                    .then_inc(t_ready, 1)
                lo(m)
            for m in range(4, 8):
                lo(m)

        kinds_ = [sub_["kind"] for sub_ in plan["subs"]]
        QA3, KA3, VA3 = E[:, 0:8, :], E[:, 8:12, :], E[:, 12:16, :]
        QB3, KB3, VB3 = A[:, 0:8, :], A[:, 8:12, :], A[:, 12:16, :]
        IQ3, IK3, OB3 = A[:, 16:18, :], A[:, 18, :], G[:, 12:16, :]
        SC3 = A[:, 19:22, :].rearrange("p a s -> p (a s)")
        SC_AT = {1: 0, 2: 256, 3: 640}
        ROPE = {64: (G[:, 16, :], G[:, 17, :]), 32: (G[:, 18, :], G[:, 19, :])}
        TURN3 = G[:, 20:22, :]
        MK3 = G[:, 22:24, :].rearrange("p a s -> p (a s)").bitcast(BF16)
        W3 = sb("W3", [P, NT, 8])
        M8 = sb("M8", [P, 8])
        LAM = sb("LAM", [P, 8])
        m3_loads, q3_zero, rot_done, roped = (sem(n) for n in ("m3_loads", "q3_zero", "rot_done", "roped"))
        dots_done, dots_read, weighed, keys_taken = (sem(n) for n in ("dots_done", "dots_read", "weighed", "keys_taken"))
        lam_in, lam_sum, lam_exp = sem("lam_in"), sem("lam_sum"), sem("lam_exp")
        TOPK = 128
        MARK = -3.0e38
        LAM_INIT = [0.8 - 0.6 * float(np.exp(-0.3 * layer)) for layer in range(2)]
        N_PROJ3 = 28
        ROPED = [(0, 0, 32, [(IK3, slice(0, P))])] + [(1, c, 32, [(IQ3[:, c, :], slice(0, P))]) for c in range(2)]
        for first_unit, q_ in ((2, QA3), (8, QB3)):
            for m_ in range(4):
                ROPED.append((first_unit + m_ // 2, m_ % 2, 64,
                              [(q_[:, 2 * m_, :], slice(0, 64)), (q_[:, 2 * m_ + 1, :], slice(64, P))]))
        for first_unit, k_ in ((4, KA3), (10, KB3)):
            for m_ in range(4):
                ROPED.append((first_unit + m_ // 2, m_ % 2, 64, [(k_[:, m_, :], slice(0, P))]))
        ROPED.sort(key=lambda r: (r[0], r[1]))
        ROUNDS = [(i, n) for i in (1, 2, 3) for n in range(TOPK // 8)]
        DOTS = [(i, hd) for i in (1, 2, 3) for hd in range(8)]
        DOTS_AFTER = {3: DOTS[0:8], 4: DOTS[8:16], 5: DOTS[16:24]}
        U3 = 14
        TOKENS3 = {6: (VA3, 0), 7: (VA3, 1), 12: (VB3, 0), 13: (VB3, 1)}

        def turns_of(u):
            return [(n, r) for n, r in enumerate(ROPED) if r[0] == u]

        AUX3 = [("lambda", 0)]
        for u_ in range(1, U3):
            AUX3 += [("turn", n) for n, _ in turns_of(u_ - 1)] + [("dots", d) for d in DOTS_AFTER.get(u_, [])]
        BANK3 = {key: 6 + n % 2 for n, key in enumerate(AUX3)}
        PROJ3, n_ = {}, 0
        for u_ in range(U3):
            k_ = {0: 2, 6: 0, 7: 4, 12: 0, 13: 4}.get(u_, 2)
            PROJ3[u_] = list(range(n_, n_ + k_))
            n_ += k_
        assert n_ == N_PROJ3

        def jobs_dsa():
            def job(hd):
                m, par = hd // 2, hd % 2
                return dict(q=lambda i: QA3[:, hd, i * P:(i + 1) * P], k=lambda w: KA3[:, m, 0:w],
                            masks=lambda i: [(MKB[:], 0, P)] if i == 0 else
                            [(MK3[:, SC_AT[i]:SC_AT[i] + (i + 1) * P], 0, (i + 1) * P)],
                            scale=0.125, ncb=None, v=lambda k: VA3[:, k, hd * 64:(hd + 1) * 64],
                            rows=(64 * par, 64 * par + 64), first=par == 0,
                            dest=Y[:, m, :] if par else None, turn=True, minus=None)
            return [job(hd) for hd in range(8)]

        def jobs_diff():
            def job(hd, c):
                return dict(q=lambda i: QB3[:, 2 * hd + c, i * P:(i + 1) * P], k=lambda w: KB3[:, hd, 0:w],
                            masks=lambda i: [(MKB[:], i * P, P)], scale=0.125, ncb=None,
                            v=lambda k: VB3[:, k, hd * P:(hd + 1) * P], rows=(0, P), first=True,
                            dest=OB3[:, hd, :] if c else None, turn=c == 1, minus=LAM[:, 7:8] if c else None)
            return [job(hd, c) for hd in range(4) for c in range(2)]

        def pool_mix3(pool, name):
            w0, hl0 = starts[name]
            pool.wait_ge(hl_done, hl0)
            pool.wait_ge(w_used, w0)
            for to, n in zip(ROPE[64] + ROPE[32], ("cos64", "sin64", "cos32", "sin32")):
                pool.dma_start(to, T[n]).then_inc(m3_loads, 16)
            pool.memset(QA3, 0.0)
            pool.memset(QB3, 0.0).then_inc(q3_zero, 1)

        def pe_mix3(pe, t, sub, h):
            w, proj0, turns0, dots0 = t("w"), t("proj"), t("turns"), t("dots")
            t.add("hl", KD)

            def bank(j):
                if j >= 6:
                    pe.wait_ge(proj_evac, proj0 + j - 5)
                return PS[j % 6]

            def aux(key):
                n = AUX3.index(key)
                if n >= 2:
                    kind, before = AUX3[n - 2]
                    if kind == "turn":
                        pe.wait_ge(roped, turns0 + before + 1)
                    elif kind == "dots":
                        pe.wait_ge(dots_read, dots0 + DOTS.index(before) + 1)
                    else:
                        pe.wait_ge(lam_exp, t("lam"))
                return PS[BANK3[key]]

            def turn(u):
                for n, r in turns_of(u):
                    pe.wait_ge(proj_evac, proj0 + PROJ3[u][r[1]] + 1)
                    ps = aux(("turn", n))
                    nc.tensor.matmul(ps[:], const(f"rot{r[2]}"), TURN3[:, r[1], :], start=True, stop=True)\
                        .then_inc(rot_done, 1)

            h["unit_arrives"](w)
            wh, wl = h["blocks"](w)
            ps = bank(0)
            for k in range(KD):
                pe.wait_ge(hl_done, t("hl") - KD + k + 1)
                h["mm3"](ps[:], wh[:, k, :], wl[:, k, :], HH[:, k, :], HL[:, k, :], k == 0, k == KD - 1)
            ps = bank(1)
            for i in range(NT):
                for k in range(KD):
                    last = h["mm3"](ps[:, 8 * i:8 * i + 8], HH[:, k, i * P:(i + 1) * P], HL[:, k, i * P:(i + 1) * P],
                                    wh[:, KD + k, 0:8], wl[:, KD + k, 0:8], k == 0, k == KD - 1)
            last.then_inc(w_used, 1)
            pe.wait_ge(lam_in, t.add("lam"))
            nc.tensor.matmul(aux(("lambda", 0))[:, 0:2], ONES[:], LAM[:, 0:2], start=True, stop=True).then_inc(lam_sum, 1)
            for u in range(1, U3):
                if u not in TOKENS3:
                    h["unit_arrives"](w + u)
                    for j in PROJ3[u]:
                        bank(j)
                    h["project"](w + u, [j % 6 for j in PROJ3[u]]).then_inc(w_used, 1)
                elif TOKENS3[u][1] == 0:
                    for j in PROJ3[u + 1]:
                        bank(j)
                    pe_token_major(pe, h, w + u, [j % 6 for j in PROJ3[u + 1]])
                turn(u - 1)
                for d in DOTS_AFTER.get(u, []):
                    i, hd = d
                    if d == DOTS[0]:
                        pe.wait_ge(roped, turns0 + 3)
                    r0 = 32 * (hd % 4)
                    ps = aux(("dots", d))
                    nc.tensor.matmul(ps[:, 0:(i + 1) * P], IQ3[r0:r0 + 32, hd // 4, i * P:(i + 1) * P],
                                     IK3[r0:r0 + 32, 0:(i + 1) * P], start=True, stop=True).then_inc(dots_done, 1)
            t.add("turns", len(ROPED))
            t.add("dots", len(DOTS))
            t.add("proj", N_PROJ3)
            pe.wait_ge(proj_evac, t("proj"))
            pe.wait_ge(roped, t("turns"))
            pe_attention(pe, t, jobs_diff())
            pe.wait_ge(keys_taken, t.add("keys_taken"))
            pe_attention(pe, t, jobs_dsa())
            pe.wait_ge(pv_evac, t("pv_out"))
            for m in range(4):
                h["norm"](1, src=SQ[:, m:m + 1, :])
            t.add("w", U3)

        def act_mix3(act, t, sub, h):
            w, split, turns0, dots0 = t("w"), h["split"], t("turns"), t("dots")
            for u in range(U3):
                act.wait_ge(w_used, w + u + 1)
                split(w + u + 2)
                for c, j in enumerate(PROJ3[u]):
                    ps = PS[j % 6]
                    if u in TOKENS3:
                        ins = nc.scalar.activation(TOKENS3[u][0][:, c, :], ps[:], ACT.Copy)
                    elif u == 0 and c == 1:
                        ins = nc.scalar.activation(W3[:].rearrange("p i h -> p (i h)"), ps[:, 0:8 * NT], ACT.Copy,
                                                   scale=float(8 ** -0.5))
                    else:
                        before = [n for n, r in enumerate(ROPED) if r[0] < u]
                        if before and c == 0:
                            act.wait_ge(roped, turns0 + before[-1] + 1)
                        ins = nc.scalar.activation(TURN3[:, c, :], ps[:], ACT.Copy)
                    ins.then_inc(proj_evac, 1)
                if u == 0:
                    act.wait_ge(lam_sum, t.add("lam"))
                    nc.scalar.activation(LAM[:, 2:4], PS[BANK3["lambda", 0]][:, 0:2], ACT.Exp).then_inc(lam_exp, 1)
                for i, hd in DOTS_AFTER.get(u, []):
                    n = dots0 + DOTS.index((i, hd)) + 1
                    act.wait_ge(dots_done, n)
                    if n > 2:
                        act.wait_ge(weighed, n - 2)
                    nc.scalar.activation(SG[:, n % 2, 0:(i + 1) * P], PS[BANK3["dots", (i, hd)]][:, 0:(i + 1) * P],
                                         ACT.Relu, scale=float(32 ** -0.5)).then_inc(dots_read, 1)
            t.add("w", U3)
            t.add("turns", len(ROPED))
            t.add("dots", len(DOTS))
            act_attention(act, t, jobs_diff())
            act_attention(act, t, jobs_dsa())
            t.add("pv_out", 8)
            act.wait_ge(pv_evac, t("pv_out") + 4 * bool("mix1" in kinds_))
            for m in range(4):
                nc.scalar.activation(SQ[:, m, :], OB3[:, m, :], ACT.Square).then_inc(sq_done, 1)
                h["rsqrt"]()
            h["high"](Y, given=4)

        def dve_mix3(dve, t, sub, h):
            w, split, chain = t("w"), h["split"], h["chain"]
            turns0, dots0, layer = t("turns"), t("dots"), sub["layer"]
            dve.wait_ge(m3_loads, 64 * t.add("m3"))
            dve.wait_ge(q3_zero, t("m3"))
            lam = cols[f"lam{layer}"]
            nc.vector.tensor_tensor(LAM[:, 0:2], PV[:, lam:lam + 2], PV[:, lam + 2:lam + 4], ALU.mult).then_inc(lam_in, 1)
            g_sub = col(f"g_sub{layer}", 0)
            chain(nc.vector.tensor_scalar(g_sub, g_sub, 1.0 - LAM_INIT[layer], None, ALU.mult))
            rounds = list(ROUNDS)

            def rope(n, r):
                _, c, size, places = r
                cos, sin = ROPE[size]
                chain(nc.vector.tensor_tensor(V[:], TURN3[:, c, :], cos, ALU.mult))
                dve.wait_ge(rot_done, turns0 + n + 1)
                chain(nc.vector.tensor_tensor(R[:], PS[BANK3["turn", n]][:], sin, ALU.mult))
                for to, rows in places:
                    last = nc.vector.tensor_tensor(to[rows, :], V[rows, :], R[rows, :], ALU.add)
                last.then_inc(roped, 1)
                dve.wait_ge(roped, turns0 + n + 1)

            def scores(i):
                return SC3[:, SC_AT[i]:SC_AT[i] + (i + 1) * P]

            def weigh(i, hd):
                n = dots0 + DOTS.index((i, hd)) + 1
                dve.wait_ge(dots_read, n)
                relu, weight = SG[:, n % 2, 0:(i + 1) * P], W3[:, i, hd:hd + 1]
                if hd == 0:
                    ins = nc.vector.tensor_scalar(scores(i), relu, weight, None, ALU.mult)
                else:
                    ins = nc.vector.scalar_tensor_tensor(scores(i), relu, weight, scores(i), ALU.mult, ALU.add)
                ins.then_inc(weighed, 1)
                dve.wait_ge(weighed, n)
                if hd == 7:
                    chain(nc.vector.memset(SC3[0:64, SC_AT[i] + i * P + 64:SC_AT[i] + (i + 1) * P], -BIG))

            def take(i, n):
                chain(nc.vector.max(M8[:], scores(i)))
                chain(nc.vector.match_replace(scores(i), M8[:], scores(i), MARK))
                if n == TOPK // 8 - 1:
                    ins = nc.vector.tensor_scalar(MK3[:, SC_AT[i]:SC_AT[i] + (i + 1) * P], scores(i), MARK / 2, -BIG,
                                                  ALU.is_gt, ALU.mult)
                    if i == 3:
                        ins.then_inc(keys_taken, 1)

            for u in range(U3):
                split(w + u + 2)
                for n, r in turns_of(u - 1):
                    rope(n, r)
                for d in DOTS_AFTER.get(u, []):
                    weigh(*d)
                if u == 1:
                    dve.wait_ge(lam_exp, t.add("lam"))
                    chain(nc.vector.tensor_tensor(LAM[:, 7:8], LAM[:, 3:4], LAM[:, 2:3], ALU.subtract))
                    chain(nc.vector.tensor_scalar(LAM[:, 7:8], LAM[:, 7:8], -LAM_INIT[layer], None, ALU.add))
                if u >= 6:
                    for _ in range(6):
                        take(*rounds.pop(0))
            assert not rounds
            t.add("w", U3)
            t.add("turns", len(ROPED))
            t.add("dots", len(DOTS))
            dve_attention(dve, t, jobs_diff(), chain)
            dve_attention(dve, t, jobs_dsa(), chain)
            lo = h["low"](Y)
            for m in range(4):
                h["rsqrt"](1)
                nc.vector.scalar_tensor_tensor(Y[:, 4 + m, :], OB3[:, m, :], g_sub, R[:], ALU.mult, ALU.mult)\
                    .then_inc(t_ready, 1)
            for m in range(8):
                lo(m)

        CH = 64
        NC2 = S // CH
        U2 = 11
        DECAY = float(np.exp(-0.5))
        TAPS = 31
        R2, K2, V2 = E[:, 0:4, :], E[:, 4:8, :], E[:, 8:12, :]
        LO2, XG2, SEG2 = E[:, 12, :], E[:, 13, :], E[:, 14, :]
        C2 = A[:, 16:20, :]
        GLU = A[:, 8:13, :].rearrange("p a s -> p (a s)")[:, 0:4 * (S + TAPS - 1)].rearrange("p (m s) -> p m s", m=4)
        RP2 = G[:, 16:21, :].rearrange("p a s -> p (a s)")[:, 0:4 * (S + 1)].rearrange("p (m s) -> p m s", m=4)
        B2, LW2, KK2, CC2, BV2 = G[:, 0:4, :], G[:, 4:8, :], G[:, 8:12, :], G[:, 12:16, :], G[:, 16:20, :]
        T2, V2W, R0W, RW = A[:, 0:4, :], A[:, 4:8, :], A[:, 8:12, :], A[:, 12:16, :]
        BH2, KH2, MU2 = G[:, 20, :], G[:, 21, :], E[:, 15, :]
        LEVELS = G[:, 22:24, :].rearrange("p a s -> p (a s)")
        TOK2 = A[:, 0:4, :]
        AU2 = A[:, 4:12, :]
        TI2 = A[:, 12:16, :]
        ML2, XS2, AV2, TZ2 = G[:, 4:6, :], G[:, 6:8, :], G[:, 12, :], G[:, 13:15, :]
        HS2 = A[:, 12:16, :].rearrange("p a (c v) -> p (a c) v", v=CH)
        PC2 = sb("PC2", [P, 4, NC2])
        LU2, GU2 = A[:, 20, :], A[:, 21, :]
        m2_loads, m2_zero, glu_done, gate_done, shifted = (
            sem(n) for n in ("m2_loads", "m2_zero", "glu_done", "gate_done", "shifted"))
        silu2 = sem("silu2")
        CHUNKS2 = 14

        pe_steps = [("decay", m) for m in range(4)] + [("rate", m) for m in range(4)] \
            + [("kk", m) for m in range(4)] + [("bonus", m) for m in range(4)]
        act_steps = [("low rank",), ("sig d",), ("sig a",), ("kk sq",), ("kk r0",), ("before",), ("inverse",), ("decays",)]
        dve_steps = [("kk raw",), ("kk v",), ("rk",), ("lw",), ("sums",), ("scaled",)]
        for m_ in range(4):
            pe_steps += [("tok", m_, x) for x in range(4)] + [("au", m_, n, par) for n in range(NT) for par in range(2)]
            pe_steps += [("av", m_)]
            act_steps += [("tok", m_, x) for x in range(4)] + [("av", m_)]
            dve_steps += [("hat", m_)] + [("au", m_, n, par) for n in range(NT) for par in range(2)] + [("ml", m_, 0, par) for par in range(2)]
            for l_ in range(6):
                pe_steps += [("x", m_, l_, par) for par in range(2)] + [("t", m_, l_, par) for par in range(2)]
                act_steps += [("x", m_, l_, par) for par in range(2)]
                for par_ in range(2):
                    dve_steps += [("t", m_, l_, par_)]
                    if l_ < 5:
                        dve_steps += [("ml", m_, l_ + 1, par_)]
            pe_steps += [("tz", m_, 0), ("tz", m_, 1), ("r", m_), ("yl", m_), ("mg", m_, 0), ("mg", m_, 1)]
            act_steps += [("tz", m_, 0), ("tz", m_, 1), ("yl", m_), ("mg", m_, 0), ("mg", m_, 1)]
            dve_steps += [("r", m_)]
        pe_steps += [("h", c) for c in range(NC2 - 1)] + [("y", m) for m in range(4)]
        dve_steps += [("h", c) for c in range(NC2)]
        for m_ in range(4):
            dve_steps += [("y", m_)]
        pe_steps += [("mean", m) for m in range(4)] + [("c mean",)]
        dve_steps += [("centred", m) for m in range(4)] + [("c centred",)]
        pe_steps += [("g", m) for m in range(4)]
        for m_ in range(4):
            dve_steps += [("out", m_)]
        dve_steps += [("c out", m) for m in range(4)]
        step_sem = {"pe": sem("tensor_steps"), "act": sem("scalar_steps"), "dve": sem("vector_steps")}
        step_at = {e: {k: n + 1 for n, k in enumerate(x)} for e, x in (("pe", pe_steps), ("act", act_steps), ("dve", dve_steps))}

        def stepper(eng, name):
            order = {"pe": pe_steps, "act": act_steps, "dve": dve_steps}[name]
            at = [0]

            def raise_(ins, *key):
                assert order[at[0]] == key, (order[at[0]], key)
                at[0] += 1
                ins.then_inc(step_sem[name], 1)
                if name != "pe":
                    eng.wait_ge(step_sem[name], at[0])

            def after(who, *key):
                eng.wait_ge(step_sem[who], step_at[who][key])

            return raise_, after

        def pool_mix2(pool):
            w0, hl0 = starts["m2"]
            pool.wait_ge(hl_done, hl0)
            pool.wait_ge(w_used, w0)
            pool.dma_start(LU2, T["lora_up"]).then_inc(m2_loads, 16)
            pool.dma_start(GU2, T["g_up"]).then_inc(m2_loads, 16)
            pool.dma_start(LEVELS[:, 0:6 * P], T["levels"]).then_inc(m2_loads, 16)
            pool.memset(GLU[:, :, 0:TAPS - 1], 0.0)
            pool.memset(RP2[:, :, 0:1], 0.0)
            pool.memset(SEG2, 1.0).then_inc(m2_zero, 1)
            pool.wait_ge(m2_zero, 1)
            pool.memset(SEG2.rearrange("p (c s) -> p c s", s=CH)[:, :, 0:1], 0.0).then_inc(m2_zero, 1)

        def pe_mix2(pe, t, sub, h):
            w, proj0 = t("w"), t("proj")
            raise_, after = stepper(pe, "pe")
            mm = nc.tensor.matmul
            t.add("hl", KD)
            for u in range(U2):
                h["unit_arrives"](w + u)
                if 4 <= u < 8:
                    pe.wait_ge(glu_done, u - 3)
                elif u >= 8:
                    pe.wait_ge(proj_evac, proj0 + 2 * (u - 8) + 2)
                h["project"](w + u, (2 * u % 8, (2 * u + 1) % 8), first=u == 0).then_inc(w_used, 1)
            t.add("proj", CHUNKS2)
            t.add("w", U2)
            pe.wait_ge(proj_evac, t("proj"))
            pe.wait_ge(m2_loads, 48)
            after("act", "low rank")
            for m in range(4):
                raise_(mm(PS[m][:], LU2[0:64, m * P:(m + 1) * P], LO2[0:64, :], start=True, stop=True), "decay", m)
            for m in range(4):
                raise_(mm(PS[4 + m][:], LU2[64:P, m * P:(m + 1) * P], LO2[64:P, :], start=True, stop=True), "rate", m)
            after("act", "kk sq")
            for m in range(4):
                raise_(mm(PS[m][:], const("blocks"), T2[:, m, :], start=True, stop=True), "kk", m)
            after("dve", "rk")
            for m in range(4):
                raise_(mm(PS[4 + m][:], const("blocks"), T2[:, m, :], start=True, stop=True), "bonus", m)
            after("dve", "scaled")
            for m in range(4):
                pair_products(pe, m, raise_, after)
            for c in range(NC2 - 1):
                after("dve", "h", c)
                for par in range(2):
                    ro = slice(64 * par, 64 * par + 64)
                    for m in range(4):
                        mg = (B2 if c % 2 == 0 else KK2)[ro, m, :]
                        last = mm(PS[2 * (c % 2) + par][ro, m * CH:(m + 1) * CH], mg[:, (c // 2) * CH:(c // 2 + 1) * CH],
                                  HS2[ro, 4 * c + m, :], start=True, stop=True)
                raise_(last, "h", c)
            after("dve", "h", NC2 - 1)
            for m in range(4):
                if m >= 2:
                    after("dve", "y", m - 2)
                for par in range(2):
                    ro = slice(64 * par, 64 * par + 64)
                    for c in range(NC2):
                        last = mm(PS[4 + 2 * (m % 2) + par][ro, c * CH:(c + 1) * CH], HS2[ro, 4 * c + m, :],
                                  R2[ro, m, c * CH:(c + 1) * CH], start=True, stop=True)
                raise_(last, "y", m)
            for m in range(4):
                after("dve", "y", m)
                raise_(mm(PS[m][:], const("blocks"), V2[:, m, :], start=True, stop=True), "mean", m)
            after("dve", "y", 3)
            for m in range(4):
                last = mm(PS[6][:], ONES[:], C2[:, m, :], start=m == 0, stop=m == 3)
            raise_(last, "c mean")
            after("dve", "c centred")
            for m in range(4):
                raise_(mm(PS[m][:], GU2[:, m * P:(m + 1) * P], XG2, start=True, stop=True), "g", m)
            for m in range(4):
                h["norm"](1, src=SQ[:, m:m + 1, :], weights=const("blocks"))
            h["norm"](4, src=SQ[:, 4:8, :])

        def pair_products(pe, m, raise_, after):
            mm = nc.tensor.matmul
            after("dve", "hat", m)
            if m:
                after("act", "mg", m - 1, 1)
                after("dve", "r", m - 1)
            for x, src in enumerate((BH2, KH2, KK2[:, m, :], V2[:, m, :])):
                for n in range(NT):
                    last = nc.tensor.transpose(PS[x][:, n * P:(n + 1) * P], src[:, n * P:(n + 1) * P], IDENT)
                raise_(last, "tok", m, x)
            for n in range(NT):
                for par in range(2):
                    q = 2 * n + par
                    if q >= 4:
                        after("dve", "au", m, (q - 4) // 2, q % 2)
                    ro, tk = slice(64 * par, 64 * par + 64), slice(n * P, (n + 1) * P)
                    for y, (left, right) in enumerate(((B2, KK2), (K2, KK2), (B2, R2), (K2, R2))):
                        last = mm(PS[4 + q % 4][:, y * P:(y + 1) * P], left[ro, m, tk], right[ro, m, tk], start=True, stop=True)
                    raise_(last, "au", m, n, par)

            def au(par, n, y):
                return AU2[:, 4 * par + n, y * P:(y + 1) * P]

            def tok(x, par, n, rows=slice(0, P)):
                return TOK2[rows, x, n * P + 64 * par:n * P + 64 * par + 64]

            after("act", "tok", m, 3)
            after("dve", "au", m, NT - 1, 1)
            for par in range(2):
                for n in range(NT):
                    last = mm(PS[0][:, (4 * par + n) * CH:(4 * par + n + 1) * CH], au(par, n, 1), tok(3, par, n), start=True, stop=True)
            raise_(last, "av", m)
            for l in range(6):
                for par in range(2):
                    after("dve", "ml", m, l, par)
                    for n in range(NT):
                        last = mm(PS[1 + par][:, n * P:(n + 1) * P], ML2[:, par, n * P:(n + 1) * P],
                                  TI2[:, 2 * par, n * P:(n + 1) * P], start=True, stop=True)
                    raise_(last, "x", m, l, par)
                for par in range(2):
                    after("act", "x", m, l, par)
                    for n in range(NT):
                        tk = slice(n * P, (n + 1) * P)
                        if l < 5:
                            mm(PS[3 + 2 * par][:, tk], TI2[:, 2 * par + 1, tk], XS2[:, par, tk], start=True, stop=True)
                        last = mm(PS[4 + 2 * par][:, tk], XS2[:, par, tk], TI2[:, 2 * par + 1, tk], start=True, stop=True)
                    raise_(last, "t", m, l, par)
            after("act", "av", m)
            for par in range(2):
                after("dve", "t", m, 5, par)
                b = 7 if par else 0
                for n in range(NT):
                    tt = TI2[:, 2 * par + 1, n * P:(n + 1) * P]
                    mm(PS[b][:, n * P:n * P + CH], tt, tok(2, par, n), start=True, stop=True)
                    last = mm(PS[b][:, n * P + CH:(n + 1) * P], tt, AV2[:, (4 * par + n) * CH:(4 * par + n + 1) * CH],
                              start=True, stop=True)
                raise_(last, "tz", m, par)

            def tz(par, n, half, rows=slice(0, P)):
                return TZ2[rows, par, n * P + half * CH:n * P + (half + 1) * CH]

            after("act", "tz", m, 1)
            for par in range(2):
                for n in range(NT):
                    last = mm(PS[1][64 * par:64 * par + 64, n * P:(n + 1) * P], tz(par, n, 0), au(par, n, 2), start=True, stop=True)
            raise_(last, "r", m)
            for par in range(2):
                for n in range(NT):
                    o = PS[2][64 * par:64 * par + 64, n * P:(n + 1) * P]
                    mm(o, tok(3, par, n), au(par, n, 3), start=True, stop=False)
                    last = mm(o, tz(par, n, 1), au(par, n, 2), start=False, stop=True)
            raise_(last, "yl", m)
            for half in range(2):
                rows = slice(64 * half, 64 * half + 64)
                for par in range(2):
                    for n in range(NT):
                        o = PS[3 + half][64 * par:64 * par + 64, :]
                        mm(o[:, n * CH:(n + 1) * CH], tz(par, n, 0, rows), tok(0, par, n, rows), start=True, stop=True)
                        g = o[:, (4 + n) * CH:(5 + n) * CH]
                        mm(g, tok(0, par, n, rows), tz(par, n, 1, rows), start=True, stop=False)
                        last = mm(g, tok(1, par, n, rows), tok(3, par, n, rows), start=False, stop=True)
                raise_(last, "mg", m, half)

        def act_mix2(act, t, sub, h):
            w, split = t("w"), h["split"]
            raise_, after = stepper(act, "act")
            ac = nc.scalar.activation
            act.wait_ge(m2_zero, 1)
            for u in range(U2):
                act.wait_ge(w_used, w + u + 1)
                split(w + u + 2)
                if u < 4:
                    if u >= 2:
                        act.wait_ge(glu_done, u - 1)
                    ac(SG[:, u % 2, :], PS[(2 * u + 1) % 8][:], ACT.Sigmoid).then_inc(gate_done, 1)
                else:
                    for c in range(2):
                        q = 2 * (u - 4) + c
                        if q >= 4:
                            act.wait_ge(shifted, q - 3)
                        ac(RP2[:, q % 4, 1:], PS[(2 * u + c) % 8][:], ACT.Copy).then_inc(proj_evac, 1)
            t.add("w", U2)
            act.wait_ge(shifted, CHUNKS2)
            ac(LO2[0:64, :], LO2[0:64, :], ACT.Tanh)
            raise_(ac(XG2, XG2, ACT.Sigmoid), "low rank")
            for m in range(4):
                after("pe", "decay", m)
                last = ac(LW2[:, m, :], PS[m][:], ACT.Sigmoid, bias=col("w0", m))
            raise_(last, "sig d")
            for m in range(4):
                after("pe", "rate", m)
                last = ac(B2[:, m, :], PS[4 + m][:], ACT.Sigmoid, bias=col("a0", m))
            raise_(last, "sig a")
            after("dve", "kk raw")
            raise_(ac(T2, KK2, ACT.Square), "kk sq")
            after("dve", "kk v")
            h["chain"](ac(R0W, V2W, ACT.Ln))
            raise_(ac(R0W, R0W, ACT.Exp, scale=-0.5), "kk r0")
            after("dve", "sums")
            raise_(ac(LW2, LW2, ACT.Exp), "before")
            after("pe", "bonus", 3)
            raise_(ac(T2, CC2, ACT.Exp, scale=-1.0), "inverse")
            raise_(ac(CC2, CC2, ACT.Exp), "decays")
            for m in range(4):
                for x in range(4):
                    after("pe", "tok", m, x)
                    raise_(ac(TOK2[:, x, :], PS[x][:], ACT.Copy), "tok", m, x)
                after("pe", "av", m)
                raise_(ac(AV2, PS[0][:], ACT.Copy), "av", m)
                for l in range(6):
                    for par in range(2):
                        after("pe", "x", m, l, par)
                        raise_(ac(XS2[:, par, :], PS[1 + par][:], ACT.Copy), "x", m, l, par)
                for par in range(2):
                    after("pe", "tz", m, par)
                    raise_(ac(TZ2[:, par, :], PS[7 if par else 0][:], ACT.Copy), "tz", m, par)
                after("pe", "yl", m)
                raise_(ac(V2[:, m, :], PS[2][:], ACT.Copy), "yl", m)
                for half, dest in enumerate((B2, KK2)):
                    after("pe", "mg", m, half)
                    raise_(ac(dest[:, m, :], PS[3 + half][:], ACT.Copy), "mg", m, half)
            for m in range(4):
                after("dve", "centred", m)
                ac(SQ[:, m, :], V2[:, m, :], ACT.Square).then_inc(sq_done, 1)
            after("dve", "c centred")
            for m in range(4):
                ac(SQ[:, 4 + m, :], C2[:, m, :], ACT.Square).then_inc(sq_done, 1)
            for m in range(5):
                h["rsqrt"]()
            for m in range(4):
                after("dve", "c out", m)
                ac(Y[:, 4 + m, :], C2[:, m, :], ACT.Silu, bias=col("conv_ln_b", m)).then_inc(silu2, 1)
            for m in range(4):
                act.wait_ge(silu2, m + 1)
            h["high"](Y, given=KD)

        def dve_mix2(dve, t, sub, h):
            w, split, chain = t("w"), h["split"], h["chain"]
            raise_, after = stepper(dve, "dve")
            v = nc.vector
            dve.wait_ge(m2_zero, 2)
            dve.wait_ge(m2_loads, 48)
            taps = [(m, n) for m in range(4) for n in range(TAPS)]

            def tap(m, n):
                src, weight = GLU[:, m, n:n + S], col("conv_dw", 4 * n + m)
                if n == 0:
                    chain(v.tensor_scalar(C2[:, m, :], src, weight, col("conv_b", m), ALU.mult, ALU.add))
                else:
                    chain(v.scalar_tensor_tensor(C2[:, m, :], src, weight, C2[:, m, :], ALU.mult, ALU.add))

            def shift(q):
                dest = (R2, K2, V2)[q // 4][:, q % 4, :] if q < 12 else (LO2, XG2)[q - 12]
                dve.wait_ge(proj_evac, t("proj") + q + 1)
                now, before = RP2[:, q % 4, 1:], RP2[:, q % 4, 0:S]
                chain(v.tensor_tensor(V[:], before, now, ALU.subtract))
                v.scalar_tensor_tensor(dest, V[:], col("mu", q), now, ALU.mult, ALU.add).then_inc(shifted, 1)
                dve.wait_ge(shifted, q + 1)

            for u in range(U2):
                split(w + u + 2)
                if u < 4:
                    dve.wait_ge(gate_done, u + 1)
                    v.tensor_tensor(GLU[:, u, TAPS - 1:], PS[2 * u % 8][:], SG[:, u % 2, :], ALU.mult).then_inc(glu_done, 1)
                    dve.wait_ge(glu_done, u + 1)
                else:
                    shift(2 * (u - 4))
                    shift(2 * (u - 4) + 1)
                for _ in range(12):
                    if taps and taps[0][0] < u:
                        tap(*taps.pop(0))
            for x in taps:
                tap(*x)
            t.add("w", U2)
            t.add("proj", CHUNKS2)
            dve.wait_ge(shifted, CHUNKS2)
            for m in range(4):
                last = v.tensor_scalar(KK2[:, m, :], K2[:, m, :], col("k_k", m), None, ALU.mult)
            raise_(last, "kk raw")
            for m in range(4):
                after("pe", "kk", m)
                last = v.tensor_scalar(V2W[:, m, :], PS[m][:], 1e-12, None, ALU.max)
            raise_(last, "kk v")
            for m in range(4):
                last = v.tensor_scalar(T2[:, m, :], B2[:, m, :], 1.0, col("k_a", m), ALU.subtract, ALU.mult)
            chain(last)
            chain(v.scalar_tensor_tensor(K2, T2, 1.0, K2, ALU.add, ALU.mult))
            chain(v.tensor_tensor(T2, R2, K2, ALU.mult))
            for m in range(4):
                last = v.tensor_scalar(T2[:, m, :], T2[:, m, :], col("r_k", m), None, ALU.mult)
            raise_(last, "rk")
            after("act", "kk r0")
            chain(v.tensor_tensor(RW, R0W, R0W, ALU.mult))
            chain(v.scalar_tensor_tensor(RW, RW, -0.5, V2W, ALU.mult, ALU.mult))
            chain(v.scalar_tensor_tensor(RW, RW, 1.5, R0W, ALU.add, ALU.mult))
            chain(v.tensor_tensor(KK2, KK2, RW, ALU.mult))
            chain(v.tensor_tensor(B2, KK2, B2, ALU.mult))
            for m in range(4):
                after("pe", "bonus", m)
                v.tensor_tensor(BV2[:, m, :], PS[4 + m][:], V2[:, m, :], ALU.mult)
            raise_(v.tensor_scalar(LW2, LW2, -DECAY, None, ALU.mult), "lw")
            for m in range(4):
                last = v.tensor_tensor_scan(CC2[:, m, :], SEG2, LW2[:, m, :], 0.0, ALU.mult, ALU.add)
            chain(last)
            raise_(v.tensor_tensor(LW2, CC2, LW2, ALU.subtract), "sums")
            after("act", "before")
            v.scalar_tensor_tensor(KK2, KK2, -1.0, LW2, ALU.mult, ALU.mult)
            after("act", "inverse")
            v.tensor_tensor(B2, B2, T2, ALU.mult)
            v.tensor_tensor(K2, K2, T2, ALU.mult)
            after("act", "decays")
            chain(v.tensor_copy(PC2[:], CC2.rearrange("p m (c s) -> p m c s", s=CH)[:, :, :, CH - 1]))
            raise_(v.tensor_tensor(R2, R2, CC2, ALU.mult), "scaled")
            for m in range(4):
                pc = PC2[:, m, :].unsqueeze(2).to_broadcast([P, NC2, CH])

                def by_chunk(x):
                    return x.rearrange("p (c s) -> p c s", s=CH)

                v.tensor_tensor(by_chunk(BH2), by_chunk(B2[:, m, :]), pc, ALU.mult)
                raise_(v.tensor_tensor(by_chunk(KH2), by_chunk(K2[:, m, :]), pc, ALU.mult), "hat", m)
                masks = const("later", 2 * P).rearrange("p (a t) -> p a t", a=2).unsqueeze(2).to_broadcast([P, 2, 2, P])
                for n in range(NT):
                    for par in range(2):
                        after("pe", "au", m, n, par)
                        q = 2 * n + par
                        ps = PS[4 + q % 4][:].rearrange("p (a b t) -> p a b t", a=2, b=2)
                        au = AU2[:, 4 * par + n, :].rearrange("p (a b t) -> p a b t", a=2, b=2)
                        raise_(v.tensor_tensor(au, ps, masks, ALU.mult), "au", m, n, par)

                def tiles(x):
                    return x.rearrange("p (n t) -> p n t", n=NT)

                def level(l, par):
                    zb = AU2[:, 4 * par:4 * par + 4, 0:P]
                    mask = LEVELS[:, l * P:(l + 1) * P].unsqueeze(1).to_broadcast([P, NT, P])
                    raise_(v.tensor_tensor(tiles(ML2[:, par, :]), zb, mask, ALU.mult), "ml", m, l, par)

                ident = IDENT.unsqueeze(1).to_broadcast([P, NT, P])
                for par in range(2):
                    for x in range(2):
                        chain(v.tensor_copy(tiles(TI2[:, 2 * par + x, :]), ident))
                    level(0, par)
                for l in range(6):
                    for par in range(2):
                        after("pe", "t", m, l, par)
                        if l < 5:
                            chain(v.tensor_tensor(TI2[:, 2 * par, :], TI2[:, 2 * par, :], PS[3 + 2 * par][:], ALU.add))
                        raise_(v.tensor_tensor(TI2[:, 2 * par + 1, :], TI2[:, 2 * par + 1, :], PS[4 + 2 * par][:], ALU.add),
                               "t", m, l, par)
                        if l < 5:
                            level(l + 1, par)
                after("pe", "r", m)
                raise_(v.tensor_tensor(R2[:, m, :], R2[:, m, :], PS[1][:], ALU.add), "r", m)
            after("act", "mg", 3, 1)
            raise_(v.memset(HS2[:, 0:4, :], 0.0), "h", 0)
            for c in range(NC2 - 1):
                g = (B2 if c % 2 == 0 else KK2)[:, :, (4 + c // 2) * CH:(5 + c // 2) * CH]
                pc = PC2[:, :, c].unsqueeze(2).to_broadcast([P, 4, CH])
                new = HS2[:, 4 * c + 4:4 * c + 8, :]
                chain(v.tensor_tensor(new, HS2[:, 4 * c:4 * c + 4, :], pc, ALU.mult))
                chain(v.tensor_tensor(new, new, g, ALU.add))
                after("pe", "h", c)
                for par in range(2):
                    ro = slice(64 * par, 64 * par + 64)
                    last = v.tensor_tensor(new[ro], new[ro], PS[2 * (c % 2) + par][ro, 0:4 * CH].rearrange(
                        "p (m v) -> p m v", m=4), ALU.add)
                raise_(last, "h", c + 1)
            for m in range(4):
                after("pe", "y", m)
                for par in range(2):
                    ro = slice(64 * par, 64 * par + 64)
                    last = v.tensor_tensor(V2[ro, m, :], V2[ro, m, :], PS[4 + 2 * (m % 2) + par][ro, :], ALU.add)
                raise_(last, "y", m)
            for m in range(4):
                after("pe", "mean", m)
                raise_(v.scalar_tensor_tensor(V2[:, m, :], PS[m][:], -1.0 / CH, V2[:, m, :], ALU.mult, ALU.add), "centred", m)
            after("pe", "c mean")
            chain(v.tensor_scalar(MU2, PS[6][:], 1.0 / (4 * P), None, ALU.mult))
            raise_(v.tensor_tensor(C2, C2, MU2.unsqueeze(1).to_broadcast([P, 4, S]), ALU.subtract), "c centred")
            lo = h["low"](Y)
            for m in range(4):
                h["rsqrt"](1, scale=1.0 / CH, eps=64e-5)
                y = V2[:, m, :]
                chain(v.scalar_tensor_tensor(y, y, col("gn_w", m), R[:], ALU.mult, ALU.mult))
                chain(v.scalar_tensor_tensor(y, y, col("gn_b", m), BV2[:, m, :], ALU.add, ALU.add))
                after("pe", "g", m)
                raise_(v.tensor_tensor(Y[:, m, :], y, PS[m][:], ALU.mult), "out", m)
            h["rsqrt"](4, eps=1e-5)
            for m in range(4):
                raise_(v.scalar_tensor_tensor(C2[:, m, :], C2[:, m, :], col("conv_ln_w", m), R[:], ALU.mult, ALU.mult), "c out", m)
            for m in range(4):
                dve.wait_ge(silu2, m + 1)
            for m in range(KD):
                lo(m)

        def pool_mixers(pool):
            for n, sub in enumerate(s for s in plan["subs"] if s["kind"] != "ffn"):
                if sub["kind"] == "mix1":
                    pool_mix1(pool)
                if sub["kind"] == "mix2":
                    pool_mix2(pool)
                if sub["kind"] == "mix3":
                    pool_mix3(pool, sub["name"])

        pe_mixers = {"mix1": pe_mix1, "mix2": pe_mix2, "mix3": pe_mix3}
        act_mixers = {"mix1": act_mix1, "mix2": act_mix2, "mix3": act_mix3}
        dve_mixers = {"mix1": dve_mix1, "mix2": dve_mix2, "mix3": dve_mix3}
        starts, n_sub_w, n_sub_hl = {}, 0, 0
        for sub_ in plan["subs"]:
            starts[sub_["name"]] = (n_sub_w, n_sub_hl + KD)
            n_sub_w += sum(c for _, c in sub_["units"])
            n_sub_hl += KD * (2 if sub_["kind"] != "ffn" else 1)
        M1_START, M1_HL = starts.get("m1", (0, 0))

        block = ctx.enter_context(nc.Block())

        @block.sync
        def _(sp):
            sp.dma_start(PV[:], T["pv"]).then_inc(params, 16)
            sp.dma_start(CN[:], T["cn"]).then_inc(params, 16)
            sp.dma_start(X[:], T["x"].rearrange("(m p) s -> p m s", p=P)).then_inc(params, 16)
            sp.dma_start(ONES[:], T["ones"]).then_inc(params, 16)

            def load(w, i=0):
                if w >= 2:
                    sp.wait_ge(w_lo, w - 1 + i)
                src = T["w"][bass.ds(w + i, 1), :, :].rearrange("o p n -> (o p) n")
                sp.dma_start(RAW[:, w % 2, :], src).then_inc(raw_loaded[w % 2], 16)

            load(0)
            load(1)
            with sp.Fori(0, (n_w - 2) // 2) as i:
                load(2, 2 * i)
                load(3, 2 * i)
            if n_w % 2:
                load(n_w - 1)
            final = T["final_reads"]
            for m in range(KD):
                sp.wait_ge(t_ready if plan["final"] else x_done, final + (m + 1 if plan["final"] else KD))
                sp.dma_start(T["out"][m * P:(m + 1) * P, :], (Y if plan["final"] else X)[:, m, :]).then_inc(stored, 16)
            sp.wait_ge(stored, 16 * KD)

        @block.gpsimd
        def _(pool):
            if plan["ada"]:
                def load_ada(a, i=0):
                    if a >= 2:
                        pool.wait_ge(ada_used, a - 1 + i)
                    src = T["ada"][bass.ds(a + i, 1), :, :].rearrange("o p n -> (o p) n")
                    pool.dma_start(E[:, 4 * (a % 2):4 * (a % 2) + 4, :].rearrange("p a b -> p (a b)"), src)\
                        .then_inc(ada_loaded[a % 2], 16)

                load_ada(0)
                load_ada(1)
                with pool.Fori(0, ADA // 2 - 1) as i:
                    load_ada(2, 2 * i)
                    load_ada(3, 2 * i)
            pool_mixers(pool)

        @block.tensor
        def _(pe):
            t = Tally()

            def mm3(out, wh, wl, xh, xl, start, stop):
                nc.tensor.matmul(out, wh, xh, start=start, stop=False)
                nc.tensor.matmul(out, wh, xl, start=False, stop=False)
                return nc.tensor.matmul(out, wl, xh, start=False, stop=stop)

            def blocks(w):
                return (WH[:, w % 2, :].rearrange("p (b c) -> p b c", c=P),
                        WL[:, w % 2, :].rearrange("p (b c) -> p b c", c=P))

            def unit_arrives(w, i=0):
                pe.wait_ge(w_hi, w + 1 + i)
                pe.wait_ge(w_lo, w + 1 + i)

            def project(w, banks, first=False):
                wh, wl = blocks(w)
                for c, bank in enumerate(banks):
                    for k in range(KD):
                        if first and c == 0:
                            pe.wait_ge(hl_done, t("hl") - KD + k + 1)
                        last = mm3(PS[bank][:], wh[:, KD * c + k, :], wl[:, KD * c + k, :],
                                   HH[:, k, :], HL[:, k, :], k == 0, k == KD - 1)
                return last

            def norm(n=KD, src=None, order=None, weights=None):
                e = t.add("norms")
                src = SQ if src is None else src
                for j in range(n):
                    pe.wait_ge(sq_done, t.add("sq"))
                    if j == 0 and e >= 2:
                        pe.wait_ge(r_done, e - 1)
                    m = order[j] if order else j
                    last = nc.tensor.matmul(PS[4 + e % 2][:], ONES[:] if weights is None else weights,
                                            src[:, m, :], start=j == 0, stop=j == n - 1)
                last.then_inc(stat_done, 1)

            def norm_out():
                e = t("norms") + 1
                t.add("y_evac", KD)
                pe.wait_ge(y_evac, t("y_evac") - KD + 1 + e % 2)
                norm(order=ORDER)

            def ada(a, i=0):
                pe.wait_ge(ada_loaded[a % 2], 16 * (a // 2 + 1) + 8 * i)
                raw = E[:, 4 * (a % 2):4 * (a % 2) + 4, :].rearrange("p a (b c) -> p (a b) c", c=P)
                for c in range(2):
                    for k in range(KD):
                        last = nc.tensor.matmul(PS[6][:, bass.ds(2 * a + c + 2 * i, 1)], raw[:, KD * c + k, :],
                                                PV[:, cols["silu_c"] + k:cols["silu_c"] + k + 1],
                                                start=k == 0, stop=k == KD - 1)
                last.then_inc(ada_used, 1)

            def ffn(sub, s):
                w, base = t("w"), t("act_ready")
                with_ada = plan["ada"] and s == 0

                def gate_up(u, i=0):
                    unit_arrives(w + u, i)
                    if u >= 2:
                        pe.wait_ge(act_ready, base + u - 1 + i)
                    project(w + u, (2 * (u % 2), 2 * (u % 2) + 1), first=u == 0).then_inc(w_used, 1)
                    if with_ada:
                        ada(ADA_FIRST + u, i)

                t.add("hl", KD)
                gate_up(0)
                gate_up(1)
                with pe.Fori(0, KF - 4, 2) as i:
                    gate_up(2, i)
                    gate_up(3, i)
                gate_up(KF - 2)
                gate_up(KF - 1)
                w = t.add("w", KF)
                t.add("act_ready", KF)
                if with_ada:
                    pe.wait_ge(cv_read, 2)

                def down(u, i=0):
                    unit_arrives(w + u, i)
                    pe.wait_ge(ah_done, t("ah") + u + 1 + i)
                    pe.wait_ge(al_done, t("ah") + u + 1 + i)
                    wh, wl = blocks(w + u)
                    for m in ORDER:
                        if u == 0 and m == 0:
                            pe.wait_ge(act_ready, t("act_ready"))
                        for k in range(2):
                            last = mm3(PS[m][:], wh[:, KD * k + m, :], wl[:, KD * k + m, :],
                                       AH[:, u % 2, k, :], AL[:, u % 2, k, :],
                                       u == 0 and k == 0, u == DOWN - 1 and k == 1)
                        if u == DOWN - 1 and m != ORDER[-1]:
                            last.then_inc(out_done, 1)
                    last.then_inc(w_used, 1)

                down(0)
                down(1)
                with pe.Fori(0, DOWN - 3, 2) as i:
                    down(2, i)
                    down(3, i)
                down(DOWN - 1)
                t.add("w", DOWN)
                t.add("ah", DOWN)

            def out_projection():
                w = t("w")
                t.add("hl", KD)
                for u in range(4):
                    unit_arrives(w + u)
                    wh, wl = blocks(w + u)
                    for c in range(2):
                        m = ORDER[2 * u + c]
                        for k in range(KD):
                            if u == 0 and c == 0:
                                pe.wait_ge(hl_done, t("hl") - KD + k + 1)
                            last = mm3(PS[m][:], wh[:, KD * c + k, :], wl[:, KD * c + k, :],
                                       HH[:, k, :], HL[:, k, :], k == 0, k == KD - 1)
                        last.then_inc(w_used if c else out_done, 1)
                t.add("w", 4)

            pe.wait_ge(params, N_PARAMS)
            pe.wait_ge(consts_ready, 3)
            if plan["ada"]:
                pe.wait_ge(sc_ready, 1)
                with pe.Fori(0, ADA_FIRST, 2) as i:
                    ada(0, i)
                    ada(1, i)
            norm()
            for s, sub in enumerate(plan["subs"]):
                if plan["ada"] and s == 0:
                    pe.wait_ge(cv_read, 1)
                if sub["kind"] == "ffn":
                    ffn(sub, s)
                else:
                    pe_mixers[sub["kind"]](pe, t, sub, dict(mm3=mm3, blocks=blocks, unit_arrives=unit_arrives,
                                                           project=project, norm=norm))
                    out_projection()
                if sub["post"]:
                    norm_out()
                if plan["ada"] and s == 0:
                    pe.wait_ge(y_evac, KD)
                    pe.wait_ge(sq_done, t("sq"))
                    with pe.Fori(0, ADA - KF - ADA_FIRST, 2) as i:
                        ada(KF + ADA_FIRST, i)
                        ada(KF + ADA_FIRST + 1, i)
                if plan["final"] or s + 1 < len(plan["subs"]):
                    if not sub["post"]:
                        pe.wait_ge(sq_done, t("sq") + 1 + (t("norms") + 1) % 2)
                    norm(order=None if sub["post"] else ORDER)

        @block.scalar
        def _(act):
            t = Tally()
            chain = Chain(act, sem("act_chain"))

            def split(w, i=0):
                if w >= n_w:
                    return
                act.wait_ge(raw_loaded[w % 2], 16 * (w // 2 + 1) + 8 * i)
                if w >= 2:
                    act.wait_ge(w_used, w - 1 + i)
                nc.scalar.activation(WH[:, w % 2, :], RAW[:, w % 2, :], ACT.Copy).then_inc(w_hi, 1)

            def rsqrt():
                e = t.add("norms")
                act.wait_ge(v_ready, e)
                chain(nc.scalar.activation(R0[:], V[:], ACT.Ln))
                nc.scalar.activation(R0[:], R0[:], ACT.Exp, scale=-0.5).then_inc(r0_done, 1)

            def norm_in(order):
                if t("norms"):
                    act.wait_ge(stat_done, t("norms"))
                for j, m in enumerate(order):
                    if t("x"):
                        act.wait_ge(x_done, t("x") - KD + j + 1)
                    nc.scalar.activation(SQ[:, m, :], X[:, m, :], ACT.Square).then_inc(sq_done, 1)
                rsqrt()

            def high(src, shift=None, given=0):
                t.add("t", KD - given)
                for m in range(KD):
                    if m >= given:
                        act.wait_ge(t_ready, t("t") - KD + m + 1)
                    if shift:
                        ins = nc.scalar.activation(HH[:, m, :], src[:, m, :], ACT.Identity, bias=col(shift, m))
                    else:
                        ins = nc.scalar.activation(HH[:, m, :], src[:, m, :], ACT.Copy)
                    ins.then_inc(hh_done, 1)

            def ffn(sub, s):
                w, base = t("w"), t("act_ready")

                def silu(u, i=0):
                    act.wait_ge(w_used, w + u + 1 + i)
                    if u >= 2:
                        act.wait_ge(act_ready, base + u - 1 + i)
                    nc.scalar.activation(SG[:, u % 2, :], PS[2 * (u % 2)][:], ACT.Silu).then_inc(silu_done, 1)

                def high_act(n, i=0):
                    nc.scalar.activation(AH[:, n % 2, :, :], A[:, bass.ds(2 * n + 2 * i, 2), :], ACT.Copy)\
                        .then_inc(ah_done, 1)

                for u in (0, 1):
                    silu(u)
                    split(w + u + 2)
                with act.Fori(0, KF - 4, 2) as i:
                    for u in (2, 3):
                        silu(u, i)
                        split(w + u + 2, i)
                act.wait_ge(act_ready, base + 4)
                high_act(0)
                high_act(1)
                for u in (KF - 2, KF - 1):
                    silu(u)
                    split(w + u + 2)
                w = t.add("w", KF)
                t.add("act_ready", KF)
                act.wait_ge(act_ready, t("act_ready"))

                def after_down(u, i=0):
                    act.wait_ge(w_used, w + u + 1 + i)
                    high_act(u + 2, i)
                    split(w + u + 2, i)

                with act.Fori(0, DOWN - 3, 2) as i:
                    after_down(0, i)
                    after_down(1, i)
                after_down(DOWN - 3)
                act.wait_ge(w_used, w + DOWN - 1)
                split(w + DOWN)
                t.add("w", DOWN)

            act.wait_ge(params, N_PARAMS)
            if plan["ada"]:
                sc = PV[:, cols["silu_c"]:cols["silu_c"] + KD]
                nc.scalar.activation(sc, PV[:, cols["c"]:cols["c"] + KD], ACT.Silu).then_inc(sc_ready, 1)
            split(0)
            split(1)
            norm_in(range(KD))
            for s, sub in enumerate(plan["subs"]):
                high(Y, sub["shift"])
                if s:
                    split(t("w") + 1)
                if sub["kind"] == "ffn":
                    ffn(sub, s)
                else:
                    act_mixers[sub["kind"]](act, t, sub, dict(split=split, rsqrt=rsqrt, chain=chain, high=high))
                    w = t("w")
                    for u in range(3):
                        act.wait_ge(w_used, w + u + 1)
                        split(w + u + 2)
                    t.add("w", 4)
                if sub["post"]:
                    act.wait_ge(stat_done, t("norms"))
                    for m in ORDER:
                        act.wait_ge(y_evac, t.add("y_evac"))
                        nc.scalar.activation(SQ[:, m, :], Y[:, m, :], ACT.Square).then_inc(sq_done, 1)
                    rsqrt()
                out_passed(t, sub)
                t.add("x", KD)
                if plan["final"] or s + 1 < len(plan["subs"]):
                    norm_in(range(KD) if sub["post"] else ORDER)

        @block.vector
        def _(dve):
            t = Tally()
            chain = Chain(dve, sem("dve_chain"))

            def split(w, i=0):
                if w >= n_w:
                    return
                dve.wait_ge(w_hi, w + 1 + i)
                nc.vector.tensor_tensor(WL[:, w % 2, :], RAW[:, w % 2, :], WH[:, w % 2, :].bitcast(F32),
                                        ALU.subtract).then_inc(w_lo, 1)

            def rsqrt(n=KD, scale=None, eps=EPS):
                e = t.add("norms")
                dve.wait_ge(stat_done, e)
                nc.vector.tensor_scalar(V[:], PS[4 + e % 2][:], 1.0 / (n * P) if scale is None else scale, eps,
                                        ALU.mult, ALU.add).then_inc(v_ready, 1)
                dve.wait_ge(r0_done, e)
                chain(nc.vector.tensor_tensor(R[:], R0[:], R0[:], ALU.mult))
                chain(nc.vector.scalar_tensor_tensor(R[:], R[:], -0.5, V[:], ALU.mult, ALU.mult))
                nc.vector.scalar_tensor_tensor(R[:], R[:], 1.5, R0[:], ALU.add, ALU.mult).then_inc(r_done, 1)
                dve.wait_ge(r_done, e)

            def low(src, shift=None):
                def one(m):
                    dve.wait_ge(hh_done, t("hh") - KD + m + 1)
                    nc.vector.scalar_tensor_tensor(HL[:, m, :], src[:, m, :], col(shift, m) if shift else 0.0,
                                                   HH[:, m, :].bitcast(F32), ALU.add, ALU.subtract)\
                        .then_inc(hl_done, 1)
                t.add("hh", KD)
                return one

            def norm_in(gain, shift):
                rsqrt()
                lo = low(Y, shift) if gain != plan["final"] else None
                for m in range(KD):
                    nc.vector.scalar_tensor_tensor(Y[:, m, :], X[:, m, :], col(gain, m), R[:], ALU.mult, ALU.mult)\
                        .then_inc(t_ready, 1)
                    if lo and m >= 1:
                        lo(m - 1)
                if lo:
                    lo(KD - 1)

            def ffn(sub, s):
                w, base = t("w"), t("silu")

                def gated(u, i=0):
                    dve.wait_ge(silu_done, base + u + 1 + i)
                    nc.vector.tensor_tensor(A[:, bass.ds(u + i, 1), :].rearrange("p o s -> p (o s)"),
                                            SG[:, u % 2, :], PS[2 * (u % 2) + 1][:], ALU.mult)\
                        .then_inc(act_ready, 1)

                def low_act(n, i=0):
                    dve.wait_ge(ah_done, t("ah") + n + 1 + i)
                    nc.vector.tensor_tensor(AL[:, n % 2, :, :], A[:, bass.ds(2 * n + 2 * i, 2), :],
                                            AH[:, n % 2, :, :].bitcast(F32), ALU.subtract).then_inc(al_done, 1)

                for u in (0, 1):
                    gated(u)
                    split(w + u + 2)
                with dve.Fori(0, KF - 4, 2) as i:
                    for u in (2, 3):
                        gated(u, i)
                        split(w + u + 2, i)
                low_act(0)
                low_act(1)
                for u in (KF - 2, KF - 1):
                    gated(u)
                    split(w + u + 2)
                w = t.add("w", KF)
                t.add("silu", KF)
                if plan["ada"] and s == 0:
                    dve.wait_ge(ada_used, ADA_FIRST + KF)
                    modulation(2 * ADA_FIRST, 2 * (ADA_FIRST + KF))

                def after_down(u, i=0):
                    low_act(u + 2, i)
                    split(w + u + 2, i)

                with dve.Fori(0, DOWN - 3, 2) as i:
                    after_down(0, i)
                    after_down(1, i)
                after_down(DOWN - 3)
                split(w + DOWN)
                t.add("w", DOWN)
                t.add("ah", DOWN)

            def modulation(a, b):
                bank = PS[6][:, a:b]
                nc.vector.tensor_tensor(CV[:, a:b], bank, PV[:, cols["b_ada"] + a:cols["b_ada"] + b], ALU.add)\
                    .then_inc(cv_read, 1)
                dve.wait_ge(cv_read, t.add("cv"))
                for v in range(a // KD, -(-b // KD)):
                    c0, c1 = max(a, v * KD), min(b, (v + 1) * KD)
                    sub, what, m = v // 3, v % 3, c0 - v * KD
                    if what == 0:
                        continue
                    name, factor = ("npre", 1.0) if what == 1 else ("npost", 0.5 if sub != 1 else 1.0)
                    g = PV[:, cols[f"{name}{sub}"] + m:cols[f"{name}{sub}"] + m + c1 - c0]
                    cv = CV[:, c0:c1]
                    chain(nc.vector.scalar_tensor_tensor(cv, cv, 1.0, g, ALU.add, ALU.mult))
                    if factor != 1.0:
                        chain(nc.vector.tensor_scalar(cv, cv, factor, None, ALU.mult))

            dve.wait_ge(params, N_PARAMS)
            half = PV[:, cols["ffn1_post_half"]:cols["ffn1_post_half"] + 2 * KD]
            chain(nc.vector.tensor_scalar(half, half, 0.5, None, ALU.mult))
            for to, name in ((IDB, "ident"), (MKC, "causal"), (MKB, "chunked")):
                nc.vector.tensor_copy(to[:], const(name)).then_inc(consts_ready, 1)
            split(0)
            split(1)
            if plan["ada"]:
                dve.wait_ge(ada_used, ADA_FIRST)
                modulation(0, 2 * ADA_FIRST)
            norm_in(plan["subs"][0]["pre"], plan["subs"][0]["shift"])
            for s, sub in enumerate(plan["subs"]):
                if s:
                    split(t("w") + 1)
                if sub["kind"] == "ffn":
                    ffn(sub, s)
                else:
                    dve_mixers[sub["kind"]](dve, t, sub, dict(split=split, rsqrt=rsqrt, chain=chain, low=low))
                    w = t("w")
                    for u in range(3):
                        split(w + u + 2)
                    t.add("w", 4)
                t.add("x", KD)
                if sub["post"]:
                    for j, m in enumerate(ORDER):
                        out_wait(dve, t, sub, j)
                        nc.vector.tensor_copy(Y[:, m, :], PS[m][:]).then_inc(y_evac, 1)
                    t.add("y_evac", KD)
                    rsqrt()
                    dve.wait_ge(y_evac, t("y_evac"))

                    def term(m):
                        return chain.mark(nc.vector.scalar_tensor_tensor(
                            SG[:, m % 2, :], Y[:, m, :], col(sub["post"], m), R[:], ALU.mult, ALU.mult))

                    ready = term(0)
                    for m in range(KD):
                        following = term(m + 1) if m + 1 < KD else None
                        chain.until(ready)
                        nc.vector.tensor_tensor(X[:, m, :], X[:, m, :], SG[:, m % 2, :], ALU.add).then_inc(x_done, 1)
                        if m + 1 < KD:
                            dve.wait_ge(x_done, t("x") - KD + m + 1)
                        ready = following
                else:
                    for j, m in enumerate(ORDER):
                        out_wait(dve, t, sub, j)
                        nc.vector.tensor_tensor(X[:, m, :], X[:, m, :], PS[m][:], ALU.add).then_inc(x_done, 1)
                out_passed(t, sub)
                dve.wait_ge(x_done, t("x"))
                if plan["ada"] and s == 0:
                    dve.wait_ge(ada_used, ADA)
                    modulation(2 * (ADA_FIRST + KF), VECTORS * KD)
                if s + 1 < len(plan["subs"]):
                    norm_in(plan["subs"][s + 1]["pre"], plan["subs"][s + 1]["shift"])
                elif plan["final"]:
                    norm_in(plan["final"], None)


def more_vectors(a, v):
    v["fox_b"] = np.concatenate([a["fox_b_f"][0], np.zeros(P - 8, np.float32)])
    v["gnorm_a"] = a["gnorm_a_g"][0]
    v["gnorm_b"] = a["gnorm_b_g"][0]
    for to, n in (("mu", "shift_mu"), ("w0", "w0"), ("a0", "a0"), ("k_k", "k_k"), ("k_a", "k_a"), ("gn_w", "gn_w"),
                  ("gn_b", "gn_b"), ("conv_b", "conv_b"), ("conv_ln_w", "conv_ln_w"), ("conv_ln_b", "conv_ln_b")):
        v[to] = a[n + "_2"][0]
    v["r_k"] = a["r_k_2"][0].reshape(-1)
    v["conv_dw"] = a["conv_dw_2"][0].reshape(-1)
    none = np.zeros(P - 64, np.float32)
    for i in range(2):
        v[f"g_sub{i}"] = a["g_subln_3"][i]
        v[f"lam{i}"] = np.concatenate([x for n in ("q1", "q2", "k1", "k2") for x in (a[f"lam_{n}_3"][i], none)])


def constants():
    q, k = np.arange(P)[:, None], np.arange(P)[None]

    def rotation(n):
        r = np.zeros((P, P), np.float32)
        for d in range(P):
            if d % n < n // 2:
                r[d + n // 2, d] = -1.0
            else:
                r[d - n // 2, d] = 1.0
        return r

    return {"ident": np.eye(P, dtype=np.float32), 
            "blocks": (q // 64 == k // 64).astype(np.float32),
            "later": np.concatenate([(q // 64 == k // 64) & (k > q), (q // 64 == k // 64) & (k >= q)], axis=1).astype(np.float32),
            "rot64": rotation(64), "rot32": rotation(32),
            "causal": np.where(k <= q, 0.0, -BIG).astype(np.float32),
            "chunked": np.where(k // 64 <= q // 64, 0.0, -BIG).astype(np.float32)}


def more_arrays(a, plan):
    def rows(v):
        return np.ascontiguousarray(np.broadcast_to(v, (P, v.size)))
    out = {}
    kinds = [s["kind"] for s in plan["subs"]]
    if "mix1" in kinds:
        out["ln_g"], out["ln_b"] = rows(a["sgu_ln_g"][0]), rows(a["sgu_ln_b"][0])
        out["sgu_w"] = np.ascontiguousarray(a["sgu_w"][0].transpose(2, 0, 1))
        b = a["sgu_b"][0].reshape(4, 2, P)
        out["sgu_b"] = np.ascontiguousarray(np.repeat(b, 64, axis=1).transpose(1, 0, 2).reshape(P, S))
    if "mix2" in kinds:
        out["lora_up"] = np.concatenate([a["w_up_2"][0], a["a_up_2"][0]])
        q, k = np.arange(P)[:, None], np.arange(P)[None]
        out["levels"] = np.concatenate([(q >> l + 1 == k >> l + 1) & (k >> l & 1 == 1) & (q >> l & 1 == 0)
                                        for l in range(6)], axis=1).astype(np.float32)
        out["g_up"] = np.ascontiguousarray(a["g_up_2"][0])
    if "mix3" in kinds:
        for n in (64, 32):
            inv = np.float32(10000.0) ** (-np.arange(0, n, 2, dtype=np.float32) / np.float32(n))
            angle = (np.arange(S, dtype=np.float32)[:, None] * inv[None]).T[np.arange(P) % (n // 2)]
            out[f"cos{n}"], out[f"sin{n}"] = np.cos(angle), np.sin(angle)
    return out


def columns(v):
    v = np.asarray(v).reshape(-1, P)
    return v.T


def channel_units(w):
    k, n = w.shape
    return w.reshape(k // P, P, n // (2 * P), 2, P).transpose(2, 1, 3, 0, 4).reshape(-1, P, UNIT)


def token_units(w):
    return w.reshape(2, 4, P, 4 * P).transpose(0, 2, 1, 3).reshape(2, P, UNIT)


def down_units(w):
    return w.reshape(-1, 2, P, D).transpose(0, 2, 1, 3).reshape(-1, P, UNIT)


def gate_up_units(gate, up):
    both = np.stack([gate.reshape(KD, P, KF, P), up.reshape(KD, P, KF, P)])
    return both.transpose(3, 2, 0, 1, 4).reshape(KF, P, UNIT)


def out_units(w):
    return channel_units(w.reshape(D, KD, P)[:, ORDER, :].reshape(D, D))


def padded(w, n):
    return np.concatenate([w, np.zeros((w.shape[0], n - w.shape[1]), w.dtype)], axis=1)


def matrices(a):
    f, w = {}, a["w_in"][0]
    for i in range(2):
        f[f"f1{i}_gu"] = lambda i=i: gate_up_units(a["ffn_w_gate"][0, i], a["ffn_w_up"][0, i])
        f[f"f1{i}_down"] = lambda i=i: down_units(a["ffn_w_down"][0, i])
        g = a[f"ffn{i + 1}_w_gu_2"][0]
        f[f"f2{i}_gu"] = lambda g=g: gate_up_units(g[:, :FF], g[:, FF:])
        f[f"f2{i}_down"] = lambda i=i: down_units(a[f"ffn{i + 1}_w_down_2"][0])
        f[f"f3{i}_gu"] = lambda i=i: gate_up_units(a["w_gate_3"][i], a["w_up_3"][i])
        f[f"f3{i}_down"] = lambda i=i: down_units(a["w_down_3"][i])
        w3 = a["w_in_3"][i]
        at = 0
        for name, n in (("qa", 512), ("ka", 512), ("va", 512), ("iq", 256), ("ik", 32), ("iw", 8),
                        ("qb", 512), ("kb", 512), ("vb", 512)):
            part = w3[:, at:at + n]
            at += n
            if name == "ik":
                ik = part
            elif name == "iw":
                f[f"ik3_{i}"] = lambda ik=ik, iw=part: channel_units(
                    np.concatenate([ik, ik, ik, ik, padded(iw, P)], axis=1))
            else:
                lay = token_units if name in ("va", "vb") else channel_units
                f[f"{name}3_{i}"] = lambda part=part, lay=lay: lay(part)
        f[f"m3{i}_out"] = lambda i=i: out_units(a["w_out_3"][i])
    f["f1"] = lambda: channel_units(padded(w[:, 2560:2568], 2 * P))
    f["u1"] = lambda: channel_units(w[:, 0:512])
    f["v1"] = lambda: token_units(w[:, 512:1024])
    f["q1"] = lambda: channel_units(w[:, 1024:1536])
    f["k1"] = lambda: channel_units(w[:, 1536:2048])
    f["va1"] = lambda: token_units(w[:, 2048:2560])
    f["m1_out"] = lambda: out_units(a["w_out"][0])
    w2 = a["w_in_2"][0]
    f["r2"] = lambda: channel_units(w2[:, 0:512])
    f["k2"] = lambda: channel_units(w2[:, 512:1024])
    f["v2"] = lambda: channel_units(w2[:, 1024:1536])
    f["lora2"] = lambda: channel_units(w2[:, 1536:1792])
    pc = w2[:, 1792:2816].reshape(D, 2, 4, P).transpose(0, 2, 1, 3).reshape(D, D)
    f["pc2"] = lambda: channel_units(pc)
    f["m2_out"] = lambda: out_units(a["w_out_2"][0])
    return f


def vectors(a):
    v = {"eps": np.full(P, EPS, np.float32), "c": a["c"][0], "silu_c": np.zeros(D, np.float32), "b_ada": a["b_ada"][0]}
    for i in range(SUBS):
        v[f"npre{i}"] = a["norm_pre_g"][0, i]
        v[f"npost{i}"] = a["norm_post_g"][0, i]
    v["ffn1_pre"] = a["ffn1_norm_pre_2"][0]
    v["ffn2_pre"] = a["ffn2_norm_pre_2"][0]
    v["ffn1_post_half"] = a["ffn1_norm_post_2"][0]
    v["ffn2_post_half"] = a["ffn2_norm_post_2"][0]
    v["mix_pre"] = a["mix_norm_pre_2"][0]
    v["mix_post"] = a["mix_norm_post_2"][0]
    for i in range(2):
        v[f"g_mix{i}"] = a["g_mix_3"][i]
        v[f"g_ffn{i}"] = a["g_ffn_3"][i]
    v["g_final"] = a["g_final_3"]
    more_vectors(a, v)
    return v


def laid_out(a, plan):
    v = vectors(a)
    cols, at = {}, 0
    for name, x in v.items():
        cols[name] = at
        at += -(-x.size // P)
    pv = np.ascontiguousarray(np.concatenate([columns(x) for x in v.values()], axis=1))
    c = constants()
    cncols, at = {}, 0
    for name, x in c.items():
        cncols[name] = at
        at += x.shape[1]
    cn = np.ascontiguousarray(np.concatenate(list(c.values()), axis=1))
    f = matrices(a)
    w = np.concatenate([f[name]() for sub in plan["subs"] for name, _ in sub["units"]])
    arrays = {"w": w, "pv": pv, "cn": cn, "ones": np.ones((P, P), np.float32),
              "x": np.ascontiguousarray(a["x"][0].T)}
    if plan["ada"]:
        arrays["ada"] = np.ascontiguousarray(channel_units(a["w_ada"][0]))
    arrays.update(more_arrays(a, plan))
    return arrays, cols, cncols


def launch_parts(a, plan, nc):
    arrays, cols, cncols = laid_out(a, plan)
    T = {n: nc.dram_tensor("in_" + n, x.shape, mybir.dt.from_np(x.dtype), kind="ExternalInput").ap()
         for n, x in arrays.items()}
    T["out"] = nc.dram_tensor("out_x", (D, S), F32, kind="ExternalOutput").ap()
    kinds = [s["kind"] for s in plan["subs"]]
    n = len(kinds)
    T["cols"], T["cncols"] = cols, cncols
    T["final_reads"] = KD * (n + kinds.count("mix1")) + 4 * kinds.count("mix3") if plan["final"] else KD * (n - 1)
    build_program(nc, T, plan)
    return {"in_" + n: x for n, x in arrays.items()}


def kernel(**inputs):
    from concourse import bacc
    from concourse.bass_utils import run_bass_kernel_spmd

    a = {n: np.asarray(x) for n, x in inputs.items()}
    nc = bacc.Bacc("TRN2", target_bir_lowering=False, num_devices=1)
    arrays = launch_parts(a, whole_plan(), nc)
    r = run_bass_kernel_spmd(nc, [arrays], core_ids=[0])
    return np.ascontiguousarray(r.results[0]["out_x"].T)[None]
```

```python
from contextlib import ExitStack

import numpy as np

import concourse.bass as bass
from concourse import mybir

F32 = mybir.dt.float32
F32R = mybir.dt.float32r
BF16 = mybir.dt.bfloat16
ACT = mybir.ActivationFunctionType
ALU = mybir.AluOpType
AX = mybir.AxisListType.X

P = 128
S = 512
D = 1024
KD = D // P
FF = 2816
KF = FF // P
NT = S // P
UNIT = 16 * P
DOWN = KF // 2
SUBS = 3
VECTORS = SUBS * 3
ADA = VECTORS * KD // 2
ADA_SLOTS = 4
ADA_FIRST = KD
_LATE = ADA_FIRST + KF - 4
ADA_LATE = [(_LATE, _LATE + 1), (_LATE + 2,), (_LATE + 3, _LATE + 4), (_LATE + 5,)]
ORDER = [4, 5, 6, 7, 0, 1, 2, 3]
EPS = 1e-6
BIG = 1.0e30


class Tally:

    def __init__(self):
        self.n = {}

    def __call__(self, name):
        return self.n.get(name, 0)

    def add(self, name, k=1):
        self.n[name] = self.n.get(name, 0) + k
        return self.n[name]


class Chain:

    def __init__(self, eng, sem):
        self.eng, self.sem, self.n = eng, sem, 0

    def __call__(self, ins):
        self.n += 1
        ins.then_inc(self.sem, 1)
        self.eng.wait_ge(self.sem, self.n)

    def mark(self, ins):
        self.n += 1
        ins.then_inc(self.sem, 1)
        return self.n

    def until(self, n):
        self.eng.wait_ge(self.sem, n)


def stream(plan):
    return [(name, i) for sub in plan["subs"] for name, count in sub["units"] for i in range(count)]


def ffn_sub(name, pre, shift, post):
    return dict(kind="ffn", name=name, pre=pre, shift=shift, post=post,
                units=[(name + "_gu", KF), (name + "_down", DOWN)])


def mix_sub(kind, name, pre, shift, post, layer=0):
    units = {
        "mix1": [("f1", 1), ("u1", 2), ("v1", 2), ("q1", 2), ("k1", 2), ("va1", 2)],
        "mix2": [("pc2", 4), ("r2", 2), ("k2", 2), ("v2", 2), ("lora2", 1)],
        "mix3": [(f"ik3_{layer}", 1), (f"iq3_{layer}", 1), (f"qa3_{layer}", 2), (f"ka3_{layer}", 2), (f"va3_{layer}", 2),
                 (f"qb3_{layer}", 2), (f"kb3_{layer}", 2), (f"vb3_{layer}", 2)],
    }[kind]
    return dict(kind=kind, name=name, pre=pre, shift=shift, post=post, layer=layer,
                units=units + [(name + "_out", 4)])


def whole_plan():
    return dict(ada=True, final="g_final", subs=[
        ffn_sub("f10", "pre0", "shift0", "post0"),
        mix_sub("mix1", "m1", "pre1", "shift1", "post1"),
        ffn_sub("f11", "pre2", "shift2", "post2"),
        ffn_sub("f20", "ffn1_pre", None, "ffn1_post_half"),
        mix_sub("mix2", "m2", "mix_pre", None, "mix_post"),
        ffn_sub("f21", "ffn2_pre", None, "ffn2_post_half"),
        mix_sub("mix3", "m30", "g_mix0", None, None, 0),
        ffn_sub("f30", "g_ffn0", None, None),
        mix_sub("mix3", "m31", "g_mix1", None, None, 1),
        ffn_sub("f31", "g_ffn1", None, None),
    ])


def build_program(nc, T, plan):
    n_w = len(stream(plan))
    ctx = ExitStack()

    def sb(name, shape, dt=F32):
        return ctx.enter_context(nc.sbuf_tensor(name, shape, dt))

    with ctx:
        X = sb("X", [P, KD, S])
        RAW = sb("RAW", [P, 2, UNIT])
        WH = sb("WH", [P, 2, UNIT], F32R)
        WL = sb("WL", [P, 2, UNIT], F32R)
        A = sb("A", [P, KF, S])
        R = sb("R", [P, S])
        R0 = sb("R0", [P, S])
        V = sb("V", [P, S])
        SG = sb("SG", [P, 2, S])
        ONES = sb("ONES", [P, P])
        PV = sb("PV", [P, T["pv"].shape[1]])
        CV = sb("CV", [P, VECTORS * KD])
        CN = sb("CN", [P, T["cn"].shape[1]])
        E = sb("E", [P, 16, S])
        with nc.sbuf_tensor("HH", [P, KD, S], F32R) as HH, nc.sbuf_tensor("HL", [P, KD, S], F32R) as HL, \
             nc.sbuf_tensor("AH", [P, 2, 2, S], F32R) as AH, nc.sbuf_tensor("AL", [P, 2, 2, S], F32R) as AL:
            pass
        G = sb("G", [P, 24, S])
        Y, SQ = A[:, 0:KD, :], A[:, KD:2 * KD, :]
        PS = [ctx.enter_context(nc.psum_tensor(f"PS{b}", [P, S], F32)) for b in range(8)]
        cols, cn = T["cols"], T["cncols"]
        sems = {}

        def sem(name):
            if name not in sems:
                sems[name] = ctx.enter_context(nc.semaphore(name))
            return sems[name]

        def col(name, m, n=1):
            for what, at in (("shift", 0), ("pre", KD), ("post", 2 * KD)):
                if name.startswith(what) and name[len(what):].isdigit():
                    c = int(name[len(what):]) * 3 * KD + at + m
                    return CV[:, c:c + n]
            return PV[:, cols[name] + m:cols[name] + m + n]

        def const(name, n=P, rows=slice(0, P)):
            return CN[rows, cn[name]:cn[name] + n]

        raw_loaded = [sem("raw_loaded0"), sem("raw_loaded1")]
        ada_loaded = [sem(f"ada_loaded{n}") for n in range(ADA_SLOTS)]
        first_loaded = [sem(f"first_loaded{n}") for n in range(ADA_FIRST)]
        x_loaded, cn_loaded = sem("x_loaded"), sem("cn_loaded")
        ada_scaled, ada_summed = sem("ada_scaled"), sem("ada_summed")
        w_hi, w_lo, w_used = sem("w_hi"), sem("w_lo"), sem("w_used")
        ada_used, cv_read, sc_ready = sem("ada_used"), sem("cv_read"), sem("sc_ready")
        params = sem("params")
        sq_added = sem("sq_added")
        sq_done, stat_done, v_ready = sem("sq_done"), sem("stat_done"), sem("v_ready")
        r0_done, r_done = sem("r0_done"), sem("r_done")
        y_evac, x_done, t_ready = sem("y_evac"), sem("x_done"), sem("t_ready")
        hh_done, hl_done, out_done = sem("hh_done"), sem("hl_done"), sem("out_done")
        silu_done, act_ready = sem("silu_done"), sem("act_ready")
        ah_done, al_done = sem("ah_done"), sem("al_done")
        stored = sem("stored")
        N_PARAMS = 2 * 16

        def ada_raw(a):
            n = a % ADA_SLOTS
            return (G if ADA_FIRST > a >= ADA_SLOTS else E)[:, 4 * n:4 * n + 4, :].rearrange("p a b -> p (a b)")

        def ada_unit(a):
            return ada_raw(a).rearrange("p (o k c) -> p o k c", o=2, c=P)

        def ada_arrives(eng, a, i=0):
            if a < ADA_FIRST:
                eng.wait_ge(first_loaded[a], 16)
            else:
                n = a - ADA_FIRST
                eng.wait_ge(ada_loaded[n % ADA_SLOTS], 16 * (n // ADA_SLOTS + 1) + 16 // ADA_SLOTS * i)

        def out_wait(eng, t, sub, j):
            if sub["kind"] == "ffn":
                if j < KD - 1:
                    eng.wait_ge(out_done, t("out") + j + 1)
                else:
                    eng.wait_ge(w_used, t("w"))
            elif j % 2 == 0:
                eng.wait_ge(out_done, t("out") + j // 2 + 1)
            else:
                eng.wait_ge(w_used, t("w") - 3 + j // 2)

        def out_passed(t, sub):
            t.add("out", KD - 1 if sub["kind"] == "ffn" else KD // 2)

        PARTS = [(3,), (2, 0), (1,)]
        S_AT = {3: (0, 0), 2: (1, 0), 0: (1, 384), 1: (2, 0)}
        GROUPS = [((0, 0),), ((1, 0), (3, 384)), ((2, 0),)]
        GROUP_AT, GROUP_W = [0, 512, 1024], [512, 512, 256]
        P_AT = [0, 128, 384, 768]
        K_AT = [0, 512, 1024, 896]
        BANK_T, BANK_O = 6, 7
        PB = G[:, 0:5, :].rearrange("p a s -> p (a s)").rearrange("p (b n) -> p b n", b=2)
        PT = G[:, 5:10, :].rearrange("p a s -> p (a s)").rearrange("p (b n) -> p b n", b=2)
        ATT = sb("ATT", [P, 2, 4, 4])
        IDB, MKC, MKB = (sb(n, [P, P], BF16) for n in ("IDB", "MKC", "MKB"))
        ONE_ROW = sb("ONE_ROW", [8, 8], F32R)
        scores_done, neg_ready, exp_done = sem("scores_done"), sem("neg_ready"), sem("exp_done")
        p_ready, pt_done, pt_evac, pv_done, pv_evac = (sem(n) for n in ("p_ready", "pt_done", "pt_evac", "pv_done", "pv_evac"))
        proj_evac, consts_ready = sem("proj_evac"), sem("consts_ready")
        IDENT = const("ident")

        def score_bank(g, i):
            b, c = S_AT[i]
            return PS[3 * (g % 2) + b][:, c:c + (i + 1) * P]

        def probs(j, i):
            return PB[:, j % 2, P_AT[i]:P_AT[i] + (i + 1) * P]

        def turns_before(jobs, j):
            return sum(job["turn"] for job in jobs[:max(j, 0)])

        def pe_attention(pe, t, jobs, before_attend=lambda j: None, before_turn=lambda j: None):
            g0, e0 = t("jobs"), t("turned")

            def scores(j, part):
                if j >= len(jobs):
                    return
                job, g = jobs[j], g0 + j
                if part == 0 and g >= 2:
                    pe.wait_ge(exp_done, g - 1)
                for i in PARTS[part]:
                    out, w = score_bank(g, i), (i + 1) * P
                    nc.tensor.matmul(out, job["q"](i), job["k"](w), start=True, stop=False)
                    added = job["added"](i)
                    for n, (left, right, c0) in enumerate(added):
                        last = nc.tensor.matmul(out[:, c0:c0 + right.shape[-1]], left, right, start=False,
                                                stop=n == len(added) - 1)
                last.then_inc(scores_done, 1)

            def turn(j, group):
                e = e0 + turns_before(jobs, j) + 1
                if group == 0:
                    before_turn(j)
                    pe.wait_ge(p_ready, e)
                if 3 * e + group > 3:
                    pe.wait_ge(pt_evac, 3 * e - 3 + group)
                for k, at in GROUPS[group]:
                    for i in range(k, NT):
                        c = at + (i - k) * P
                        last = nc.tensor.transpose(PS[BANK_T][:, c:c + P], probs(j, i)[:, k * P:(k + 1) * P], IDENT)
                last.then_inc(pt_done, 1)

            def attend(j):
                job, e = jobs[j], e0 + turns_before(jobs, j) + 1
                if job["first"] and t("pv_out"):
                    pe.wait_ge(pv_evac, t("pv_out"))
                r0, r1 = job["rows"]
                order = [k for group in GROUPS for k, _ in group]
                for n, k in enumerate(order):
                    if n != 2:
                        pe.wait_ge(pt_evac, 3 * (e - 1) + (1, 2, 0, 3)[n])
                    last = nc.tensor.matmul(PS[BANK_O][r0:r1, k * P:S], job["v"](k),
                                            PT[:, e % 2, K_AT[k]:K_AT[k] + S - k * P], start=n == 0, stop=n == NT - 1)
                last.then_inc(pv_done, 1)
                if job["dest"] is not None:
                    t.add("pv_out")

            for j in range(2):
                for part in range(3):
                    scores(j, part)
            for j, job in enumerate(jobs):
                for part in range(3):
                    if job["turn"]:
                        turn(j, part)
                    scores(j + 2, part)
                if job["turn"]:
                    before_attend(j)
                    attend(j)
            t.add("jobs", len(jobs))
            t.add("turned", turns_before(jobs, len(jobs)))

        def act_attention(act, t, jobs, between=lambda j: None):
            g0, e0 = t("jobs"), t("turned")

            def exps(j, part):
                if j >= len(jobs):
                    return
                job, g = jobs[j], g0 + j
                if part == 0:
                    act.wait_ge(neg_ready, g + 1)
                    before = jobs[j - 2] if j >= 2 else None
                    if before is None and e0:
                        act.wait_ge(pt_done, 3 * e0)
                    elif before is not None and before["turn"]:
                        act.wait_ge(pt_done, 3 * (e0 + turns_before(jobs, j - 1)))
                    elif before is not None:
                        act.wait_ge(p_ready, e0 + turns_before(jobs, j))
                for i in PARTS[part]:
                    last = nc.scalar.activation(probs(j, i), score_bank(g, i), ACT.Exp,
                                                bias=ATT[:, g % 2, 1, i:i + 1], scale=job["scale"],
                                                accum_out=ATT[:, g % 2, 2, i:i + 1])
                if part == 2:
                    last.then_inc(exp_done, 1)

            def copy_turned(j, group):
                e = e0 + turns_before(jobs, j) + 1
                act.wait_ge(pt_done, 3 * (e - 1) + group + 1)
                if group == 0 and e > 2:
                    act.wait_ge(pv_done, e - 2)
                a, w = GROUP_AT[group], GROUP_W[group]
                nc.scalar.activation(PT[:, e % 2, a:a + w], PS[BANK_T][:, 0:w], ACT.Copy).then_inc(pt_evac, 1)

            for part in range(3):
                exps(0, part)
            for j, job in enumerate(jobs):
                for part in range(3):
                    exps(j + 1, part)
                    if job["turn"]:
                        copy_turned(j, part)
                between(j)
            t.add("jobs", len(jobs))
            t.add("turned", turns_before(jobs, len(jobs)))

        def dve_attention(dve, t, jobs, chain, between=lambda j: None):
            g0, e0 = t("jobs"), t("turned")

            def maxima(j, part):
                if j >= len(jobs):
                    return
                job, g = jobs[j], g0 + j
                mx, nm = ATT[:, g % 2, 0, :], ATT[:, g % 2, 1, :]
                dve.wait_ge(scores_done, 3 * g + part + 1)
                for i in PARTS[part]:
                    last = nc.vector.reduce_max(mx[:, i:i + 1], score_bank(g, i), AX)
                if part == 2:
                    chain(last)
                    nc.vector.tensor_scalar(nm, mx, -job["scale"], None, ALU.mult).then_inc(neg_ready, 1)

            def scale(j):
                if j >= len(jobs):
                    return
                job, g = jobs[j], g0 + j
                rs, rc = ATT[:, g % 2, 2, :], ATT[:, g % 2, 3, :]
                dve.wait_ge(exp_done, g + 1)
                chain(nc.vector.reciprocal(rc, rs))
                if job["minus"] is not None:
                    chain(nc.vector.tensor_scalar(rc, rc, job["minus"], None, ALU.mult))
                for i in range(NT):
                    p, first = probs(j, i), probs(j + 1, i)
                    if job["minus"] is not None:
                        last = nc.vector.scalar_tensor_tensor(p, p, rc[:, i:i + 1], first, ALU.mult, ALU.add)
                    else:
                        last = nc.vector.tensor_scalar(p, p, rc[:, i:i + 1], None, ALU.mult)
                if job["turn"]:
                    last.then_inc(p_ready, 1)
                else:
                    chain(last)

            def copy_out(j):
                if j >= 0 and jobs[j]["turn"] and jobs[j]["dest"] is not None:
                    dve.wait_ge(pv_done, e0 + turns_before(jobs, j + 1))
                    nc.vector.tensor_copy(jobs[j]["dest"], PS[BANK_O][:]).then_inc(pv_evac, 1)

            for j in range(2):
                for part in range(3):
                    maxima(j, part)
            scale(0)
            for j in range(len(jobs)):
                copy_out(j - 1)
                maxima(j + 2, 0)
                maxima(j + 2, 1)
                scale(j + 1)
                maxima(j + 2, 2)
                between(j)
            copy_out(len(jobs) - 1)
            t.add("jobs", len(jobs))
            t.add("turned", turns_before(jobs, len(jobs)))
            t.add("pv_out", sum(job["dest"] is not None for job in jobs))
            dve.wait_ge(pv_evac, t("pv_out"))

        def pe_bank(pe, t, j):
            if j >= 8:
                pe.wait_ge(proj_evac, t("proj") + j - 7)
            return j % 8

        def pe_token_major(pe, h, w, banks, between=lambda u: None):
            for u in range(2):
                h["unit_arrives"](w + u)
                wh, wl = (x[:, (w + u) % 2, :].rearrange("p (k c) -> p k c", k=4) for x in (WH, WL))
                for k in range(4):
                    kk = 4 * u + k
                    for i, b in enumerate(banks):
                        last = h["mm3"](PS[b][:], HH[:, kk, i * P:(i + 1) * P], HL[:, kk, i * P:(i + 1) * P],
                                        wh[:, k, :], wl[:, k, :], kk == 0, kk == KD - 1)
                last.then_inc(w_used, 1)
                between(u)

        U1, V1, Q1 = E[:, 0:4, :], E[:, 4:8, :], E[:, 8:16, :]
        K1, VA1, YB1 = A[:, 4:8, :], G[:, 16:20, :], G[:, 12:16, :]
        WT1, YA1 = A[:, 16:18, :].rearrange("p a (h i) -> p (a h) i", i=P), A[:, 18:22, :]
        LNG, LNB, SGB = G[:, 20, :], G[:, 21, :], G[:, 22, :]
        F1, F2, NC1 = (A[0:8, c, :] for c in (12, 13, 14))
        NCH, NCL = HL[0:8, 2, :], HL[0:8, 3, :]
        ST1 = G[:, 23, 0:12 * NT].rearrange("p (i x) -> p i x", i=NT)
        m1_loads, q_zero, wt_masked, ln_r0 = (sem(n) for n in ("m1_loads", "q_zero", "wt_masked", "ln_r0"))
        ln_var, v_normed, sgu_done, ya_ready, lf_done, nc_ready = (
            sem(n) for n in ("ln_var", "v_normed", "sgu_done", "ya_ready", "lf_done", "nc_ready"))

        def jobs_fox():
            def job(h):
                m, par = h // 2, h % 2
                pick = ONE_ROW[:, h:h + 1].to_broadcast([8, P])
                return dict(q=lambda i: Q1[:, h, i * P:(i + 1) * P], k=lambda w: K1[:, m, 0:w],
                            added=lambda i: [(pick, NCH[:, 0:(i + 1) * P], 0), (pick, NCL[:, 0:(i + 1) * P], 0),
                                             (IDB[:], MKC[:], i * P)], scale=1.0,
                            v=lambda k: VA1[:, k, h * 64:(h + 1) * 64], rows=(64 * par, 64 * par + 64),
                            first=par == 0, dest=YB1[:, m, :] if par else None, turn=True, minus=None)
            return [job(h) for h in range(8)]

        def pool_mix1(pool):
            if plan["ada"]:
                pool.wait_ge(ada_used, ADA)
            pool.memset(E[:, 8:16, :], 0.0).then_inc(q_zero, 1)
            pool.wait_ge(w_used, M1_START)
            pool.wait_ge(hl_done, M1_HL)
            pool.dma_start(WT1, T["sgu_w"]).then_inc(m1_loads, 16)
            for x, name in ((LNG, "ln_g"), (LNB, "ln_b"), (SGB, "sgu_b")):
                pool.dma_start(x, T[name]).then_inc(m1_loads, 16)

        def pe_mix1(pe, t, sub, h):
            w = t("w")
            t.add("hl", KD)
            h["unit_arrives"](w)
            wh, wl = h["blocks"](w)
            for k in range(KD):
                pe.wait_ge(hl_done, t("hl") - KD + k + 1)
                last = h["mm3"](PS[0][:], wh[:, k, :], wl[:, k, :], HH[:, k, :], HL[:, k, :], k == 0, k == KD - 1)
            last.then_inc(w_used, 1)
            j = 1
            at = w + 1
            for what in "uvqka":
                if what in "va":
                    banks = [pe_bank(pe, t, j + i) for i in range(4)]
                    pe_token_major(pe, h, at, banks)
                else:
                    for u in range(2):
                        h["unit_arrives"](at + u)
                        banks = [pe_bank(pe, t, j + 2 * u + c) for c in range(2)]
                        h["project"](at + u, banks)
                at += 2
                j += 4
            pe.wait_ge(v_normed, 1)
            pe.wait_ge(wt_masked, 1)
            pe.wait_ge(proj_evac, t("proj") + j)
            t.add("proj", j)
            for m in range(4):
                for par in range(2):
                    hd = 2 * m + par
                    for n in range(NT):
                        last = nc.tensor.matmul(PS[m][64 * par:64 * par + 64, n * P:(n + 1) * P],
                                                V1[:, n, hd * 64:(hd + 1) * 64], WT1[:, hd, :], start=True, stop=True)
                last.then_inc(sgu_done, 1)
            h["norm"](4)
            pe.wait_ge(nc_ready, 1)
            pe.wait_ge(ya_ready, 4)
            pe.wait_ge(r_done, t("norms"))
            pe_attention(pe, t, jobs_fox())
            h["norm"](4)
            t.add("w", 11)

        def act_mix1(act, t, sub, h):
            w, split, chain = t("w"), h["split"], h["chain"]

            def done(n):
                act.wait_ge(w_used, w + n + 1)

            done(0)
            chain(nc.scalar.activation(F1, PS[0][0:8, :], ACT.Identity, bias=PV[0:8, cols["fox_b"]:cols["fox_b"] + 1]))
            nc.scalar.activation(F2, F1, ACT.Abs).then_inc(proj_evac, 1)
            split(w + 2)
            for n in (1, 2):
                done(n)
                for c in range(2):
                    m = 2 * (n - 1) + c
                    nc.scalar.activation(U1[:, m, :], PS[(1 + m) % 8][:], ACT.Gelu_apprx_tanh).then_inc(proj_evac, 1)
                split(w + n + 2)
            done(3)
            split(w + 5)
            done(4)
            for i in range(NT):
                nc.scalar.activation(V1[:, i, :], PS[(5 + i) % 8][:], ACT.Gelu_apprx_tanh).then_inc(proj_evac, 1)
            split(w + 6)
            act.wait_ge(q_zero, 1)
            for n in (5, 6):
                done(n)
                for c in range(2):
                    m = 2 * (n - 5) + c
                    ps = PS[(9 + m) % 8]
                    nc.scalar.activation(Q1[0:64, 2 * m, :], ps[0:64, :], ACT.Copy, scale=0.125)
                    nc.scalar.activation(Q1[64:P, 2 * m + 1, :], ps[64:P, :], ACT.Copy, scale=0.125)\
                        .then_inc(proj_evac, 1)
                split(w + n + 2)
            for n in (7, 8):
                done(n)
                for c in range(2):
                    m = 2 * (n - 7) + c
                    nc.scalar.activation(K1[:, m, :], PS[(13 + m) % 8][:], ACT.Copy).then_inc(proj_evac, 1)
                split(w + n + 2)
            act.wait_ge(ln_var, 1)
            chain(nc.scalar.activation(ST1[:, :, 8], ST1[:, :, 7], ACT.Ln))
            nc.scalar.activation(ST1[:, :, 8], ST1[:, :, 8], ACT.Exp, scale=-0.5).then_inc(ln_r0, 1)
            chain(nc.scalar.activation(F2, F2, ACT.Exp, scale=-1.0))
            nc.scalar.activation(F2, F2, ACT.Ln, bias=1.0).then_inc(lf_done, 1)
            done(9)
            split(w + 11)
            done(10)
            for i in range(NT):
                nc.scalar.activation(VA1[:, i, :], PS[(17 + i) % 8][:], ACT.Copy).then_inc(proj_evac, 1)
            split(w + 12)
            t.add("w", 11)
            for m in range(4):
                act.wait_ge(ya_ready, m + 1)
                nc.scalar.activation(SQ[:, m, :], YA1[:, m, :], ACT.Square).then_inc(sq_done, 1)
            h["rsqrt"]()
            act_attention(act, t, jobs_fox())
            for m in range(4):
                act.wait_ge(pv_evac, m + 1)
                nc.scalar.activation(SQ[:, m, :], YB1[:, m, :], ACT.Square).then_inc(sq_done, 1)
            h["rsqrt"]()
            h["high"](Y)

        def dve_mix1(dve, t, sub, h):
            w, split, chain = t("w"), h["split"], h["chain"]
            dve.wait_ge(m1_loads, 4 * 16)
            nc.vector.memset(WT1[64:P, :, 0:64], 0.0).then_inc(wt_masked, 1)
            for n in range(5):
                split(w + n + 2)
            base = t("proj")
            for i in range(NT):
                dve.wait_ge(proj_evac, base + 6 + i)
                chain(nc.vector.bn_stats(ST1[:, i, 0:6], V1[:, i, :]))
                chain(nc.vector.bn_aggr(ST1[:, i, 6:8], ST1[:, i, 0:6]))
            chain(nc.vector.tensor_copy(ST1[:, :, 9], ST1[:, :, 6]))
            nc.vector.tensor_scalar(ST1[:, :, 7], ST1[:, :, 7], EPS, None, ALU.add).then_inc(ln_var, 1)
            for n in (5, 6, 7, 8):
                split(w + n + 2)
            v_, r0_, tmp = ST1[:, :, 7], ST1[:, :, 8], ST1[:, :, 10]
            dve.wait_ge(ln_r0, 1)
            chain(nc.vector.tensor_tensor(tmp, r0_, r0_, ALU.mult))
            chain(nc.vector.tensor_tensor(tmp, tmp, v_, ALU.mult))
            chain(nc.vector.tensor_scalar(tmp, tmp, -0.5, 1.5, ALU.mult, ALU.add))
            chain(nc.vector.tensor_tensor(tmp, tmp, r0_, ALU.mult))
            for i in range(NT):
                v = V1[:, i, :]
                chain(nc.vector.tensor_scalar(v, v, ST1[:, i, 9:10], ST1[:, i, 10:11], ALU.subtract, ALU.mult))
                chain(nc.vector.tensor_tensor(v, v, LNG, ALU.mult))
                last = nc.vector.tensor_tensor(v, v, LNB, ALU.add)
                if i < NT - 1:
                    chain(last)
            last.then_inc(v_normed, 1)
            dve.wait_ge(lf_done, 1)
            chain(nc.vector.scalar_tensor_tensor(F1, F1, 0.0, F2, ALU.min, ALU.subtract))
            chain(nc.vector.memset(F2, 1.0))
            chain(nc.vector.tensor_tensor_scan(NC1, F2, F1, 0.0, ALU.mult, ALU.add))
            chain(nc.vector.tensor_scalar(NC1, NC1, -1.0, None, ALU.mult))
            dve.wait_ge(w_used, w + 11)
            chain(nc.vector.tensor_copy(NCH, NC1))
            nc.vector.tensor_tensor(NCL, NC1, NCH.bitcast(F32), ALU.subtract).then_inc(nc_ready, 1)
            split(w + 11)
            split(w + 12)
            t.add("w", 11)
            t.add("proj", 21)
            for m in range(4):
                dve.wait_ge(sgu_done, m + 1)
                ya = YA1[:, m, :].rearrange("p (n i) -> p n i", n=NT)
                bias = SGB[:, m * P:(m + 1) * P].unsqueeze(1).to_broadcast([P, NT, P])
                chain(nc.vector.tensor_tensor(ya, PS[m][:].rearrange("p (n i) -> p n i", n=NT), bias, ALU.add))
                nc.vector.tensor_tensor(YA1[:, m, :], YA1[:, m, :], U1[:, m, :], ALU.mult).then_inc(ya_ready, 1)
            h["rsqrt"](4)
            dve.wait_ge(ya_ready, 4)
            for m in range(4):
                nc.vector.scalar_tensor_tensor(Y[:, m, :], YA1[:, m, :], col("gnorm_a", m), R[:], ALU.mult, ALU.mult)\
                    .then_inc(t_ready, 1)
            dve_attention(dve, t, jobs_fox(), chain)
            h["rsqrt"](4)
            lo = h["low"](Y)
            for m in range(4):
                nc.vector.scalar_tensor_tensor(Y[:, 4 + m, :], YB1[:, m, :], col("gnorm_b", m), R[:], ALU.mult, ALU.mult)\
                    .then_inc(t_ready, 1)
                lo(m)
            for m in range(4, 8):
                lo(m)

        kinds_ = [sub_["kind"] for sub_ in plan["subs"]]
        QA3, KA3, VA3 = E[:, 0:8, :], E[:, 8:12, :], E[:, 12:16, :]
        QB3, KB3, VB3 = A[:, 0:8, :], A[:, 8:12, :], A[:, 12:16, :]
        IQ3, IK3, OB3 = A[:, 16:18, :], A[:, 18, :], G[:, 12:16, :]
        SC3 = A[:, 19:22, :].rearrange("p a s -> p (a s)")
        SC_AT = {1: 0, 2: 256, 3: 640}
        ROPE = {64: (G[:, 16, :], G[:, 17, :]), 32: (G[:, 18, :], G[:, 19, :])}
        SUB_V, SUB_R0 = A[:, 12:16, :], A[:, 8:12, :]
        TURN3 = [G[:, 20, :], G[:, 21, :], R0[:]]
        SIN3 = [V[:], R[:]]
        MK3 = G[:, 22:24, :].rearrange("p a s -> p (a s)").bitcast(BF16)
        W3 = sb("W3", [P, NT, 8])
        M8 = sb("M8", [P, 8])
        GLU_LAST = sb("GLU_LAST", [P, S + 30])
        LAM = sb("LAM", [P, 8])
        m3_loads, q3_zero, rot_done, roped = (sem(n) for n in ("m3_loads", "q3_zero", "rot_done", "roped"))
        sub_y, half_roped = sem("sub_y"), sem("half_roped")
        cos_done, sin_done = sem("cos_done"), sem("sin_done")
        sub_squared, sub_summed, sub_read, sub_r0 = (sem(n) for n in ("sub_squared", "sub_summed", "sub_read", "sub_r0"))
        dots_done, dots_read, weighed, keys_taken = (sem(n) for n in ("dots_done", "dots_read", "weighed", "keys_taken"))
        lam_in, lam_sum, lam_exp = sem("lam_in"), sem("lam_sum"), sem("lam_exp")
        TOPK = 128
        MARK = -3.0e38
        LAM_INIT = [0.8 - 0.6 * float(np.exp(-0.3 * layer)) for layer in range(2)]
        N_PROJ3 = 28
        ROPED = [(0, 0, 32, [(IK3, slice(0, P))])] + [(1, c, 32, [(IQ3[:, c, :], slice(0, P))]) for c in range(2)]
        for first_unit, q_ in ((2, QA3), (8, QB3)):
            for m_ in range(4):
                ROPED.append((first_unit + m_ // 2, m_ % 2, 64,
                              [(q_[:, 2 * m_, :], slice(0, 64)), (q_[:, 2 * m_ + 1, :], slice(64, P))]))
        for first_unit, k_ in ((4, KA3), (10, KB3)):
            for m_ in range(4):
                ROPED.append((first_unit + m_ // 2, m_ % 2, 64, [(k_[:, m_, :], slice(0, P))]))
        ROPED.sort(key=lambda r: (r[0], r[1]))
        ROUNDS = [(i, n) for i in (1, 2, 3) for n in range(TOPK // 8)]
        DOTS = [(i, hd) for i in (1, 2, 3) for hd in range(8)]
        SLOTS3 = [(u, c) for u in (3, 4, 5, 6, 7) for c in ((0, 1) if u < 6 else (0,))]
        DOTS_AFTER = {x: DOTS[3 * n:3 * n + 3] for n, x in enumerate(SLOTS3)}
        TAKES = {5: 4, 6: 6, 7: 8, 8: 5, 9: 5, 10: 4, 11: 4, 12: 6, 13: 6}
        U3 = 14
        TOKENS3 = {6: (VA3, 0), 7: (VA3, 1), 12: (VB3, 0), 13: (VB3, 1)}

        def turns_of(u):
            return [(n, r) for n, r in enumerate(ROPED) if r[0] == u]

        AUX3 = [("lambda", 0)]
        for u_ in range(1, U3):
            for c_ in (0, 1):
                AUX3 += [("dots", d) for d in DOTS_AFTER.get((u_, c_), [])] \
                    + [("turn", n) for n, r in turns_of(u_ - 1) if r[1] == c_]
        BANK3 = {key: 6 + n % 2 for n, key in enumerate(AUX3)}
        PROJ3, n_ = {}, 0
        for u_ in range(U3):
            k_ = {0: 2, 6: 0, 7: 4, 12: 0, 13: 4}.get(u_, 2)
            PROJ3[u_] = list(range(n_, n_ + k_))
            n_ += k_
        assert n_ == N_PROJ3

        def jobs_dsa():
            def job(hd):
                m, par = hd // 2, hd % 2
                return dict(q=lambda i: QA3[:, hd, i * P:(i + 1) * P], k=lambda w: KA3[:, m, 0:w],
                            added=lambda i: [(IDB[:], MK3[:, SC_AT[i]:SC_AT[i] + (i + 1) * P] if i else MKB[:], 0)],
                            scale=0.125, v=lambda k: VA3[:, k, hd * 64:(hd + 1) * 64],
                            rows=(64 * par, 64 * par + 64), first=par == 0,
                            dest=Y[:, m, :] if par else None, turn=True, minus=None)
            return [job(hd) for hd in range(8)]

        def jobs_diff():
            def job(hd, c):
                return dict(q=lambda i: QB3[:, 2 * hd + c, i * P:(i + 1) * P], k=lambda w: KB3[:, hd, 0:w],
                            added=lambda i: [(IDB[:], MKB[:], i * P)], scale=0.125,
                            v=lambda k: VB3[:, k, hd * P:(hd + 1) * P], rows=(0, P), first=True,
                            dest=OB3[:, hd, :] if c else None, turn=c == 1, minus=LAM[:, 7:8] if c else None)
            return [job(hd, c) for hd in range(4) for c in range(2)]

        pool_t = Tally()

        def pool_mix3(pool, name):
            w0, hl0 = starts[name]
            pool.wait_ge(hl_done, hl0)
            pool.wait_ge(w_used, w0)
            for to, n in zip(ROPE[64] + ROPE[32], ("cos64", "sin64", "cos32", "sin32")):
                pool.dma_start(to, T[n]).then_inc(m3_loads, 16)
            pool.memset(QA3, 0.0)
            n = pool_t.add("m3")
            pool.memset(QB3, 0.0).then_inc(q3_zero, 1)
            pool.wait_ge(m3_loads, 64 * n)
            pool.wait_ge(q3_zero, n)
            for n, (_, c, size, places) in enumerate(ROPED):
                x, n_all = TURN3[n % 3], pool_t.add("turns")
                pool.wait_ge(rot_done, n_all)
                pool.tensor_tensor(x, x, ROPE[size][0], ALU.mult).then_inc(cos_done, 1)
                pool.wait_ge(cos_done, n_all)
                pool.wait_ge(sin_done, n_all)
                for to, rows in places:
                    last = pool.tensor_tensor(to[rows, :], x[rows, :], SIN3[n % 2][rows, :], ALU.add)
                    if to is places[-1][0]:
                        last.then_inc(roped, 1)
                        pool.wait_ge(roped, n_all)
                    else:
                        last.then_inc(half_roped, 1)
                        pool.wait_ge(half_roped, pool_t.add("halves"))

        def pe_mix3(pe, t, sub, h):
            w, proj0, turns0, dots0 = t("w"), t("proj"), t("turns"), t("dots")
            t.add("hl", KD)

            def bank(j):
                if j >= 6:
                    pe.wait_ge(proj_evac, proj0 + j - 5)
                return PS[j % 6]

            def aux(key):
                n = AUX3.index(key)
                if n >= 2:
                    kind, before = AUX3[n - 2]
                    if kind == "turn":
                        pe.wait_ge(sin_done, turns0 + before + 1)
                    elif kind == "dots":
                        pe.wait_ge(dots_read, dots0 + DOTS.index(before) + 1)
                    else:
                        pe.wait_ge(lam_exp, t("lam"))
                return PS[BANK3[key]]

            def turn(n, r):
                u, c, size, _ = r
                pe.wait_ge(proj_evac, proj0 + PROJ3[u][c] + 1)
                nc.tensor.matmul(aux(("turn", n))[:], const(f"rot{size}"), TURN3[n % 3], start=True, stop=True)\
                    .then_inc(rot_done, 1)

            def dot(d):
                i, hd = d
                if d == DOTS[0]:
                    pe.wait_ge(roped, turns0 + 3)
                r0 = 32 * (hd % 4)
                nc.tensor.matmul(aux(("dots", d))[:, 0:(i + 1) * P], IQ3[r0:r0 + 32, hd // 4, i * P:(i + 1) * P],
                                 IK3[r0:r0 + 32, 0:(i + 1) * P], start=True, stop=True).then_inc(dots_done, 1)

            def between(u):
                def after(c):
                    for d in DOTS_AFTER.get((u, c), []):
                        dot(d)
                    for n, r in turns_of(u - 1):
                        if r[1] == c:
                            turn(n, r)
                return after

            h["unit_arrives"](w)
            wh, wl = h["blocks"](w)
            ps = bank(0)
            for k in range(KD):
                pe.wait_ge(hl_done, t("hl") - KD + k + 1)
                h["mm3"](ps[:], wh[:, k, :], wl[:, k, :], HH[:, k, :], HL[:, k, :], k == 0, k == KD - 1)
            ps = bank(1)
            for i in range(NT):
                for k in range(KD):
                    last = h["mm3"](ps[:, 8 * i:8 * i + 8], HH[:, k, i * P:(i + 1) * P], HL[:, k, i * P:(i + 1) * P],
                                    wh[:, KD + k, 0:8], wl[:, KD + k, 0:8], k == 0, k == KD - 1)
            last.then_inc(w_used, 1)
            pe.wait_ge(lam_in, t.add("lam"))
            nc.tensor.matmul(aux(("lambda", 0))[:, 0:2], ONES[:], LAM[:, 0:2], start=True, stop=True).then_inc(lam_sum, 1)
            for u in range(1, U3):
                if u not in TOKENS3:
                    h["unit_arrives"](w + u)
                    for j in PROJ3[u]:
                        bank(j)
                    h["project"](w + u, [j % 6 for j in PROJ3[u]], between=between(u))
                elif TOKENS3[u][1] == 0:
                    for j in PROJ3[u + 1]:
                        bank(j)

                    def after(x):
                        for c in (0, 1):
                            between(u + x)(c)
                    pe_token_major(pe, h, w + u, [j % 6 for j in PROJ3[u + 1]], after)
            t.add("turns", len(ROPED))
            t.add("dots", len(DOTS))
            t.add("proj", N_PROJ3)
            pe.wait_ge(proj_evac, t("proj"))
            pe.wait_ge(roped, t("turns"))
            pe_attention(pe, t, jobs_diff())
            pe.wait_ge(keys_taken, t.add("keys_taken"))

            def sum_of_squares(j):
                if 1 <= j <= 4:
                    pe.wait_ge(pt_evac, 3 * (t("turned") + j + 1))
                    pe.wait_ge(sub_squared, t.add("sub"))
                    nc.tensor.matmul(PS[BANK_T][:], ONES[:], SQ[:, j - 1, :], start=True, stop=True).then_inc(sub_summed, 1)

            def sums_read(j):
                if 2 <= j <= 5:
                    pe.wait_ge(sub_read, t("sub"))
            pe_attention(pe, t, jobs_dsa(), sum_of_squares, sums_read)
            pe.wait_ge(pv_evac, t("pv_out"))
            t.add("w", U3)

        def act_mix3(act, t, sub, h):
            w, split, turns0, dots0 = t("w"), h["split"], t("turns"), t("dots")

            def read_dots(u, c):
                for i, hd in DOTS_AFTER.get((u, c), []):
                    n = dots0 + DOTS.index((i, hd)) + 1
                    act.wait_ge(dots_done, n)
                    if n > 2:
                        act.wait_ge(weighed, n - 2)
                    nc.scalar.activation(SG[:, n % 2, 0:(i + 1) * P], PS[BANK3["dots", (i, hd)]][:, 0:(i + 1) * P],
                                         ACT.Relu, scale=float(32 ** -0.5)).then_inc(dots_read, 1)

            for u in range(U3):
                read_dots(u, 0)
                act.wait_ge(w_used, w + u + 1)
                split(w + u + 2)
                for c, j in enumerate(PROJ3[u]):
                    ps = PS[j % 6]
                    if u in TOKENS3:
                        ins = nc.scalar.activation(TOKENS3[u][0][:, c, :], ps[:], ACT.Copy)
                    elif u == 0 and c == 1:
                        ins = nc.scalar.activation(W3[:].rearrange("p i h -> p (i h)"), ps[:, 0:8 * NT], ACT.Copy,
                                                   scale=float(8 ** -0.5))
                    else:
                        n = [(r[0], r[1]) for r in ROPED].index((u, c))
                        if turns0 + n >= 3:
                            act.wait_ge(roped, turns0 + n - 2)
                        ins = nc.scalar.activation(TURN3[n % 3], ps[:], ACT.Copy)
                    ins.then_inc(proj_evac, 1)
                if u == 0:
                    act.wait_ge(lam_sum, t.add("lam"))
                    nc.scalar.activation(LAM[:, 2:4], PS[BANK3["lambda", 0]][:, 0:2], ACT.Exp).then_inc(lam_exp, 1)
                read_dots(u, 1)
            t.add("w", U3)
            t.add("turns", len(ROPED))
            t.add("dots", len(DOTS))
            act_attention(act, t, jobs_diff())
            n0 = t("sub_squares")
            act.wait_ge(pv_evac, t.add("pv_out", 4) + 4 * bool("mix1" in kinds_))

            def sub_norm(j):
                if j < 4:
                    if j == 0:
                        act.wait_ge(pv_done, t("turned"))
                    nc.scalar.activation(SQ[:, j, :], OB3[:, j, :], ACT.Square).then_inc(sub_squared, 1)
                elif j == 5:
                    act.wait_ge(sub_read, n0 + 4)
                    h["chain"](nc.scalar.activation(SUB_R0, SUB_V, ACT.Ln))
                    nc.scalar.activation(SUB_R0, SUB_R0, ACT.Exp, scale=-0.5).then_inc(sub_r0, 1)
            act_attention(act, t, jobs_dsa(), sub_norm)
            t.add("sub_squares", 4)
            t.add("pv_out", 4)
            act.wait_ge(sub_y, t.add("sub_y"))
            h["high"](Y, given=KD, ready=lambda m: m < 4 and act.wait_ge(pv_evac, t("pv_out") - 3 + m + 4 * bool("mix1" in kinds_)))

        def dve_mix3(dve, t, sub, h):
            w, split, chain = t("w"), h["split"], h["chain"]
            turns0, dots0, layer = t("turns"), t("dots"), sub["layer"]
            dve.wait_ge(m3_loads, 64 * t.add("m3"))
            dve.wait_ge(q3_zero, t("m3"))
            lam = cols[f"lam{layer}"]
            nc.vector.tensor_tensor(LAM[:, 0:2], PV[:, lam:lam + 2], PV[:, lam + 2:lam + 4], ALU.mult).then_inc(lam_in, 1)
            g_sub = col(f"g_sub{layer}", 0)
            chain(nc.vector.tensor_scalar(g_sub, g_sub, 1.0 - LAM_INIT[layer], None, ALU.mult))
            rounds = list(ROUNDS)

            def rope(n, r):
                dve.wait_ge(rot_done, turns0 + n + 1)
                if turns0 + n >= 2:
                    dve.wait_ge(roped, turns0 + n - 1)
                nc.vector.tensor_tensor(SIN3[n % 2], PS[BANK3["turn", n]][:], ROPE[r[2]][1], ALU.mult).then_inc(sin_done, 1)

            def scores(i):
                return SC3[:, SC_AT[i]:SC_AT[i] + (i + 1) * P]

            def weigh(i, hd):
                n = dots0 + DOTS.index((i, hd)) + 1
                dve.wait_ge(dots_read, n)
                relu, weight = SG[:, n % 2, 0:(i + 1) * P], W3[:, i, hd:hd + 1]
                if hd == 0:
                    ins = nc.vector.tensor_scalar(scores(i), relu, weight, None, ALU.mult)
                else:
                    ins = nc.vector.scalar_tensor_tensor(scores(i), relu, weight, scores(i), ALU.mult, ALU.add)
                ins.then_inc(weighed, 1)
                dve.wait_ge(weighed, n)
                if hd == 7:
                    chain(nc.vector.memset(SC3[0:64, SC_AT[i] + i * P + 64:SC_AT[i] + (i + 1) * P], -BIG))

            def take(i, n):
                chain(nc.vector.max(M8[:], scores(i)))
                chain(nc.vector.match_replace(scores(i), M8[:], scores(i), MARK))
                if n == TOPK // 8 - 1:
                    ins = nc.vector.tensor_scalar(MK3[:, SC_AT[i]:SC_AT[i] + (i + 1) * P], scores(i), MARK / 2, -BIG,
                                                  ALU.is_gt, ALU.mult)
                    if i == 3:
                        ins.then_inc(keys_taken, 1)

            for u in range(U3):
                for c in (0, 1):
                    if c == 1:
                        split(w + u + 2)
                    for d in DOTS_AFTER.get((u, c), []):
                        weigh(*d)
                    for n, r in turns_of(u - 1):
                        if r[1] == c:
                            rope(n, r)
                if u == 1:
                    dve.wait_ge(lam_exp, t.add("lam"))
                    chain(nc.vector.tensor_tensor(LAM[:, 7:8], LAM[:, 3:4], LAM[:, 2:3], ALU.subtract))
                    chain(nc.vector.tensor_scalar(LAM[:, 7:8], LAM[:, 7:8], -LAM_INIT[layer], None, ALU.add))
                for _ in range(TAKES.get(u, 0)):
                    take(*rounds.pop(0))
            assert not rounds
            t.add("w", U3)
            t.add("turns", len(ROPED))
            t.add("dots", len(DOTS))
            dve_attention(dve, t, jobs_diff(), chain)
            n0 = t("sub")

            def sub_norm(j):
                if 1 <= j <= 4:
                    n = t.add("sub")
                    dve.wait_ge(sub_summed, n)
                    nc.vector.tensor_scalar(SUB_V[:, j - 1, :], PS[BANK_T][:], 1.0 / P, EPS, ALU.mult, ALU.add)\
                        .then_inc(sub_read, 1)
                elif j == 6:
                    dve.wait_ge(sub_r0, t.add("sub_r0"))
                    tmp = V[:]
                    for m in range(4):
                        r0, v_ = SUB_R0[:, m, :], SUB_V[:, m, :]
                        chain(nc.vector.tensor_tensor(tmp, r0, r0, ALU.mult))
                        chain(nc.vector.scalar_tensor_tensor(tmp, tmp, -0.5, v_, ALU.mult, ALU.mult))
                        chain(nc.vector.scalar_tensor_tensor(tmp, tmp, 1.5, r0, ALU.add, ALU.mult))
                        last = nc.vector.scalar_tensor_tensor(Y[:, 4 + m, :], OB3[:, m, :], g_sub, tmp, ALU.mult, ALU.mult)
                        if m < 3:
                            chain(last)
                    last.then_inc(sub_y, 1)
                    t.add("sub_y")
            dve_attention(dve, t, jobs_dsa(), chain, sub_norm)
            lo = h["low"](Y)
            dve.wait_ge(sub_y, t("sub_y"))
            for m in range(8):
                lo(m)

        CH = 64
        NC2 = S // CH
        U2 = 11
        DECAY = float(np.exp(-0.5))
        TAPS = 31
        R2, K2, V2 = E[:, 0:4, :], E[:, 4:8, :], E[:, 8:12, :]
        LO2, XG2, SEG2 = E[:, 12, :], E[:, 13, :], E[:, 14, :]
        C2 = A[:, 16:20, :]
        GLU = A[:, 8:12, :].rearrange("p a s -> p (a s)")[:, 0:3 * (S + TAPS - 1)].rearrange("p (m s) -> p m s", m=3)
        RP2 = G[:, 16:21, :].rearrange("p a s -> p (a s)")[:, 0:4 * (S + 1)].rearrange("p (m s) -> p m s", m=4)
        B2, LW2, KK2, CC2, BV2 = G[:, 0:4, :], G[:, 4:8, :], G[:, 8:12, :], G[:, 12:16, :], G[:, 16:20, :]
        T2, V2W, R0W, RW = A[:, 0:4, :], A[:, 4:8, :], A[:, 8:12, :], A[:, 12:16, :]
        BH2, KH2, MU2 = G[:, 20, :], G[:, 21, :], E[:, 15, :]
        LEVELS = G[:, 22:24, :].rearrange("p a s -> p (a s)")
        TOK2 = A[:, 0:4, :]
        AU2 = A[:, 4:12, :]
        TI2 = A[:, 12:16, :]
        ML2, XS2, AV2, TZ2 = G[:, 4:6, :], G[:, 6:8, :], G[:, 12, :], G[:, 13:15, :]
        HS2 = A[:, 12:16, :].rearrange("p a (c v) -> p (a c) v", v=CH)
        PC2 = sb("PC2", [P, 4, NC2])
        LU2, GU2 = A[:, 20, :], A[:, 21, :]
        m2_loads, m2_zero, glu_done, gate_done, shifted = (
            sem(n) for n in ("m2_loads", "m2_zero", "glu_done", "gate_done", "shifted"))
        V_5, R0_5, R_5 = G[:, 8:13, :], G[:, 0:5, :], E[:, 0:5, :]
        G_BANKS = [4, 5, 6, 0]
        POOL_CHUNKS = (0,)
        silu2, pool_taps, pool_terms = sem("silu2"), sem("pool_taps"), sem("pool_terms")
        CHUNKS2 = 14

        pe_steps = [("decay", m) for m in range(4)] + [("rate", m) for m in range(4)] \
            + [("kk", m) for m in range(4)] + [("bonus", m) for m in range(4)]
        act_steps = [("low rank",), ("sig d",), ("sig a",), ("kk sq",), ("kk r0",), ("before",), ("inverse",), ("decays",)]
        dve_steps = [("kk raw",), ("sums",), ("kk v",), ("rk",), ("bonus read",), ("scaled",)]
        for m_ in range(4):
            pe_steps += [("tok", m_, x) for x in range(4)] + [("au", m_, n, par) for n in range(NT) for par in range(2)]
            pe_steps += [("av", m_)]
            act_steps += [("tok", m_, x) for x in range(4)] + [("av", m_)]
            dve_steps += [("hat", m_)] + [("au", m_, n, par) for n in range(NT) for par in range(2)] + [("ml", m_, 0, par) for par in range(2)]
            for l_ in range(6):
                pe_steps += [("x", m_, l_, par) for par in range(2) if l_] + [("t", m_, l_, par) for par in range(2)]
                act_steps += [("x", m_, l_, par) for par in range(2) if l_]
                if l_ == 0:
                    for par_ in range(2):
                        dve_steps += [("t", m_, 0, par_), ("ml", m_, 1, par_)]
                else:
                    dve_steps += [("ml", m_, l_ + 1, par) for par in range(2) if l_ < 5]
                    for par_ in range(2):
                        dve_steps += [(x, m_, l_, par_) for x in ("inv", "t") if x == "t" or l_ < 5]
            pe_steps += [("tz", m_, 0), ("tz", m_, 1), ("r", m_), ("yl", m_), ("mg", m_, 0), ("mg", m_, 1)]
            act_steps += [("tz", m_, 0), ("tz", m_, 1), ("yl", m_), ("mg", m_, 0), ("mg", m_, 1)]
            dve_steps += [("r", m_)]
        pe_steps += [("h", c) for c in range(NC2 - 1)] + [("y", m) for m in range(4)]
        dve_steps += [("h", c) for c in range(NC2)]
        for m_ in range(4):
            dve_steps += [("y", m_)]
        pe_steps += [("mean", m) for m in range(4)] + [("c mean",)]
        dve_steps += [("centred", m) for m in range(4)] + [("c centred",)]
        act_steps += [("squares", m) for m in range(5)] + [("norms r0",)]
        pe_steps += [("variance", m) for m in range(5)] + [("g", m) for m in range(4)]
        dve_steps += [("variances",)] + [("c out", m) for m in range(4)]
        for m_ in range(4):
            dve_steps += [("out", m_)]
        step_sem = {"pe": sem("tensor_steps"), "act": sem("scalar_steps"), "dve": sem("vector_steps")}
        step_at = {e: {k: n + 1 for n, k in enumerate(x)} for e, x in (("pe", pe_steps), ("act", act_steps), ("dve", dve_steps))}

        def stepper(eng, name):
            order = {"pe": pe_steps, "act": act_steps, "dve": dve_steps}[name]
            at = [0]

            def raise_(ins, *key):
                assert order[at[0]] == key, (order[at[0]], key)
                at[0] += 1
                ins.then_inc(step_sem[name], 1)
                if name != "pe":
                    eng.wait_ge(step_sem[name], at[0])

            def after(who, *key):
                eng.wait_ge(step_sem[who], step_at[who][key])

            return raise_, after

        def glu(m, n):
            return GLU[:, m, n:n + S] if m < 3 else GLU_LAST[:, n:n + S]

        def tap(eng, m, n):
            src, weight = glu(m, n), col("conv_dw", 4 * n + m)
            if n == 0:
                return eng.tensor_scalar(C2[:, m, :], src, weight, col("conv_b", m), ALU.mult, ALU.add)
            return eng.scalar_tensor_tensor(C2[:, m, :], src, weight, C2[:, m, :], ALU.mult, ALU.add)

        def pool_mix2(pool):
            w0, hl0 = starts["m2"]
            pool.wait_ge(hl_done, hl0)
            pool.wait_ge(w_used, w0)
            pool.dma_start(LU2, T["lora_up"]).then_inc(m2_loads, 16)
            pool.dma_start(GU2, T["g_up"]).then_inc(m2_loads, 16)
            pool.dma_start(LEVELS[:, 0:6 * P], T["levels"]).then_inc(m2_loads, 16)
            pool.memset(GLU[:, :, 0:TAPS - 1], 0.0)
            pool.memset(GLU_LAST[:, 0:TAPS - 1], 0.0)
            pool.memset(RP2[:, :, 0:1], 0.0)
            pool.memset(SEG2, 1.0).then_inc(m2_zero, 1)
            pool.wait_ge(m2_zero, 1)
            pool.memset(SEG2.rearrange("p (c s) -> p c s", s=CH)[:, :, 0:1], 0.0).then_inc(m2_zero, 1)
            for x, m in enumerate(POOL_CHUNKS):
                pool.wait_ge(glu_done, m + 1)
                for n in range(TAPS):
                    if n == 0:
                        tap(pool, m, n).then_inc(pool_terms, 1)
                        pool.wait_ge(pool_terms, x * TAPS + 1)
                        continue
                    term = (R, R0)[n % 2][:]
                    pool.tensor_scalar(term, GLU[:, m, n:n + S], col("conv_dw", 4 * n + m), None, ALU.mult)\
                        .then_inc(pool_terms, 1)
                    pool.wait_ge(pool_terms, x * TAPS + n + 1)
                    pool.tensor_tensor(C2[:, m, :], C2[:, m, :], term, ALU.add).then_inc(pool_taps, 1)
                    pool.wait_ge(pool_taps, x * (TAPS - 1) + n)

        def pe_mix2(pe, t, sub, h):
            w, proj0 = t("w"), t("proj")
            raise_, after = stepper(pe, "pe")
            mm = nc.tensor.matmul
            t.add("hl", KD)
            for u in range(U2):
                h["unit_arrives"](w + u)
                if 4 <= u < 8:
                    pe.wait_ge(glu_done, u - 3)
                elif u >= 8:
                    pe.wait_ge(proj_evac, proj0 + 2 * (u - 8) + 2)
                h["project"](w + u, (2 * u % 8, (2 * u + 1) % 8), first=u == 0)
            t.add("proj", CHUNKS2)
            t.add("w", U2)
            pe.wait_ge(proj_evac, t("proj"))
            pe.wait_ge(m2_loads, 48)
            after("act", "low rank")
            for m in range(4):
                raise_(mm(PS[m][:], LU2[0:64, m * P:(m + 1) * P], LO2[0:64, :], start=True, stop=True), "decay", m)
            for m in range(4):
                raise_(mm(PS[4 + m][:], LU2[64:P, m * P:(m + 1) * P], LO2[64:P, :], start=True, stop=True), "rate", m)
            after("act", "kk sq")
            for m in range(4):
                raise_(mm(PS[m][:], const("blocks"), T2[:, m, :], start=True, stop=True), "kk", m)
            after("dve", "rk")
            for m in range(4):
                raise_(mm(PS[4 + m][:], const("blocks"), T2[:, m, :], start=True, stop=True), "bonus", m)
            after("dve", "scaled")
            for m in range(4):
                pair_products(pe, m, raise_, after)
            for c in range(NC2 - 1):
                after("dve", "h", c)
                for par in range(2):
                    ro = slice(64 * par, 64 * par + 64)
                    for m in range(4):
                        mg = (B2 if c % 2 == 0 else KK2)[ro, m, :]
                        last = mm(PS[2 * (c % 2) + par][ro, m * CH:(m + 1) * CH], mg[:, (c // 2) * CH:(c // 2 + 1) * CH],
                                  HS2[ro, 4 * c + m, :], start=True, stop=True)
                raise_(last, "h", c)
            after("dve", "h", NC2 - 1)
            for m in range(4):
                if m >= 2:
                    after("dve", "y", m - 2)
                for par in range(2):
                    ro = slice(64 * par, 64 * par + 64)
                    for c in range(NC2):
                        last = mm(PS[4 + 2 * (m % 2) + par][ro, c * CH:(c + 1) * CH], HS2[ro, 4 * c + m, :],
                                  R2[ro, m, c * CH:(c + 1) * CH], start=True, stop=True)
                raise_(last, "y", m)
            for m in range(4):
                after("dve", "y", m)
                raise_(mm(PS[m][:], const("blocks"), V2[:, m, :], start=True, stop=True), "mean", m)
            after("dve", "y", 3)
            pe.wait_ge(pool_taps, len(POOL_CHUNKS) * (TAPS - 1))
            for m in range(4):
                last = mm(PS[6][:], ONES[:], C2[:, m, :], start=m == 0, stop=m == 3)
            raise_(last, "c mean")
            for m in range(4):
                after("act", "squares", m)
                raise_(mm(PS[m][:], const("blocks"), SQ[:, m, :], start=True, stop=True), "variance", m)
            after("act", "squares", 4)
            for m in range(4):
                last = mm(PS[7][:], ONES[:], SQ[:, 4 + m, :], start=m == 0, stop=m == 3)
            raise_(last, "variance", 4)
            for m in range(4):
                if G_BANKS[m] < 4:
                    after("dve", "variances")
                raise_(mm(PS[G_BANKS[m]][:], GU2[:, m * P:(m + 1) * P], XG2, start=True, stop=True), "g", m)

        def pair_products(pe, m, raise_, after):
            mm = nc.tensor.matmul
            after("dve", "hat", m)
            if m:
                after("act", "mg", m - 1, 1)
                after("dve", "r", m - 1)
            for x, src in enumerate((BH2, KH2, KK2[:, m, :], V2[:, m, :])):
                for n in range(NT):
                    last = nc.tensor.transpose(PS[x][:, n * P:(n + 1) * P], src[:, n * P:(n + 1) * P], IDENT)
                raise_(last, "tok", m, x)
            for n in range(NT):
                for par in range(2):
                    q = 2 * n + par
                    if q >= 4:
                        after("dve", "au", m, (q - 4) // 2, q % 2)
                    ro, tk = slice(64 * par, 64 * par + 64), slice(n * P, (n + 1) * P)
                    for y, (left, right) in enumerate(((B2, KK2), (K2, KK2), (B2, R2), (K2, R2))):
                        last = mm(PS[4 + q % 4][:, y * P:(y + 1) * P], left[ro, m, tk], right[ro, m, tk], start=True, stop=True)
                    raise_(last, "au", m, n, par)

            def au(par, n, y):
                return AU2[:, 4 * par + n, y * P:(y + 1) * P]

            def tok(x, par, n, rows=slice(0, P)):
                return TOK2[rows, x, n * P + 64 * par:n * P + 64 * par + 64]

            after("act", "tok", m, 3)
            after("dve", "au", m, NT - 1, 1)
            for par in range(2):
                for n in range(NT):
                    last = mm(PS[0][:, (4 * par + n) * CH:(4 * par + n + 1) * CH], au(par, n, 1), tok(3, par, n), start=True, stop=True)
            raise_(last, "av", m)
            for par in range(2):
                after("dve", "ml", m, 0, par)
                for n in range(NT):
                    last = nc.tensor.transpose(PS[3 + 2 * par][:, n * P:(n + 1) * P], ML2[:, par, n * P:(n + 1) * P], IDENT)
                raise_(last, "t", m, 0, par)
            for l in range(1, 6):
                for par in range(2):
                    after("dve", "ml", m, l, par)
                    if l > 1:
                        after("dve", "inv", m, l - 1, par)
                    for n in range(NT):
                        last = mm(PS[1 + par][:, n * P:(n + 1) * P], ML2[:, par, n * P:(n + 1) * P],
                                  TI2[:, 2 * par, n * P:(n + 1) * P], start=True, stop=True)
                    raise_(last, "x", m, l, par)
                for par in range(2):
                    after("act", "x", m, l, par)
                    if l > 1:
                        after("dve", "t", m, l - 1, par)
                    for n in range(NT):
                        tk = slice(n * P, (n + 1) * P)
                        if l < 5:
                            mm(PS[3 + 2 * par][:, tk], TI2[:, 2 * par + 1, tk], XS2[:, par, tk], start=True, stop=True)
                        last = mm(PS[4 + 2 * par][:, tk], XS2[:, par, tk], TI2[:, 2 * par + 1, tk], start=True, stop=True)
                    raise_(last, "t", m, l, par)
            after("act", "av", m)
            for par in range(2):
                after("dve", "t", m, 5, par)
                b = 7 if par else 0
                for n in range(NT):
                    tt = TI2[:, 2 * par + 1, n * P:(n + 1) * P]
                    mm(PS[b][:, n * P:n * P + CH], tt, tok(2, par, n), start=True, stop=True)
                    last = mm(PS[b][:, n * P + CH:(n + 1) * P], tt, AV2[:, (4 * par + n) * CH:(4 * par + n + 1) * CH],
                              start=True, stop=True)
                raise_(last, "tz", m, par)

            def tz(par, n, half, rows=slice(0, P)):
                return TZ2[rows, par, n * P + half * CH:n * P + (half + 1) * CH]

            after("act", "tz", m, 1)
            for par in range(2):
                for n in range(NT):
                    last = mm(PS[1][64 * par:64 * par + 64, n * P:(n + 1) * P], tz(par, n, 0), au(par, n, 2), start=True, stop=True)
            raise_(last, "r", m)
            for par in range(2):
                for n in range(NT):
                    o = PS[2][64 * par:64 * par + 64, n * P:(n + 1) * P]
                    mm(o, tok(3, par, n), au(par, n, 3), start=True, stop=False)
                    last = mm(o, tz(par, n, 1), au(par, n, 2), start=False, stop=True)
            raise_(last, "yl", m)
            for half in range(2):
                rows = slice(64 * half, 64 * half + 64)
                for par in range(2):
                    for n in range(NT):
                        o = PS[3 + half][64 * par:64 * par + 64, :]
                        mm(o[:, n * CH:(n + 1) * CH], tz(par, n, 0, rows), tok(0, par, n, rows), start=True, stop=True)
                        g = o[:, (4 + n) * CH:(5 + n) * CH]
                        mm(g, tok(0, par, n, rows), tz(par, n, 1, rows), start=True, stop=False)
                        last = mm(g, tok(1, par, n, rows), tok(3, par, n, rows), start=False, stop=True)
                raise_(last, "mg", m, half)

        def act_mix2(act, t, sub, h):
            w, split = t("w"), h["split"]
            raise_, after = stepper(act, "act")
            ac = nc.scalar.activation
            act.wait_ge(m2_zero, 1)
            for u in range(U2):
                act.wait_ge(w_used, w + u + 1)
                split(w + u + 2)
                if u < 4:
                    if u >= 2:
                        act.wait_ge(glu_done, u - 1)
                    ac(SG[:, u % 2, :], PS[(2 * u + 1) % 8][:], ACT.Sigmoid).then_inc(gate_done, 1)
                else:
                    for c in range(2):
                        q = 2 * (u - 4) + c
                        if q >= 4:
                            act.wait_ge(shifted, q - 3)
                        ac(RP2[:, q % 4, 1:], PS[(2 * u + c) % 8][:], ACT.Copy).then_inc(proj_evac, 1)
            t.add("w", U2)
            act.wait_ge(shifted, CHUNKS2)
            ac(LO2[0:64, :], LO2[0:64, :], ACT.Tanh)
            raise_(ac(XG2, XG2, ACT.Sigmoid), "low rank")
            for m in range(4):
                after("pe", "decay", m)
                last = ac(LW2[:, m, :], PS[m][:], ACT.Sigmoid, bias=col("w0", m))
            raise_(last, "sig d")
            for m in range(4):
                after("pe", "rate", m)
                last = ac(B2[:, m, :], PS[4 + m][:], ACT.Sigmoid, bias=col("a0", m))
            raise_(last, "sig a")
            after("dve", "kk raw")
            raise_(ac(T2, KK2, ACT.Square), "kk sq")
            after("dve", "kk v")
            h["chain"](ac(R0W, V2W, ACT.Ln))
            raise_(ac(R0W, R0W, ACT.Exp, scale=-0.5), "kk r0")
            after("dve", "sums")
            raise_(ac(LW2, LW2, ACT.Exp, scale=-DECAY), "before")
            after("pe", "bonus", 3)
            raise_(ac(T2, CC2, ACT.Exp, scale=DECAY), "inverse")
            raise_(ac(CC2, CC2, ACT.Exp, scale=-DECAY), "decays")
            for m in range(4):
                for x in range(4):
                    after("pe", "tok", m, x)
                    raise_(ac(TOK2[:, x, :], PS[x][:], ACT.Copy), "tok", m, x)
                after("pe", "av", m)
                raise_(ac(AV2, PS[0][:], ACT.Copy), "av", m)
                for l in range(1, 6):
                    for par in range(2):
                        after("pe", "x", m, l, par)
                        raise_(ac(XS2[:, par, :], PS[1 + par][:], ACT.Copy), "x", m, l, par)
                for par in range(2):
                    after("pe", "tz", m, par)
                    raise_(ac(TZ2[:, par, :], PS[7 if par else 0][:], ACT.Copy), "tz", m, par)
                after("pe", "yl", m)
                raise_(ac(V2[:, m, :], PS[2][:], ACT.Copy), "yl", m)
                for half, dest in enumerate((B2, KK2)):
                    after("pe", "mg", m, half)
                    raise_(ac(dest[:, m, :], PS[3 + half][:], ACT.Copy), "mg", m, half)
            for m in range(4):
                after("dve", "centred", m)
                raise_(ac(SQ[:, m, :], V2[:, m, :], ACT.Square), "squares", m)
            after("dve", "c centred")
            raise_(ac(SQ[:, 4:8, :], C2, ACT.Square), "squares", 4)
            after("dve", "variances")
            h["chain"](ac(R0_5, V_5, ACT.Ln))
            raise_(ac(R0_5, R0_5, ACT.Exp, scale=-0.5), "norms r0")
            for m in range(4):
                after("dve", "c out", m)
                ac(Y[:, 4 + m, :], C2[:, m, :], ACT.Silu, bias=col("conv_ln_b", m)).then_inc(silu2, 1)
            act.wait_ge(silu2, 4)
            h["high"](Y, given=KD, ready=lambda m: m < 4 and after("dve", "out", m))

        def dve_mix2(dve, t, sub, h):
            w, split, chain = t("w"), h["split"], h["chain"]
            raise_, after = stepper(dve, "dve")
            v = nc.vector
            dve.wait_ge(m2_zero, 2)
            dve.wait_ge(m2_loads, 48)
            taps = [(m, n) for m in range(3) if m not in POOL_CHUNKS for n in range(TAPS)]
            last_taps = list(range(TAPS))

            def shift(q):
                dest = (R2, K2, V2)[q // 4][:, q % 4, :] if q < 12 else (LO2, XG2)[q - 12]
                dve.wait_ge(proj_evac, t("proj") + q + 1)
                now, before = RP2[:, q % 4, 1:], RP2[:, q % 4, 0:S]
                chain(v.tensor_tensor(V[:], before, now, ALU.subtract))
                v.scalar_tensor_tensor(dest, V[:], col("mu", q), now, ALU.mult, ALU.add).then_inc(shifted, 1)
                dve.wait_ge(shifted, q + 1)

            for u in range(U2):
                split(w + u + 2)
                if u < 4:
                    dve.wait_ge(gate_done, u + 1)
                    v.tensor_tensor(glu(u, TAPS - 1), PS[2 * u % 8][:], SG[:, u % 2, :], ALU.mult).then_inc(glu_done, 1)
                    dve.wait_ge(glu_done, u + 1)
                else:
                    shift(2 * (u - 4))
                    shift(2 * (u - 4) + 1)
                for _ in range(8):
                    if taps and taps[0][0] < u:
                        chain(tap(v, *taps.pop(0)))
            for x in taps:
                chain(tap(v, *x))
            t.add("w", U2)
            t.add("proj", CHUNKS2)
            dve.wait_ge(shifted, CHUNKS2)
            for m in range(4):
                last = v.tensor_scalar(KK2[:, m, :], K2[:, m, :], col("k_k", m), None, ALU.mult)
            raise_(last, "kk raw")
            for _ in range(10):
                chain(tap(v, 3, last_taps.pop(0)))
            after("act", "sig d")
            for m in range(4):
                last = v.tensor_tensor_scan(CC2[:, m, :], SEG2, LW2[:, m, :], 0.0, ALU.mult, ALU.add)
            chain(last)
            raise_(v.tensor_tensor(LW2, CC2, LW2, ALU.subtract), "sums")
            for _ in range(7):
                chain(tap(v, 3, last_taps.pop(0)))
            dve.wait_ge(pool_taps, len(POOL_CHUNKS) * (TAPS - 1))
            for m in range(4):
                after("pe", "kk", m)
                last = v.tensor_scalar(V2W[:, m, :], PS[m][:], 1e-12, None, ALU.max)
            raise_(last, "kk v")
            for m in range(4):
                last = v.tensor_scalar(T2[:, m, :], B2[:, m, :], 1.0, col("k_a", m), ALU.subtract, ALU.mult)
            chain(last)
            chain(v.scalar_tensor_tensor(K2, T2, 1.0, K2, ALU.add, ALU.mult))
            chain(v.tensor_tensor(T2, R2, K2, ALU.mult))
            for m in range(4):
                last = v.tensor_scalar(T2[:, m, :], T2[:, m, :], col("r_k", m), None, ALU.mult)
            raise_(last, "rk")
            after("act", "kk r0")
            chain(v.tensor_tensor(RW, R0W, R0W, ALU.mult))
            chain(v.scalar_tensor_tensor(RW, RW, -0.5, V2W, ALU.mult, ALU.mult))
            chain(v.scalar_tensor_tensor(RW, RW, 1.5, R0W, ALU.add, ALU.mult))
            chain(v.tensor_tensor(KK2, KK2, RW, ALU.mult))
            chain(v.tensor_tensor(B2, KK2, B2, ALU.mult))
            for m in range(4):
                after("pe", "bonus", m)
                last = v.tensor_tensor(BV2[:, m, :], PS[4 + m][:], V2[:, m, :], ALU.mult)
            raise_(last, "bonus read")
            after("act", "before")
            v.scalar_tensor_tensor(KK2, KK2, -1.0, LW2, ALU.mult, ALU.mult)
            after("act", "inverse")
            v.tensor_tensor(B2, B2, T2, ALU.mult)
            v.tensor_tensor(K2, K2, T2, ALU.mult)
            after("act", "decays")
            chain(v.tensor_copy(PC2[:], CC2.rearrange("p m (c s) -> p m c s", s=CH)[:, :, :, CH - 1]))
            raise_(v.tensor_tensor(R2, R2, CC2, ALU.mult), "scaled")
            for m in range(4):
                pc = PC2[:, m, :].unsqueeze(2).to_broadcast([P, NC2, CH])

                def by_chunk(x):
                    return x.rearrange("p (c s) -> p c s", s=CH)

                v.tensor_tensor(by_chunk(BH2), by_chunk(B2[:, m, :]), pc, ALU.mult)
                raise_(v.tensor_tensor(by_chunk(KH2), by_chunk(K2[:, m, :]), pc, ALU.mult), "hat", m)
                masks = const("later", 2 * P).rearrange("p (a t) -> p a t", a=2).unsqueeze(2).to_broadcast([P, 2, 2, P])
                for n in range(NT):
                    for par in range(2):
                        after("pe", "au", m, n, par)
                        q = 2 * n + par
                        ps = PS[4 + q % 4][:].rearrange("p (a b t) -> p a b t", a=2, b=2)
                        au = AU2[:, 4 * par + n, :].rearrange("p (a b t) -> p a b t", a=2, b=2)
                        raise_(v.tensor_tensor(au, ps, masks, ALU.mult), "au", m, n, par)

                def tiles(x):
                    return x.rearrange("p (n t) -> p n t", n=NT)

                def level(l, par):
                    zb = AU2[:, 4 * par:4 * par + 4, 0:P]
                    mask = LEVELS[:, l * P:(l + 1) * P].unsqueeze(1).to_broadcast([P, NT, P])
                    raise_(v.tensor_tensor(tiles(ML2[:, par, :]), zb, mask, ALU.mult), "ml", m, l, par)

                ident = IDENT.unsqueeze(1).to_broadcast([P, NT, P])
                for par in range(2):
                    level(0, par)
                    chain(v.tensor_tensor(tiles(TI2[:, 2 * par + 1, :]), ident, tiles(ML2[:, par, :]), ALU.add))
                for par in range(2):
                    after("pe", "t", m, 0, par)
                    raise_(v.tensor_tensor(tiles(TI2[:, 2 * par, :]), ident, tiles(PS[3 + 2 * par][:]), ALU.add), "t", m, 0, par)
                    level(1, par)
                for l in range(1, 6):
                    for par in range(2):
                        if l < 5:
                            after("pe", "x", m, l, par)
                            level(l + 1, par)
                    for par in range(2):
                        after("pe", "t", m, l, par)
                        if l < 5:
                            raise_(v.tensor_tensor(TI2[:, 2 * par, :], TI2[:, 2 * par, :], PS[3 + 2 * par][:], ALU.add),
                                   "inv", m, l, par)
                        raise_(v.tensor_tensor(TI2[:, 2 * par + 1, :], TI2[:, 2 * par + 1, :], PS[4 + 2 * par][:], ALU.add),
                               "t", m, l, par)
                        if last_taps and par:
                            chain(tap(v, 3, last_taps.pop(0)))
                for _ in range(4):
                    if last_taps:
                        chain(tap(v, 3, last_taps.pop(0)))
                after("pe", "r", m)
                raise_(v.tensor_tensor(R2[:, m, :], R2[:, m, :], PS[1][:], ALU.add), "r", m)
            assert not last_taps
            after("act", "mg", 3, 1)
            raise_(v.memset(HS2[:, 0:4, :], 0.0), "h", 0)
            for c in range(NC2 - 1):
                g = (B2 if c % 2 == 0 else KK2)[:, :, (4 + c // 2) * CH:(5 + c // 2) * CH]
                pc = PC2[:, :, c].unsqueeze(2).to_broadcast([P, 4, CH])
                new = HS2[:, 4 * c + 4:4 * c + 8, :]
                chain(v.tensor_tensor(new, HS2[:, 4 * c:4 * c + 4, :], pc, ALU.mult))
                chain(v.tensor_tensor(new, new, g, ALU.add))
                after("pe", "h", c)
                for par in range(2):
                    ro = slice(64 * par, 64 * par + 64)
                    last = v.tensor_tensor(new[ro], new[ro], PS[2 * (c % 2) + par][ro, 0:4 * CH].rearrange(
                        "p (m v) -> p m v", m=4), ALU.add)
                raise_(last, "h", c + 1)
            for m in range(4):
                after("pe", "y", m)
                for par in range(2):
                    ro = slice(64 * par, 64 * par + 64)
                    last = v.tensor_tensor(V2[ro, m, :], V2[ro, m, :], PS[4 + 2 * (m % 2) + par][ro, :], ALU.add)
                raise_(last, "y", m)
            for m in range(4):
                after("pe", "mean", m)
                raise_(v.scalar_tensor_tensor(V2[:, m, :], PS[m][:], -1.0 / CH, V2[:, m, :], ALU.mult, ALU.add), "centred", m)
            after("pe", "c mean")
            chain(v.tensor_scalar(MU2, PS[6][:], 1.0 / (4 * P), None, ALU.mult))
            raise_(v.tensor_tensor(C2, C2, MU2.unsqueeze(1).to_broadcast([P, 4, S]), ALU.subtract), "c centred")
            lo = h["low"](Y)
            for m in range(4):
                after("pe", "variance", m)
                v.tensor_scalar(V_5[:, m, :], PS[m][:], 1.0 / CH, 64e-5, ALU.mult, ALU.add)
            after("pe", "variance", 4)
            raise_(v.tensor_scalar(V_5[:, 4, :], PS[7][:], 1.0 / (4 * P), 1e-5, ALU.mult, ALU.add), "variances")
            after("act", "norms r0")
            for m in (4, 0, 1, 2, 3):
                r, r0, v_ = R_5[:, m, :], R0_5[:, m, :], V_5[:, m, :]
                chain(v.tensor_tensor(r, r0, r0, ALU.mult))
                chain(v.scalar_tensor_tensor(r, r, -0.5, v_, ALU.mult, ALU.mult))
                chain(v.scalar_tensor_tensor(r, r, 1.5, r0, ALU.add, ALU.mult))
                if m == 4:
                    for c in range(4):
                        raise_(v.scalar_tensor_tensor(C2[:, c, :], C2[:, c, :], col("conv_ln_w", c), r, ALU.mult, ALU.mult),
                               "c out", c)
                    continue
                y = V2[:, m, :]
                chain(v.scalar_tensor_tensor(y, y, col("gn_w", m), r, ALU.mult, ALU.mult))
                chain(v.scalar_tensor_tensor(y, y, col("gn_b", m), BV2[:, m, :], ALU.add, ALU.add))
                after("pe", "g", m)
                raise_(v.tensor_tensor(Y[:, m, :], y, PS[G_BANKS[m]][:], ALU.mult), "out", m)
            for m in range(4):
                dve.wait_ge(silu2, m + 1)
            for m in range(KD):
                lo(m)

        def pool_mixers(pool):
            for sub in plan["subs"]:
                if sub["kind"] == "mix1":
                    pool_mix1(pool)
                if sub["kind"] == "mix2":
                    pool_mix2(pool)
                if sub["kind"] == "mix3":
                    pool_mix3(pool, sub["name"])

        pe_mixers = {"mix1": pe_mix1, "mix2": pe_mix2, "mix3": pe_mix3}
        act_mixers = {"mix1": act_mix1, "mix2": act_mix2, "mix3": act_mix3}
        dve_mixers = {"mix1": dve_mix1, "mix2": dve_mix2, "mix3": dve_mix3}
        starts, n_sub_w, n_sub_hl = {}, 0, 0
        for sub_ in plan["subs"]:
            starts[sub_["name"]] = (n_sub_w, n_sub_hl + KD)
            n_sub_w += sum(c for _, c in sub_["units"])
            n_sub_hl += KD * (2 if sub_["kind"] != "ffn" else 1)
        M1_START, M1_HL = starts.get("m1", (0, 0))

        block = ctx.enter_context(nc.Block())

        @block.sync
        def _(sp):
            sp.dma_start(PV[:], T["pv"]).then_inc(params, 16)
            sp.dma_start(ONES[:], T["ones"]).then_inc(params, 16)
            if plan["ada"]:
                for a in range(ADA_FIRST):
                    sp.dma_start(ada_raw(a), T["ada"][a]).then_inc(first_loaded[a], 16)
                    if a == 1:
                        sp.dma_start(X[:], T["x"].rearrange("(m p) s -> p m s", p=P)).then_inc(x_loaded, 16)
            else:
                sp.dma_start(X[:], T["x"].rearrange("(m p) s -> p m s", p=P)).then_inc(x_loaded, 16)
            sp.dma_start(CN[:], T["cn"]).then_inc(cn_loaded, 16)

            def load(w, i=0):
                if w >= 2:
                    sp.wait_ge(w_lo, w - 1 + i)
                src = T["w"][bass.ds(w + i, 1), :, :].rearrange("o p n -> (o p) n")
                sp.dma_start(RAW[:, w % 2, :], src).then_inc(raw_loaded[w % 2], 16)

            load(0)
            load(1)
            with sp.Fori(0, (n_w - 2) // 2) as i:
                load(2, 2 * i)
                load(3, 2 * i)
            if n_w % 2:
                load(n_w - 1)
            final = T["final_reads"]
            for m in range(KD):
                sp.wait_ge(t_ready if plan["final"] else x_done, final + (m + 1 if plan["final"] else KD))
                sp.dma_start(T["out"][m * P:(m + 1) * P, :], (Y if plan["final"] else X)[:, m, :]).then_inc(stored, 16)
            sp.wait_ge(stored, 16 * KD)

        @block.gpsimd
        def _(pool):
            if plan["ada"]:
                def load_ada(a, i=0):
                    pool.wait_ge(ada_used, a - ADA_SLOTS + 1 + i)
                    src = T["ada"][bass.ds(a + i, 1), :, :].rearrange("o p n -> (o p) n")
                    n = a % ADA_SLOTS
                    pool.dma_start(ada_raw(n), src).then_inc(ada_loaded[n], 16)

                with pool.Fori(0, (ADA - ADA_FIRST) // ADA_SLOTS) as i:
                    for a in range(ADA_FIRST, ADA_FIRST + ADA_SLOTS):
                        load_ada(a, ADA_SLOTS * i)
            pool_mixers(pool)

        @block.tensor
        def _(pe):
            t = Tally()

            def mm3(out, wh, wl, xh, xl, start, stop):
                nc.tensor.matmul(out, wh, xh, start=start, stop=False)
                nc.tensor.matmul(out, wh, xl, start=False, stop=False)
                return nc.tensor.matmul(out, wl, xh, start=False, stop=stop)

            def blocks(w):
                return (WH[:, w % 2, :].rearrange("p (b c) -> p b c", c=P),
                        WL[:, w % 2, :].rearrange("p (b c) -> p b c", c=P))

            def unit_arrives(w, i=0):
                pe.wait_ge(w_hi, w + 1 + i)
                pe.wait_ge(w_lo, w + 1 + i)

            def project(w, banks, first=False, between=lambda c: None):
                wh, wl = blocks(w)

                def block(c, k):
                    return mm3(PS[banks[c]][:], wh[:, KD * c + k, :], wl[:, KD * c + k, :],
                               HH[:, k, :], HL[:, k, :], k == 0, k == KD - 1)

                if first:
                    for k in range(KD):
                        pe.wait_ge(hl_done, t("hl") - KD + k + 1)
                        block(0, k)
                        last = block(1, k)
                    last.then_inc(w_used, 1)
                    return
                for c in range(2):
                    for k in range(KD):
                        last = block(c, k)
                    if c == 1:
                        last.then_inc(w_used, 1)
                    between(c)

            def norm(n=KD, src=None, order=None, weights=None):
                e = t.add("norms")
                src = SQ if src is None else src
                for j in range(n):
                    pe.wait_ge(sq_done, t.add("sq"))
                    if j == 0 and e >= 2:
                        pe.wait_ge(r_done, e - 1)
                    m = order[j] if order else j
                    last = nc.tensor.matmul(PS[4 + e % 2][:], ONES[:] if weights is None else weights,
                                            src[:, m, :], start=j == 0, stop=j == n - 1)
                last.then_inc(stat_done, 1)

            def norm_added():
                e = t.add("norms")
                t.add("sq", KD)
                pe.wait_ge(sq_added, t.add("added"))
                nc.tensor.matmul(PS[4 + e % 2][:], ONES[:], SQ[:, ORDER[0], :], start=True, stop=True).then_inc(stat_done, 1)

            def ada(a, i=0):
                raw = ada_unit(a)
                for c in range(2):
                    out = PS[6][:, bass.ds(2 * a + c + 2 * i, 1)]
                    if a < ADA_FIRST and c == 0:
                        ada_arrives(pe, a)
                        for k in range(KD):
                            nc.tensor.matmul(out, raw[:, c, k, :], PV[:, cols["silu_c"] + k:cols["silu_c"] + k + 1],
                                             start=k == 0, stop=k == KD - 1)
                    else:
                        if a < ADA_FIRST or c == 0:
                            pe.wait_ge(ada_summed, a + 1 + i)
                        last = nc.tensor.matmul(out, raw[:, c, 0, :], ONES[:, 0:1], start=True, stop=True)
                last.then_inc(ada_used, 1)

            def ffn(sub, s):
                w, base = t("w"), t("act_ready")
                with_ada = plan["ada"] and s == 0

                def gate_up(u, i=0):
                    unit_arrives(w + u, i)
                    if u >= 2:
                        pe.wait_ge(act_ready, base + u - 1 + i)
                    project(w + u, (2 * (u % 2), 2 * (u % 2) + 1), first=u == 0)
                    if with_ada and 2 <= u < KF - 4:
                        ada(ADA_FIRST + u - 2, i)
                    elif with_ada and u >= KF - 4:
                        for a in ADA_LATE[u - KF + 4]:
                            ada(a - 2)

                t.add("hl", KD)
                gate_up(0)
                gate_up(1)
                with pe.Fori(0, KF - 6, 4) as i:
                    for u in (2, 3, 4, 5):
                        gate_up(u, i)
                for u in range(KF - 4, KF):
                    gate_up(u)
                w = t.add("w", KF)
                t.add("act_ready", KF)
                def down(u, i=0):
                    unit_arrives(w + u, i)
                    pe.wait_ge(ah_done, t("ah") + u + 1 + i)
                    pe.wait_ge(al_done, t("ah") + u + 1 + i)
                    wh, wl = blocks(w + u)
                    for m in ORDER:
                        if u == 0 and m == 0:
                            pe.wait_ge(act_ready, t("act_ready"))
                        if u == 0 and m == 6 and with_ada:
                            for a in range(ADA - ADA_SLOTS - 2, ADA - ADA_SLOTS):
                                ada(a)
                            pe.wait_ge(cv_read, 2)
                        for k in range(2):
                            last = mm3(PS[m][:], wh[:, KD * k + m, :], wl[:, KD * k + m, :],
                                       AH[:, u % 2, k, :], AL[:, u % 2, k, :],
                                       u == 0 and k == 0, u == DOWN - 1 and k == 1)
                        if u == DOWN - 1 and m != ORDER[-1]:
                            last.then_inc(out_done, 1)
                    last.then_inc(w_used, 1)

                down(0)
                down(1)
                with pe.Fori(0, DOWN - 3, 2) as i:
                    down(2, i)
                    down(3, i)
                down(DOWN - 1)
                t.add("w", DOWN)
                t.add("ah", DOWN)

            def out_projection():
                w = t("w")
                t.add("hl", KD)
                for u in range(4):
                    unit_arrives(w + u)
                    wh, wl = blocks(w + u)
                    pairs = [(c, k) for c in range(2) for k in range(KD)]
                    if u == 0:
                        pairs.sort(key=lambda x: x[1])
                    for c, k in pairs:
                        m = ORDER[2 * u + c]
                        if u == 0 and c == 0:
                            pe.wait_ge(hl_done, t("hl") - KD + k + 1)
                        last = mm3(PS[m][:], wh[:, KD * c + k, :], wl[:, KD * c + k, :],
                                   HH[:, k, :], HL[:, k, :], k == 0, k == KD - 1)
                        if k == KD - 1:
                            last.then_inc(w_used if c else out_done, 1)
                t.add("w", 4)

            pe.wait_ge(params, N_PARAMS)
            if plan["ada"]:
                pe.wait_ge(sc_ready, 1)
                ada(0)
            norm()
            if plan["ada"]:
                for a in range(1, ADA_FIRST):
                    ada(a)
            pe.wait_ge(consts_ready, 4)
            for s, sub in enumerate(plan["subs"]):
                if plan["ada"] and s == 0:
                    pe.wait_ge(cv_read, 1)
                if sub["kind"] == "ffn":
                    ffn(sub, s)
                else:
                    pe_mixers[sub["kind"]](pe, t, sub, dict(mm3=mm3, blocks=blocks, unit_arrives=unit_arrives,
                                                           project=project, norm=norm))
                    out_projection()
                if sub["post"]:
                    norm_added()
                    t.add("y_evac", KD)
                if plan["ada"] and s == 0:
                    pe.wait_ge(y_evac, KD)
                    pe.wait_ge(sq_done, t("sq"))
                    for a in range(ADA - ADA_SLOTS, ADA):
                        ada(a)
                if plan["final"] or s + 1 < len(plan["subs"]):
                    norm() if sub["post"] else norm_added()

        @block.scalar
        def _(act):
            t = Tally()
            chain = Chain(act, sem("act_chain"))

            def split(w, i=0):
                if w >= n_w:
                    return
                act.wait_ge(raw_loaded[w % 2], 16 * (w // 2 + 1) + 8 * i)
                if w >= 2:
                    act.wait_ge(w_used, w - 1 + i)
                nc.scalar.activation(WH[:, w % 2, :], RAW[:, w % 2, :], ACT.Copy).then_inc(w_hi, 1)

            def rsqrt():
                e = t.add("norms")
                act.wait_ge(v_ready, e)
                chain(nc.scalar.activation(R0[:], V[:], ACT.Ln))
                nc.scalar.activation(R0[:], R0[:], ACT.Exp, scale=-0.5).then_inc(r0_done, 1)

            def norm_in(order, meanwhile=lambda: None):
                if t("norms"):
                    act.wait_ge(stat_done, t("norms"))
                for j, m in enumerate(order):
                    if t("x"):
                        act.wait_ge(x_done, t("x") - KD + j + 1)
                    nc.scalar.activation(SQ[:, m, :], X[:, m, :], ACT.Square).then_inc(sq_done, 1)
                meanwhile()
                rsqrt()

            def high(src, shift=None, given=0, ready=lambda m: None):
                t.add("t", KD - given)
                for m in range(KD):
                    ready(m)
                    if m >= given:
                        act.wait_ge(t_ready, t("t") - KD + m + 1)
                    if shift:
                        ins = nc.scalar.activation(HH[:, m, :], src[:, m, :], ACT.Identity, bias=col(shift, m))
                    else:
                        ins = nc.scalar.activation(HH[:, m, :], src[:, m, :], ACT.Copy)
                    ins.then_inc(hh_done, 1)

            def ffn(sub, s):
                w, base = t("w"), t("act_ready")

                def silu(u, i=0):
                    act.wait_ge(w_used, w + u + 1 + i)
                    if u >= 2:
                        act.wait_ge(act_ready, base + u - 1 + i)
                    nc.scalar.activation(SG[:, u % 2, :], PS[2 * (u % 2)][:], ACT.Silu).then_inc(silu_done, 1)

                def high_act(n, i=0):
                    nc.scalar.activation(AH[:, n % 2, :, :], A[:, bass.ds(2 * n + 2 * i, 2), :], ACT.Copy)\
                        .then_inc(ah_done, 1)

                for u in (0, 1):
                    silu(u)
                    split(w + u + 2)
                with act.Fori(0, KF - 4, 2) as i:
                    for u in (2, 3):
                        silu(u, i)
                        split(w + u + 2, i)
                act.wait_ge(act_ready, base + 4)
                high_act(0)
                high_act(1)
                for u in (KF - 2, KF - 1):
                    silu(u)
                    split(w + u + 2)
                w = t.add("w", KF)
                t.add("act_ready", KF)
                act.wait_ge(act_ready, t("act_ready"))

                def after_down(u, i=0):
                    act.wait_ge(w_used, w + u + 1 + i)
                    high_act(u + 2, i)
                    split(w + u + 2, i)

                with act.Fori(0, DOWN - 3, 2) as i:
                    after_down(0, i)
                    after_down(1, i)
                after_down(DOWN - 3)
                act.wait_ge(w_used, w + DOWN - 1)
                split(w + DOWN)
                t.add("w", DOWN)

            act.wait_ge(params, N_PARAMS)
            if plan["ada"]:
                sc = PV[:, cols["silu_c"]:cols["silu_c"] + KD]
                nc.scalar.activation(sc, PV[:, cols["c"]:cols["c"] + KD], ACT.Silu).then_inc(sc_ready, 1)
            act.wait_ge(x_loaded, 16)
            norm_in(range(KD))
            split(0)
            split(1)
            for s, sub in enumerate(plan["subs"]):
                high(Y, sub["shift"])
                if sub["kind"] == "ffn":
                    ffn(sub, s)
                else:
                    act_mixers[sub["kind"]](act, t, sub, dict(split=split, rsqrt=rsqrt, chain=chain, high=high))
                    w = t("w")
                    for u in range(3):
                        act.wait_ge(w_used, w + u + 1)
                        split(w + u + 2)
                    t.add("w", 4)
                if sub["post"]:
                    act.wait_ge(stat_done, t("norms"))
                    for m in ORDER:
                        act.wait_ge(y_evac, t.add("y_evac"))
                        nc.scalar.activation(SQ[:, m, :], Y[:, m, :], ACT.Square).then_inc(sq_done, 1)
                    rsqrt()
                out_passed(t, sub)
                t.add("x", KD)
                if plan["final"] or s + 1 < len(plan["subs"]):
                    if sub["post"]:
                        split(t("w") + 1)
                        norm_in(range(KD))
                    else:
                        norm_in(ORDER, lambda: split(t("w") + 1))

        @block.vector
        def _(dve):
            t = Tally()
            chain = Chain(dve, sem("dve_chain"))

            def split(w, i=0):
                if w >= n_w:
                    return
                dve.wait_ge(w_hi, w + 1 + i)
                nc.vector.tensor_tensor(WL[:, w % 2, :], RAW[:, w % 2, :], WH[:, w % 2, :].bitcast(F32),
                                        ALU.subtract).then_inc(w_lo, 1)

            def rsqrt(n=KD, scale=None, eps=EPS, meanwhile=lambda: None):
                e = t.add("norms")
                dve.wait_ge(stat_done, e)
                nc.vector.tensor_scalar(V[:], PS[4 + e % 2][:], 1.0 / (n * P) if scale is None else scale, eps,
                                        ALU.mult, ALU.add).then_inc(v_ready, 1)
                meanwhile()
                dve.wait_ge(r0_done, e)
                chain(nc.vector.tensor_tensor(R[:], R0[:], R0[:], ALU.mult))
                chain(nc.vector.scalar_tensor_tensor(R[:], R[:], -0.5, V[:], ALU.mult, ALU.mult))
                nc.vector.scalar_tensor_tensor(R[:], R[:], 1.5, R0[:], ALU.add, ALU.mult).then_inc(r_done, 1)
                dve.wait_ge(r_done, e)

            def low(src, shift=None):
                def one(m):
                    dve.wait_ge(hh_done, t("hh") - KD + m + 1)
                    nc.vector.scalar_tensor_tensor(HL[:, m, :], src[:, m, :], col(shift, m) if shift else 0.0,
                                                   HH[:, m, :].bitcast(F32), ALU.add, ALU.subtract)\
                        .then_inc(hl_done, 1)
                t.add("hh", KD)
                return one

            def norm_in(gain, shift, summed=False):
                if not summed:
                    rsqrt(meanwhile=lambda: split(t("w") + 1))
                lo = low(Y, shift) if gain != plan["final"] else None
                for m in range(KD):
                    nc.vector.scalar_tensor_tensor(Y[:, m, :], X[:, m, :], col(gain, m), R[:], ALU.mult, ALU.mult)\
                        .then_inc(t_ready, 1)
                    if lo and m >= 1:
                        lo(m - 1)
                if lo:
                    lo(KD - 1)

            def ffn(sub, s):
                w, base = t("w"), t("silu")

                def gated(u, i=0):
                    dve.wait_ge(silu_done, base + u + 1 + i)
                    nc.vector.tensor_tensor(A[:, bass.ds(u + i, 1), :].rearrange("p o s -> p (o s)"),
                                            SG[:, u % 2, :], PS[2 * (u % 2) + 1][:], ALU.mult)\
                        .then_inc(act_ready, 1)

                def low_act(n, i=0):
                    dve.wait_ge(ah_done, t("ah") + n + 1 + i)
                    nc.vector.tensor_tensor(AL[:, n % 2, :, :], A[:, bass.ds(2 * n + 2 * i, 2), :],
                                            AH[:, n % 2, :, :].bitcast(F32), ALU.subtract).then_inc(al_done, 1)

                with_ada = plan["ada"] and s == 0

                def step(u, i=0):
                    gated(u, i)
                    split(w + u + 2, i)
                    if with_ada and u < KF - 4:
                        ada_sums(ADA_FIRST + u, i)
                    elif with_ada:
                        for a in ADA_LATE[u - KF + 4]:
                            ada_sums(a)

                for u in (0, 1):
                    step(u)
                with dve.Fori(0, KF - 6, 4) as i:
                    for u in (2, 3, 4, 5):
                        step(u, i)
                for u in range(KF - 4, KF - 2):
                    step(u)
                low_act(0)
                low_act(1)
                for u in range(KF - 2, KF):
                    step(u)
                w = t.add("w", KF)
                t.add("silu", KF)
                if with_ada:
                    dve.wait_ge(ada_used, ADA - ADA_SLOTS)
                    modulation(2 * ADA_FIRST, 2 * (ADA - ADA_SLOTS))

                def after_down(u, i=0):
                    low_act(u + 2, i)
                    split(w + u + 2, i)

                if with_ada:
                    for u in range(DOWN - 3):
                        after_down(u)
                        if u < ADA_SLOTS:
                            ada_sums(ADA - ADA_SLOTS + u)
                else:
                    with dve.Fori(0, DOWN - 3, 2) as i:
                        after_down(0, i)
                        after_down(1, i)
                after_down(DOWN - 3)
                split(w + DOWN)
                t.add("w", DOWN)
                t.add("ah", DOWN)

            def add_squares(j):
                if j < 1:
                    return
                dve.wait_ge(sq_done, t("sq") + j + 1)
                first = SQ[:, ORDER[0], :]
                ins = nc.vector.tensor_tensor(first, first, SQ[:, ORDER[j], :], ALU.add)
                if j < KD - 1:
                    chain(ins)
                else:
                    ins.then_inc(sq_added, 1)

            def ada_sums(a, i=0):
                raw = ada_unit(a)
                silu_c = PV[:, cols["silu_c"]:cols["silu_c"] + KD].unsqueeze(2)
                ada_arrives(dve, a, i)
                if a < ADA_FIRST:
                    x, by = raw[:, 1, :, :], silu_c.to_broadcast([P, KD, P])
                else:
                    x, by = raw, silu_c.unsqueeze(1).to_broadcast([P, 2, KD, P])
                nc.vector.tensor_tensor(x, x, by, ALU.mult).then_inc(ada_scaled, 1)
                for n, half in enumerate((4, 2, 1)):
                    dve.wait_ge(ada_scaled, 3 * a + n + 1 + 3 * i)
                    nc.vector.tensor_tensor(x[..., 0:half, :], x[..., 0:half, :], x[..., half:2 * half, :], ALU.add)\
                        .then_inc(ada_summed if half == 1 else ada_scaled, 1)

            def modulation(a, b):
                bank = PS[6][:, a:b]
                nc.vector.tensor_tensor(CV[:, a:b], bank, PV[:, cols["b_ada"] + a:cols["b_ada"] + b], ALU.add)\
                    .then_inc(cv_read, 1)
                dve.wait_ge(cv_read, t.add("cv"))
                for v in range(a // KD, -(-b // KD)):
                    c0, c1 = max(a, v * KD), min(b, (v + 1) * KD)
                    sub, what, m = v // 3, v % 3, c0 - v * KD
                    if what == 0:
                        continue
                    name, factor = ("npre", 1.0) if what == 1 else ("npost", 0.5 if sub != 1 else 1.0)
                    g = PV[:, cols[f"{name}{sub}"] + m:cols[f"{name}{sub}"] + m + c1 - c0]
                    cv = CV[:, c0:c1]
                    chain(nc.vector.scalar_tensor_tensor(cv, cv, 1.0, g, ALU.add, ALU.mult))
                    if factor != 1.0:
                        chain(nc.vector.tensor_scalar(cv, cv, factor, None, ALU.mult))

            dve.wait_ge(params, N_PARAMS)
            t.add("sq", KD)
            if plan["ada"]:
                dve.wait_ge(sc_ready, 1)
                ada_sums(0)
            rsqrt()
            if plan["ada"]:
                for a in range(1, ADA_FIRST):
                    ada_sums(a)
                dve.wait_ge(ada_used, ADA_FIRST)
                modulation(0, 2 * ADA_FIRST)
            dve.wait_ge(cn_loaded, 16)
            for to, name in ((IDB, "ident"), (MKC, "causal"), (MKB, "chunked")):
                nc.vector.tensor_copy(to[:], const(name)).then_inc(consts_ready, 1)
            nc.vector.tensor_copy(ONE_ROW[:], const("ident")[0:8, 0:8]).then_inc(consts_ready, 1)
            half = PV[:, cols["ffn1_post_half"]:cols["ffn1_post_half"] + 2 * KD]
            chain(nc.vector.tensor_scalar(half, half, 0.5, None, ALU.mult))
            split(0)
            norm_in(plan["subs"][0]["pre"], plan["subs"][0]["shift"], summed=True)
            split(1)
            for s, sub in enumerate(plan["subs"]):
                if sub["kind"] == "ffn":
                    ffn(sub, s)
                else:
                    dve_mixers[sub["kind"]](dve, t, sub, dict(split=split, rsqrt=rsqrt, chain=chain, low=low))
                    w = t("w")
                    for u in range(3):
                        split(w + u + 2)
                    t.add("w", 4)
                t.add("x", KD)
                t.add("sq", KD if sub["kind"] == "mix1" else 0)
                more = plan["final"] or s + 1 < len(plan["subs"])
                if sub["post"]:
                    for j, m in enumerate(ORDER):
                        out_wait(dve, t, sub, j)
                        nc.vector.tensor_copy(Y[:, m, :], PS[m][:]).then_inc(y_evac, 1)
                        add_squares(j - 1)
                    add_squares(KD - 1)
                    t.add("sq", 2 * KD)
                    t.add("y_evac", KD)
                    rsqrt()
                    dve.wait_ge(y_evac, t("y_evac"))

                    def term(m):
                        return chain.mark(nc.vector.scalar_tensor_tensor(
                            SG[:, m % 2, :], Y[:, m, :], col(sub["post"], m), R[:], ALU.mult, ALU.mult))

                    ready = term(0)
                    for m in range(KD):
                        following = term(m + 1) if m + 1 < KD else None
                        chain.until(ready)
                        nc.vector.tensor_tensor(X[:, m, :], X[:, m, :], SG[:, m % 2, :], ALU.add).then_inc(x_done, 1)
                        if m + 1 < KD:
                            dve.wait_ge(x_done, t("x") - KD + m + 1)
                        ready = following
                else:
                    for j, m in enumerate(ORDER):
                        out_wait(dve, t, sub, j)
                        nc.vector.tensor_tensor(X[:, m, :], X[:, m, :], PS[m][:], ALU.add).then_inc(x_done, 1)
                        if more:
                            add_squares(j - 1)
                    if more:
                        add_squares(KD - 1)
                        t.add("sq", KD)
                out_passed(t, sub)
                dve.wait_ge(x_done, t("x"))
                if plan["ada"] and s == 0:
                    dve.wait_ge(ada_used, ADA)
                    modulation(2 * (ADA - ADA_SLOTS), VECTORS * KD)
                if s + 1 < len(plan["subs"]):
                    norm_in(plan["subs"][s + 1]["pre"], plan["subs"][s + 1]["shift"])
                elif plan["final"]:
                    norm_in(plan["final"], None)


def more_vectors(a, v):
    v["fox_b"] = np.concatenate([a["fox_b_f"][0], np.zeros(P - 8, np.float32)])
    v["gnorm_a"] = a["gnorm_a_g"][0]
    v["gnorm_b"] = a["gnorm_b_g"][0]
    for to, n in (("mu", "shift_mu"), ("w0", "w0"), ("a0", "a0"), ("k_k", "k_k"), ("k_a", "k_a"), ("gn_w", "gn_w"),
                  ("gn_b", "gn_b"), ("conv_b", "conv_b"), ("conv_ln_w", "conv_ln_w"), ("conv_ln_b", "conv_ln_b")):
        v[to] = a[n + "_2"][0]
    v["r_k"] = a["r_k_2"][0].reshape(-1)
    v["conv_dw"] = a["conv_dw_2"][0].reshape(-1)
    none = np.zeros(P - 64, np.float32)
    for i in range(2):
        v[f"g_sub{i}"] = a["g_subln_3"][i]
        v[f"lam{i}"] = np.concatenate([x for n in ("q1", "q2", "k1", "k2") for x in (a[f"lam_{n}_3"][i], none)])


def constants():
    q, k = np.arange(P)[:, None], np.arange(P)[None]

    def rotation(n):
        r = np.zeros((P, P), np.float32)
        for d in range(P):
            if d % n < n // 2:
                r[d + n // 2, d] = -1.0
            else:
                r[d - n // 2, d] = 1.0
        return r

    return {"ident": np.eye(P, dtype=np.float32), 
            "blocks": (q // 64 == k // 64).astype(np.float32),
            "later": np.concatenate([(q // 64 == k // 64) & (k > q), (q // 64 == k // 64) & (k >= q)], axis=1).astype(np.float32),
            "rot64": rotation(64), "rot32": rotation(32),
            "causal": np.where(k <= q, 0.0, -BIG).astype(np.float32),
            "chunked": np.where(k // 64 <= q // 64, 0.0, -BIG).astype(np.float32)}


def more_arrays(a, plan):
    def rows(v):
        return np.ascontiguousarray(np.broadcast_to(v, (P, v.size)))
    out = {}
    kinds = [s["kind"] for s in plan["subs"]]
    if "mix1" in kinds:
        out["ln_g"], out["ln_b"] = rows(a["sgu_ln_g"][0]), rows(a["sgu_ln_b"][0])
        out["sgu_w"] = np.ascontiguousarray(a["sgu_w"][0].transpose(2, 0, 1))
        b = a["sgu_b"][0].reshape(4, 2, P)
        out["sgu_b"] = np.ascontiguousarray(np.repeat(b, 64, axis=1).transpose(1, 0, 2).reshape(P, S))
    if "mix2" in kinds:
        out["lora_up"] = np.concatenate([a["w_up_2"][0], a["a_up_2"][0]])
        q, k = np.arange(P)[:, None], np.arange(P)[None]
        out["levels"] = np.concatenate([(q >> l + 1 == k >> l + 1) & (k >> l & 1 == 1) & (q >> l & 1 == 0)
                                        for l in range(6)], axis=1).astype(np.float32)
        out["g_up"] = np.ascontiguousarray(a["g_up_2"][0])
    if "mix3" in kinds:
        for n in (64, 32):
            inv = np.float32(10000.0) ** (-np.arange(0, n, 2, dtype=np.float32) / np.float32(n))
            angle = (np.arange(S, dtype=np.float32)[:, None] * inv[None]).T[np.arange(P) % (n // 2)]
            out[f"cos{n}"], out[f"sin{n}"] = np.cos(angle), np.sin(angle)
    return out


def columns(v):
    v = np.asarray(v).reshape(-1, P)
    return v.T


def channel_units(w):
    k, n = w.shape
    return w.reshape(k // P, P, n // (2 * P), 2, P).transpose(2, 1, 3, 0, 4).reshape(-1, P, UNIT)


def token_units(w):
    return w.reshape(2, 4, P, 4 * P).transpose(0, 2, 1, 3).reshape(2, P, UNIT)


def down_units(w):
    return w.reshape(-1, 2, P, D).transpose(0, 2, 1, 3).reshape(-1, P, UNIT)


def gate_up_units(gate, up):
    both = np.stack([gate.reshape(KD, P, KF, P), up.reshape(KD, P, KF, P)])
    return both.transpose(3, 2, 0, 1, 4).reshape(KF, P, UNIT)


def out_units(w):
    return channel_units(w.reshape(D, KD, P)[:, ORDER, :].reshape(D, D))


def padded(w, n):
    return np.concatenate([w, np.zeros((w.shape[0], n - w.shape[1]), w.dtype)], axis=1)


def matrices(a):
    f, w = {}, a["w_in"][0]
    for i in range(2):
        f[f"f1{i}_gu"] = lambda i=i: gate_up_units(a["ffn_w_gate"][0, i], a["ffn_w_up"][0, i])
        f[f"f1{i}_down"] = lambda i=i: down_units(a["ffn_w_down"][0, i])
        g = a[f"ffn{i + 1}_w_gu_2"][0]
        f[f"f2{i}_gu"] = lambda g=g: gate_up_units(g[:, :FF], g[:, FF:])
        f[f"f2{i}_down"] = lambda i=i: down_units(a[f"ffn{i + 1}_w_down_2"][0])
        f[f"f3{i}_gu"] = lambda i=i: gate_up_units(a["w_gate_3"][i], a["w_up_3"][i])
        f[f"f3{i}_down"] = lambda i=i: down_units(a["w_down_3"][i])
        w3 = a["w_in_3"][i]
        at = 0
        for name, n in (("qa", 512), ("ka", 512), ("va", 512), ("iq", 256), ("ik", 32), ("iw", 8),
                        ("qb", 512), ("kb", 512), ("vb", 512)):
            part = w3[:, at:at + n]
            at += n
            if name == "ik":
                ik = part
            elif name == "iw":
                f[f"ik3_{i}"] = lambda ik=ik, iw=part: channel_units(
                    np.concatenate([ik, ik, ik, ik, padded(iw, P)], axis=1))
            else:
                lay = token_units if name in ("va", "vb") else channel_units
                f[f"{name}3_{i}"] = lambda part=part, lay=lay: lay(part)
        f[f"m3{i}_out"] = lambda i=i: out_units(a["w_out_3"][i])
    f["f1"] = lambda: channel_units(padded(w[:, 2560:2568], 2 * P))
    f["u1"] = lambda: channel_units(w[:, 0:512])
    f["v1"] = lambda: token_units(w[:, 512:1024])
    f["q1"] = lambda: channel_units(w[:, 1024:1536])
    f["k1"] = lambda: channel_units(w[:, 1536:2048])
    f["va1"] = lambda: token_units(w[:, 2048:2560])
    f["m1_out"] = lambda: out_units(a["w_out"][0])
    w2 = a["w_in_2"][0]
    f["r2"] = lambda: channel_units(w2[:, 0:512])
    f["k2"] = lambda: channel_units(w2[:, 512:1024])
    f["v2"] = lambda: channel_units(w2[:, 1024:1536])
    f["lora2"] = lambda: channel_units(w2[:, 1536:1792])
    pc = w2[:, 1792:2816].reshape(D, 2, 4, P).transpose(0, 2, 1, 3).reshape(D, D)
    f["pc2"] = lambda: channel_units(pc)
    f["m2_out"] = lambda: out_units(a["w_out_2"][0])
    return f


def vectors(a):
    v = {"eps": np.full(P, EPS, np.float32), "c": a["c"][0], "silu_c": np.zeros(D, np.float32), "b_ada": a["b_ada"][0]}
    for i in range(SUBS):
        v[f"npre{i}"] = a["norm_pre_g"][0, i]
        v[f"npost{i}"] = a["norm_post_g"][0, i]
    v["ffn1_pre"] = a["ffn1_norm_pre_2"][0]
    v["ffn2_pre"] = a["ffn2_norm_pre_2"][0]
    v["ffn1_post_half"] = a["ffn1_norm_post_2"][0]
    v["ffn2_post_half"] = a["ffn2_norm_post_2"][0]
    v["mix_pre"] = a["mix_norm_pre_2"][0]
    v["mix_post"] = a["mix_norm_post_2"][0]
    for i in range(2):
        v[f"g_mix{i}"] = a["g_mix_3"][i]
        v[f"g_ffn{i}"] = a["g_ffn_3"][i]
    v["g_final"] = a["g_final_3"]
    more_vectors(a, v)
    return v


def laid_out(a, plan):
    v = vectors(a)
    cols, at = {}, 0
    for name, x in v.items():
        cols[name] = at
        at += -(-x.size // P)
    pv = np.ascontiguousarray(np.concatenate([columns(x) for x in v.values()], axis=1))
    c = constants()
    cncols, at = {}, 0
    for name, x in c.items():
        cncols[name] = at
        at += x.shape[1]
    cn = np.ascontiguousarray(np.concatenate(list(c.values()), axis=1))
    f = matrices(a)
    w = np.concatenate([f[name]() for sub in plan["subs"] for name, _ in sub["units"]])
    arrays = {"w": w, "pv": pv, "cn": cn, "ones": np.ones((P, P), np.float32),
              "x": np.ascontiguousarray(a["x"][0].T)}
    if plan["ada"]:
        arrays["ada"] = np.ascontiguousarray(channel_units(a["w_ada"][0]))
    arrays.update(more_arrays(a, plan))
    return arrays, cols, cncols


def launch_parts(a, plan, nc):
    arrays, cols, cncols = laid_out(a, plan)
    T = {n: nc.dram_tensor("in_" + n, x.shape, mybir.dt.from_np(x.dtype), kind="ExternalInput").ap()
         for n, x in arrays.items()}
    T["out"] = nc.dram_tensor("out_x", (D, S), F32, kind="ExternalOutput").ap()
    kinds = [s["kind"] for s in plan["subs"]]
    n = len(kinds)
    T["cols"], T["cncols"] = cols, cncols
    T["final_reads"] = KD * (n + kinds.count("mix1")) if plan["final"] else KD * (n - 1)
    build_program(nc, T, plan)
    return {"in_" + n: x for n, x in arrays.items()}


def kernel(**inputs):
    from concourse import bacc
    from concourse.bass_utils import run_bass_kernel_spmd

    a = {n: np.asarray(x) for n, x in inputs.items()}
    nc = bacc.Bacc("TRN2", target_bir_lowering=False, num_devices=1)
    arrays = launch_parts(a, whole_plan(), nc)
    r = run_bass_kernel_spmd(nc, [arrays], core_ids=[0])
    return np.ascontiguousarray(r.results[0]["out_x"].T)[None]
```
